# Optimizing a Trainium2 kernel written in Bass

```python
import math
import jax
import jax.numpy as jnp
from jax import lax
import numpy as np

D_MODEL = 1024
BATCH = 1
SEQ = 2048
DEPTH = 1
DEC_BATCH = 8
DEC_SEQ = 1
PAST_LEN = 8192
PAGE_SIZE = 128

HEAD_DIM = 64
N_HEADS = 8
N_KV = 2
GROUP = N_HEADS // N_KV
ATT_WIDTH = N_HEADS * HEAD_DIM
KV_WIDTH = N_KV * HEAD_DIM
CONV_DIM = D_MODEL - ATT_WIDTH
CONV_GROUPS = 8
CONV_WIDTH = 3
MIX_WIDTH = ATT_WIDTH + CONV_DIM
PROJ_WIDTH = ATT_WIDTH + 6 * KV_WIDTH + 3 * N_HEADS + 3 * CONV_DIM
CMP_BLOCK = 32
SEL_BLOCK = 64
TOP_N = 8
WINDOW = 512
SEL_QCHUNK = 64
WIN_QBLOCK = 128
RP_BUCKETS = 32
RP_MAX_DIST = 128
D_FF = 4 * D_MODEL
PLE_DIM = 256
SCALE = HEAD_DIM ** -0.5
NEG = -1e30
FORCE = 1e4
EPS = 1e-6

kernel_name = 'nsa_shortconv_hybrid_decode_step'

def rmsnorm(x, g):
    xf = x.astype(jnp.float32)
    y = xf * lax.rsqrt(jnp.mean(xf * xf, axis=-1, keepdims=True) + EPS)
    return (y * g.astype(jnp.float32)).astype(x.dtype)

def rel_bucket(dist):
    n = jnp.maximum(dist, 0)
    max_exact = RP_BUCKETS // 2
    nf = jnp.maximum(n, 1).astype(jnp.float32)
    large = max_exact + (jnp.log(nf / max_exact) / math.log(RP_MAX_DIST / max_exact)
                         * (RP_BUCKETS - max_exact)).astype(jnp.int32)
    large = jnp.minimum(large, RP_BUCKETS - 1)
    return jnp.where(n < max_exact, n, large)

def rel_bias_lookup(rel_bias, dist):
    return rel_bias[rel_bucket(dist)].reshape(dist.shape + (N_KV, GROUP)).astype(jnp.float32)

def pad_seq(x):
    extra = (-x.shape[1]) % SEL_BLOCK
    return jnp.pad(x, ((0, 0), (0, extra)) + ((0, 0),) * (x.ndim - 2))

def join_pad(past, new):
    extra = (-(past.shape[1] + new.shape[1])) % SEL_BLOCK
    zeros = jnp.zeros((new.shape[0], extra) + new.shape[2:], new.dtype)
    return jnp.concatenate([past.astype(new.dtype), new, zeros], axis=1)

def mixer_inputs(h, norm_mix, w_in, q_norm, k_norm):
    B, T, _ = h.shape
    sizes = [ATT_WIDTH] + [KV_WIDTH] * 6 + [3 * N_HEADS] + [CONV_DIM] * 3
    points = [int(v) for v in np.cumsum(sizes)[:-1]]
    z = rmsnorm(h, norm_mix) @ w_in
    q, kc, vc, ks, vs, kw, vw, g, cb, cc, ch = jnp.split(z, points, axis=-1)
    heads = lambda t: t.reshape(B, T, N_KV, HEAD_DIM)
    q = rmsnorm(q.reshape(B, T, N_KV, GROUP, HEAD_DIM), q_norm)
    ks = rmsnorm(heads(ks), k_norm[1])
    kw = rmsnorm(heads(kw), k_norm[2])
    gates = jax.nn.sigmoid(g.astype(jnp.float32)).reshape(B, T, 3, N_KV, GROUP).astype(h.dtype)
    return q, heads(kc), heads(vc), ks, heads(vs), kw, heads(vw), gates, cb, cc * ch

def compress(x_raw, pe, w):
    B, Tk = x_raw.shape[:2]
    xb = x_raw.reshape(B, Tk // CMP_BLOCK, CMP_BLOCK, N_KV, HEAD_DIM) + pe[:, None, :]
    return jnp.einsum('bnlgd,lde->bnge', xb, w)

def cmp_branch(q, kc_raw, vc_raw, q_pos, pe, w, k_norm_c, rel_bias):
    k = rmsnorm(compress(kc_raw, pe[0], w[0]), k_norm_c)
    v = compress(vc_raw, pe[1], w[1])
    nc = k.shape[1]
    blk_end = jnp.arange(nc) * CMP_BLOCK + CMP_BLOCK - 1
    dist = q_pos[:, None] - blk_end[None, :]
    valid = dist >= 0
    bias = jnp.transpose(rel_bias_lookup(rel_bias, dist), (2, 3, 0, 1))
    s = jnp.einsum('btgrd,bngd->bgrtn', q, k, preferred_element_type=jnp.float32) * SCALE + bias
    s = jnp.where(valid, s, NEG)
    p = jax.nn.softmax(s, axis=-1) * valid
    o = jnp.einsum('bgrtn,bngd->btgrd', p.astype(v.dtype), v)
    return o, p

def select_blocks(p, q_pos):
    B, G, R, Tq, nc = p.shape
    ratio = SEL_BLOCK // CMP_BLOCK
    ns = nc // ratio
    imp = p.reshape(B, G, R, Tq, ns, ratio).sum(axis=(2, 5))
    cur = (q_pos // SEL_BLOCK)[:, None]
    j = jnp.arange(ns)[None, :]
    forced = (j == 0) | (j == cur) | (j == cur - 1)
    score = jnp.where(forced, FORCE, jnp.where(j <= cur, imp, NEG))
    _, idx = lax.top_k(score, min(TOP_N, ns))
    return idx

def sel_attend(q, q_pos, idx, ksb, vsb, rel_bias):
    B, tc = q.shape[:2]
    n = idx.shape[-1]
    bi = jnp.arange(B)[:, None, None, None]
    gi = jnp.arange(N_KV)[None, :, None, None]
    kg = ksb[bi, gi, idx].reshape(B, N_KV, tc, n * SEL_BLOCK, HEAD_DIM)
    vg = vsb[bi, gi, idx].reshape(B, N_KV, tc, n * SEL_BLOCK, HEAD_DIM)
    kpos = idx[..., None] * SEL_BLOCK + jnp.arange(SEL_BLOCK)
    dist = q_pos[None, None, :, None, None] - kpos
    rb = rel_bias.reshape(RP_BUCKETS, N_KV, GROUP)
    bias = rb[rel_bucket(dist), jnp.arange(N_KV)[None, :, None, None, None]].astype(jnp.float32)
    bias = jnp.moveaxis(bias.reshape(B, N_KV, tc, n * SEL_BLOCK, GROUP), -1, 2)
    valid = (dist >= 0).reshape(B, N_KV, 1, tc, n * SEL_BLOCK)
    s = jnp.einsum('btgrd,bgtkd->bgrtk', q, kg, preferred_element_type=jnp.float32) * SCALE
    p = jax.nn.softmax(jnp.where(valid, s + bias, NEG), axis=-1)
    return jnp.einsum('bgrtk,bgtkd->btgrd', p.astype(vg.dtype), vg)

def sel_branch(q, ks, vs, q_pos, idx, rel_bias):
    B, Tq = q.shape[:2]
    ns = ks.shape[1] // SEL_BLOCK
    ksb = jnp.moveaxis(ks.reshape(B, ns, SEL_BLOCK, N_KV, HEAD_DIM), 3, 1)
    vsb = jnp.moveaxis(vs.reshape(B, ns, SEL_BLOCK, N_KV, HEAD_DIM), 3, 1)
    tc = math.gcd(Tq, SEL_QCHUNK)
    nch = Tq // tc
    qc = jnp.moveaxis(q.reshape(B, nch, tc, N_KV, GROUP, HEAD_DIM), 1, 0)
    ic = jnp.moveaxis(idx.reshape(B, N_KV, nch, tc, idx.shape[-1]), 2, 0)
    pc = q_pos.reshape(nch, tc)
    o = lax.map(lambda a: sel_attend(a[0], a[1], a[2], ksb, vsb, rel_bias), (qc, pc, ic))
    return jnp.moveaxis(o, 0, 1).reshape(B, Tq, N_KV, GROUP, HEAD_DIM)

def win_attend(q, q_pos, k, v, k_pos, rel_bias):
    dist = q_pos[:, None] - k_pos[None, :]
    valid = (dist >= 0) & (dist < WINDOW) & (k_pos[None, :] >= 0)
    bias = jnp.transpose(rel_bias_lookup(rel_bias, dist), (2, 3, 0, 1))
    s = jnp.einsum('btgrd,bkgd->bgrtk', q, k, preferred_element_type=jnp.float32) * SCALE + bias
    p = jax.nn.softmax(jnp.where(valid, s, NEG), axis=-1)
    return jnp.einsum('bgrtk,bkgd->btgrd', p.astype(v.dtype), v)

def win_branch_full(q, kw, vw, rel_bias):
    B, T = q.shape[:2]
    tb = math.gcd(T, WIN_QBLOCK)
    nb = T // tb
    pad = ((0, 0), (WINDOW, 0), (0, 0), (0, 0))
    kp = jnp.pad(kw, pad)
    vp = jnp.pad(vw, pad)
    qb = jnp.moveaxis(q.reshape(B, nb, tb, N_KV, GROUP, HEAD_DIM), 1, 0)
    starts = jnp.arange(nb) * tb

    def blk(a):
        qi, s0 = a
        k = lax.dynamic_slice_in_dim(kp, s0, WINDOW + tb, axis=1)
        v = lax.dynamic_slice_in_dim(vp, s0, WINDOW + tb, axis=1)
        k_pos = s0 - WINDOW + jnp.arange(WINDOW + tb)
        return win_attend(qi, s0 + jnp.arange(tb), k, v, k_pos, rel_bias)

    o = lax.map(blk, (qb, starts))
    return jnp.moveaxis(o, 0, 1).reshape(B, T, N_KV, GROUP, HEAD_DIM)

def short_conv(u, prev, w):
    T = u.shape[1]
    uu = jnp.concatenate([prev.astype(u.dtype), u], axis=1)
    y = w[0] * uu[:, 0:T] + w[1] * uu[:, 1:T + 1] + w[2] * uu[:, 2:T + 2]
    return y, uu[:, -(CONV_WIDTH - 1):]

def layer_out(h, gates, o_c, o_s, o_w, y_conv, p_l, out_norm, w_out, norm_mlp, w_up, w_down,
              norm_ple, w_ple_gate, w_ple_proj):
    B, T, _ = h.shape
    o_att = (gates[:, :, 0, ..., None] * o_c + gates[:, :, 1, ..., None] * o_s
             + gates[:, :, 2, ..., None] * o_w).reshape(B, T, ATT_WIDTH)
    mix = jnp.concatenate([rmsnorm(o_att, out_norm[:ATT_WIDTH]),
                           rmsnorm(y_conv, out_norm[ATT_WIDTH:])], axis=-1)
    h = h + mix @ w_out
    h = h + jnp.square(jax.nn.relu(rmsnorm(h, norm_mlp) @ w_up)) @ w_down
    h = h + jax.nn.sigmoid(rmsnorm(h, norm_ple) @ w_ple_gate) * (p_l @ w_ple_proj)
    return h

def setup_inputs(seed: int = 0) -> dict:
    key = jax.random.key(seed)
    k = jax.random.split(key, 26)
    n_pages = PAST_LEN // PAGE_SIZE
    n_phys = (DEC_BATCH * n_pages * 5) // 4
    wlen = min(WINDOW, PAST_LEN)
    nrm = lambda kk, shape, scale=1.0: jax.random.normal(kk, shape, jnp.float32) * scale
    gain = lambda kk, shape: 1.0 + 0.02 * jax.random.normal(kk, shape, jnp.float32)
    page_table = jax.random.permutation(k[8], n_phys)[: DEC_BATCH * n_pages].reshape(
        DEC_BATCH, n_pages).astype(jnp.int32)
    return {
        'x_prompt': nrm(k[0], (BATCH, SEQ, D_MODEL)),
        'x_sample': nrm(k[1], (DEC_BATCH, DEC_SEQ, D_MODEL)),
        'p_prompt': nrm(k[2], (DEPTH, BATCH, SEQ, PLE_DIM)),
        'p_sample': nrm(k[3], (DEPTH, DEC_BATCH, DEC_SEQ, PLE_DIM)),
        'cache_cmp_kv': nrm(k[4], (DEPTH, n_phys, PAGE_SIZE, 2, N_KV, HEAD_DIM)),
        'cache_sel_kv': nrm(k[5], (DEPTH, n_phys, PAGE_SIZE, 2, N_KV, HEAD_DIM)),
        'state_win_kv': nrm(k[6], (DEPTH, DEC_BATCH, wlen, 2, N_KV, HEAD_DIM)),
        'state_conv': nrm(k[7], (DEPTH, DEC_BATCH, CONV_WIDTH - 1, CONV_DIM)),
        'page_table': page_table,
        'rel_bias': nrm(k[9], (RP_BUCKETS, N_HEADS), 0.5),
        'norm_mix': gain(k[10], (DEPTH, D_MODEL)),
        'w_in': nrm(k[11], (DEPTH, D_MODEL, PROJ_WIDTH), D_MODEL ** -0.5),
        'q_norm': gain(k[12], (DEPTH, HEAD_DIM)),
        'k_norm': gain(k[13], (DEPTH, 3, HEAD_DIM)),
        'cmp_pe': nrm(k[14], (DEPTH, 2, CMP_BLOCK, HEAD_DIM), 0.1),
        'w_cmp': nrm(k[15], (DEPTH, 2, CMP_BLOCK, HEAD_DIM, HEAD_DIM), (CMP_BLOCK * HEAD_DIM) ** -0.5),
        'conv_w': nrm(k[16], (DEPTH, CONV_WIDTH, CONV_DIM), CONV_WIDTH ** -0.5),
        'out_norm': gain(k[17], (DEPTH, MIX_WIDTH)),
        'w_out': nrm(k[18], (DEPTH, MIX_WIDTH, D_MODEL), MIX_WIDTH ** -0.5),
        'norm_mlp': gain(k[19], (DEPTH, D_MODEL)),
        'w_up': nrm(k[20], (DEPTH, D_MODEL, D_FF), D_MODEL ** -0.5),
        'w_down': nrm(k[21], (DEPTH, D_FF, D_MODEL), D_FF ** -0.5),
        'norm_ple': gain(k[22], (DEPTH, D_MODEL)),
        'w_ple_gate': nrm(k[23], (DEPTH, D_MODEL, D_MODEL), D_MODEL ** -0.5),
        'w_ple_proj': nrm(k[24], (DEPTH, PLE_DIM, D_MODEL), PLE_DIM ** -0.5),
    }

def reference(x_prompt, x_sample, p_prompt, p_sample, cache_cmp_kv, cache_sel_kv, state_win_kv,
              state_conv, page_table, rel_bias, norm_mix, w_in, q_norm, k_norm, cmp_pe, w_cmp,
              conv_w, out_norm, w_out, norm_mlp, w_up, w_down, norm_ple, w_ple_gate, w_ple_proj):
    h_p, h_s = x_prompt, x_sample
    bp, tp = h_p.shape[:2]
    bs, ts = h_s.shape[:2]
    pos_p = jnp.arange(tp)
    pos_s = PAST_LEN + jnp.arange(ts)
    pc_l, ps_l, pw_l, pv_l, sc_l, ss_l, sw_l, sv_l = [], [], [], [], [], [], [], []
    for l in range(DEPTH):
        lw = (norm_mix[l], w_in[l], q_norm[l], k_norm[l])
        tail = (out_norm[l], w_out[l], norm_mlp[l], w_up[l], w_down[l], norm_ple[l],
                w_ple_gate[l], w_ple_proj[l])
        q, kc, vc, ks, vs, kw, vw, gates, cb, u = mixer_inputs(h_p, *lw)
        o_c, p_c = cmp_branch(q, pad_seq(kc), pad_seq(vc), pos_p, cmp_pe[l], w_cmp[l], k_norm[l, 0], rel_bias)
        idx = select_blocks(p_c, pos_p)
        o_s = sel_branch(q, pad_seq(ks), pad_seq(vs), pos_p, idx, rel_bias)
        o_w = win_branch_full(q, kw, vw, rel_bias)
        y_c, conv_new = short_conv(u, jnp.zeros((bp, CONV_WIDTH - 1, CONV_DIM), u.dtype), conv_w[l])
        h_p = layer_out(h_p, gates, o_c, o_s, o_w, cb * y_c, p_prompt[l], *tail)
        pc_l.append(jnp.stack([kc, vc], axis=2))
        ps_l.append(jnp.stack([ks, vs], axis=2))
        pw_l.append(jnp.stack([kw, vw], axis=2)[:, -min(WINDOW, tp):])
        pv_l.append(conv_new)
        q, kc, vc, ks, vs, kw, vw, gates, cb, u = mixer_inputs(h_s, *lw)
        cc_l, cs_l = cache_cmp_kv[l], cache_sel_kv[l]
        past_kc = cc_l[page_table, :, 0].reshape(bs, -1, N_KV, HEAD_DIM)
        past_vc = cc_l[page_table, :, 1].reshape(bs, -1, N_KV, HEAD_DIM)
        past_ks = cs_l[page_table, :, 0].reshape(bs, -1, N_KV, HEAD_DIM)
        past_vs = cs_l[page_table, :, 1].reshape(bs, -1, N_KV, HEAD_DIM)
        o_c, p_c = cmp_branch(q, join_pad(past_kc, kc), join_pad(past_vc, vc), pos_s, cmp_pe[l], w_cmp[l],
                              k_norm[l, 0], rel_bias)
        idx = select_blocks(p_c, pos_s)
        o_s = sel_branch(q, join_pad(past_ks, ks), join_pad(past_vs, vs), pos_s, idx, rel_bias)
        win = state_win_kv[l]
        wlen = win.shape[1]
        kw_all = jnp.concatenate([win[:, :, 0].astype(kw.dtype), kw], axis=1)
        vw_all = jnp.concatenate([win[:, :, 1].astype(vw.dtype), vw], axis=1)
        k_pos = PAST_LEN - wlen + jnp.arange(wlen + ts)
        o_w = win_attend(q, pos_s, kw_all, vw_all, k_pos, rel_bias)
        y_c, conv_new = short_conv(u, state_conv[l], conv_w[l])
        h_s = layer_out(h_s, gates, o_c, o_s, o_w, cb * y_c, p_sample[l], *tail)
        sc_l.append(jnp.stack([kc, vc], axis=2))
        ss_l.append(jnp.stack([ks, vs], axis=2))
        sw_l.append(jnp.stack([kw_all, vw_all], axis=2)[:, -min(WINDOW, PAST_LEN + ts):])
        sv_l.append(conv_new)
    prompt_cmp_kv = jnp.stack(pc_l)
    prompt_sel_kv = jnp.stack(ps_l)
    prompt_win_kv = jnp.stack(pw_l)
    prompt_conv = jnp.stack(pv_l)
    sample_cmp_kv = jnp.stack(sc_l)
    sample_sel_kv = jnp.stack(ss_l)
    sample_win_kv = jnp.stack(sw_l)
    sample_conv = jnp.stack(sv_l)
    return (h_p, h_s, prompt_cmp_kv, prompt_sel_kv, prompt_win_kv, prompt_conv,
            sample_cmp_kv, sample_sel_kv, sample_win_kv, sample_conv)


_drawn_inputs = setup_inputs


def setup_inputs(seed=0):
    import zlib

    import numpy as np

    out = dict(_drawn_inputs(seed))
    spreads = {}
    factors = {'out_norm': 3.856, 'norm_mlp': 3.825, 'norm_ple': 8.0}
    for name, (base, spread) in spreads.items():
        noise = np.random.default_rng([zlib.crc32(name.encode()), seed]).standard_normal(out[name].shape)
        drawn = base * np.exp(spread * noise) if base else spread * noise
        out[name] = jnp.asarray(drawn.astype(out[name].dtype))
    for name, factor in factors.items():
        out[name] = (out[name] * factor).astype(out[name].dtype)
    return out
```

```python
from contextlib import ExitStack, contextmanager

import numpy as np

import concourse.bass as bass
from concourse import mybir

ALU = mybir.AluOpType
ACT = mybir.ActivationFunctionType
F32 = mybir.dt.float32
I32 = mybir.dt.int32
U32 = mybir.dt.uint32
X = mybir.AxisListType.X
XY = mybir.AxisListType.XY

D = 1024
SEQ = 2048
NB = 8
NTOK = SEQ + NB
CH = NTOK // 4
HF = CH // 2
NEG = -1e30
EPS = 1e-6
HD = 64
NH = 8
KT = D // 128
FT = 4 * D // 128
PAST = 8192
PAGE = 128
NPAGE = PAST // PAGE
CB = 32
BANDW = 1024
LINEW = 1152
NCP = SEQ // CB
NCS = NB * PAST // CB
ZT = ["q0", "q1", "q2", "q3", "ks", "kw", "kc", "vc", "vs", "vw"] + \
     [f"{a}{j}" for j in range(4) for a in ("cc", "ch", "cb")] + ["g"]
NORMED = ZT[:6]
KVROW = {"kc": 0, "vc": 1, "ks": 2, "vs": 3, "kw": 4, "vw": 5}


class Own:

    def __init__(self, eng):
        self.eng, self.i, self.count = eng, 0, {}

    def iteration(self, i):
        self.close()
        self.i, self.count = i, {}

    def close(self):
        for name, (n, per) in self.count.items():
            assert n == per, (name, n, per)
        self.count = {}

    def __call__(self, ins, sem, per):
        n = self.count.get(sem.name, (0, per))[0] + 1
        self.count[sem.name] = (n, per)
        ins.then_inc(sem, 1)
        self.eng.wait_ge(sem, per * self.i + n)


@contextmanager
def semaphores(nc, prefix):
    taken = []

    def sem(name):
        taken.append(nc.alloc_semaphore(name=prefix + name))
        return taken[-1]
    yield sem
    nc.clear_and_free_semaphores(taken)
    nc.all_engine_barrier()


def ds(a, n):
    return bass.ds(a, n)


def setup(nc, d, t):
    with ExitStack() as ctx:
        sb = lambda n, s, dt=F32: ctx.enter_context(nc.sbuf_tensor(n, s, dt))
        sem = ctx.enter_context(semaphores(nc, "st_"))
        relb = sb("relb", [32, NH])
        oneh = sb("oneh", [32, LINEW])
        line = sb("line_sb", [NH, LINEW])
        cmask = sb("cmask", [128, BANDW])
        ps = ctx.enter_context(nc.psum_tensor("ps_line", [NH, 3, 512], F32))
        s_in, s_mm, s_line, s_ld, s_st, s_band, s_out = (sem(n) for n in (
            "inputs", "line_matmul", "line_copied", "consts", "line_stored", "band_loaded", "band_masked"))
        with nc.Block() as block:
            @block.sync
            def _(sp):
                sp.dma_start(relb[:], d["rel_bias"]).then_inc(s_in, 16)
                sp.dma_start(oneh[:], d["onehot"]).then_inc(s_in, 16)
                sp.dma_start(cmask[:], d["cmask"]).then_inc(s_ld, 16)
                sp.wait_ge(s_line, 3)
                sp.dma_start(d["line"], line[:]).then_inc(s_st, 16)
                sp.wait_ge(s_st, 16)
                every = bass.AP(tensor=d["line"].tensor, offset=0, ap=[[0, 128], [1, NH * LINEW]])
                sp.dma_start(d["skew"], every).then_inc(s_st, 16)
                sp.wait_ge(s_st, 32)
                src = bass.AP(tensor=d["skew"].tensor, offset=128,
                              ap=[[NH * LINEW - 1, 128], [LINEW, NH], [1, BANDW]])
                sp.dma_start(t["band"][:], src).then_inc(s_band, 16)

            @block.tensor
            def _(pe):
                pe.wait_ge(s_in, 32)
                for i, (a, n) in enumerate(((0, 512), (512, 512), (1024, 128))):
                    pe.matmul(ps[:, i, 0:n], relb[:], oneh[:, a:a + n], start=True, stop=True).then_inc(s_mm, 1)

            @block.vector
            def _(dve):
                for i, (a, n) in enumerate(((0, 512), (512, 512), (1024, 128))):
                    dve.wait_ge(s_mm, i + 1)
                    dve.tensor_copy(line[:, a:a + n], ps[:, i, 0:n]).then_inc(s_line, 1)
                dve.wait_ge(s_band, 16)
                dve.wait_ge(s_ld, 16)
                for h in range(NH):
                    dve.tensor_tensor(t["band"][:, h, :], t["band"][:, h, :], cmask[:], ALU.add).then_inc(s_out, 1)


def project(nc, d, t):
    with ExitStack() as ctx:
        sb = lambda n, s, dt=F32: ctx.enter_context(nc.sbuf_tensor(n, s, dt))
        pb = lambda n, s: ctx.enter_context(nc.psum_tensor(n, s, F32))
        sem = ctx.enter_context(semaphores(nc, "pj_"))
        win = sb("w_in_sb", [128, len(ZT) - 1, KT, 128])
        wg = sb("w_gates_sb", [128, KT, 24])
        xb = sb("x_chunk", [128, KT, CH])
        aT = sb("a_chunk", [128, KT, CH])
        sqx = sb("x_squares", [128, 2, CH])
        rs = sb("rstd_x", [128, CH])
        zs = sb("z_copy", [128, 2, CH])
        sqz = sb("z_square", [128, 2, CH])
        rn = sb("rstd_z", [128, 2, CH])
        ccs = sb("cc_copy", [128, CH])
        cv = sb("conv_sum", [128, CH])
        u = sb("u", [128, 4, CH + 2])
        y = sb("y_conv", [128, 4, CH])
        stg = sb("stage", [128, 5, CH])
        sst = sb("state_conv_sb", [128, 4, 2, NB])
        gn = sb("norm_mix_sb", [128, KT])
        gq = sb("qk_gain", [128, 6])
        gy = sb("conv_gain", [128, 4])
        cw = sb("conv_w_sb", [128, 4, 3])
        zp = [pb("ps_z0", [128, 2, 512]), pb("ps_z1", [128, 2, 512])]
        ssp = pb("ps_ssq", [128, 2, 512])
        nsp = pb("ps_nsq", [128, 2, 512])
        V = lambda ps: ps[:, :, 0:HF]
        W = lambda a: a.rearrange("p (h n) -> p h n", h=2)

        s_w, s_c, s_x, s_sq, s_sqf, s_ss, s_a, s_z, s_zt, s_nq, s_nd, s_nt, s_ysq, s_ys = (sem(n) for n in (
            "w_loaded", "consts_loaded", "x_loaded", "x_squared", "x_square_used", "x_summed", "a_ready", "z_done", "z_taken",
            "z_squared", "z_summed", "z_sum_taken", "y_squared", "y_summed"))
        s_st, s_gp, s_gs, s_chain, s_uo, s_rt = (sem(n) for n in (
            "staged", "gates_done", "gates_staged", "dve_steps", "u_out", "roots_taken"))
        s_u0, s_carry, s_fix = sem("u_cleared"), sem("u_carried"), sem("sample_conv")
        s_o = [sem(f"stage{i}_out") for i in range(5)]
        sends = [("q", j) for j in range(4)] + [("kv", KVROW[k]) for k in ("ks", "kw", "kc", "vc", "vs", "vw")] + \
                [("g", 0)] + [("mix", 4 + j) for j in range(4)]
        NS = len(sends)

        with nc.Block() as block:
            @block.sync
            def _(sp):
                def load_x(c):
                    sp.dma_start(xb[:], d["xT"][:, :, ds(c * CH, CH)].rearrange("k p n -> p k n")).then_inc(s_x, 16)

                load_x(0)
                for a, b in ((gn, "norm_mix"), (gq, "qk_gain"), (gy, "conv_gain"), (cw, "conv_w"), (sst, "state_conv")):
                    sp.dma_start(a[:], d[b]).then_inc(s_c, 16)
                for m in range(len(ZT) - 1):
                    sp.dma_start(win[:, m], d["w_in"][m]).then_inc(s_w, 16)
                sp.dma_start(wg[:], d["w_gates"]).then_inc(s_w, 16)

                def body(c, last):
                    for n, (what, row) in enumerate(sends):
                        sl = n % 5
                        if n == 10 and not last:
                            sp.wait_ge(s_a, KT * (c + 1))
                            load_x(c + 1)
                        if what == "g":
                            sp.wait_ge(s_gs, c + 1)
                        else:
                            sp.wait_ge(s_st, (NS - 1) * c + n + (n < 10))
                        dst = d["gT"][:, ds(c * CH, CH)] if what == "g" else \
                            d[{"q": "qT", "kv": "kvT", "mix": "mixT"}[what]][row, :, ds(c * CH, CH)]
                        src = stg[0:24, sl, :] if what == "g" else stg[:, sl, :]
                        sp.dma_start(dst, src).then_inc(s_o[sl], 16)
                with sp.Fori(0, 3) as c:
                    body(c, False)
                body(3, True)
                sp.dma_start(d["uT"].rearrange("j p n -> p j n"), u[:, :, CH - NB:CH + 2]).then_inc(s_uo, 16)
                sp.wait_ge(s_uo, 16)
                for sl in range(5):
                    sp.wait_ge(s_o[sl], 16 * 4 * NS // 5)

            @block.scalar
            def _(act):
                with act.Fori(0, 4) as c:
                    act.wait_ge(s_x, 16 * c + 16)
                    for k in range(KT):
                        if k >= 2:
                            act.wait_ge(s_sqf, KT * c + k - 1)
                        act.activation(sqx[:, k % 2], xb[:, k], ACT.Square).then_inc(s_sq, 1)
                    act.wait_ge(s_sqf, KT * (c + 1))
                    act.activation(W(rs[:]), V(ssp), ACT.Sqrt, bias=t["eps"][:]).then_inc(s_rt, 1)
                    for n in range(6):
                        act.wait_ge(s_nd, 6 * c + n + 1)
                        act.activation(W(rn[:, n % 2]), V(nsp), ACT.Sqrt, bias=t["eps"][:]).then_inc(s_nt, 1)
                    act.wait_ge(s_gp, c + 1)
                    act.wait_ge(s_o[0], 16 * 3 * c + 32)
                    act.activation(W(stg[0:24, 0, :]), V(zp[0])[0:24], ACT.Sigmoid).then_inc(s_gs, 1)
                    act.wait_ge(s_ys, c + 1)
                    act.activation(W(rn[:, 0]), V(nsp), ACT.Sqrt, bias=t["eps"][:]).then_inc(s_rt, 1)

            @block.tensor
            def _(pe):
                with pe.Fori(0, 4) as c:
                    for k in range(KT):
                        pe.wait_ge(s_sq, KT * c + k + 1)
                        for h in range(2):
                            mm = pe.matmul(ssp[:, h, 0:HF], t["ones_d"][:], sqx[:, k % 2, h * HF:(h + 1) * HF],
                                           start=(k == 0), stop=(k == KT - 1))
                        mm.then_inc(s_sqf, 1)

                    def norm(n):
                        pe.wait_ge(s_nq, 6 * c + n + 1)
                        if n:
                            pe.wait_ge(s_nt, 6 * c + n)
                        for h in range(2):
                            mm = pe.matmul(nsp[:, h, 0:HF], t["ones_hd"][:], sqz[:, n % 2, h * HF:(h + 1) * HF],
                                           start=True, stop=True)
                        mm.then_inc(s_nd, 1)
                    for m, name in enumerate(ZT):
                        if m == 0:
                            pe.wait_ge(s_a, KT * (c + 1))
                            pe.wait_ge(s_w, 16 * len(ZT))
                        if m >= 2:
                            pe.wait_ge(s_zt, (len(ZT) - 1) * c + m - 1)
                        for h in range(2):
                            for k in range(KT):
                                o = zp[m % 2][0:24, h, 0:HF] if name == "g" else zp[m % 2][:, h, 0:HF]
                                mm = pe.matmul(o, wg[:, k] if name == "g" else win[:, m, k],
                                               aT[:, k, h * HF:(h + 1) * HF], start=(k == 0), stop=(k == KT - 1))
                        mm.then_inc(s_gp if name == "g" else s_z, 1)
                        if 1 <= m <= 6:
                            norm(m - 1)
                    for j in range(4):
                        pe.wait_ge(s_ysq, 4 * c + j + 1)
                        for h in range(2):
                            mm = pe.matmul(nsp[:, h, 0:HF], t["ones_w"][:], aT[:, j, h * HF:(h + 1) * HF],
                                           start=(j == 0), stop=(j == 3))
                    mm.then_inc(s_ys, 1)

            @block.vector
            def _(dve):
                own = Own(dve)
                NZ = len(ZT) - 1
                link = lambda ins: own(ins, s_chain, 1 + 6 + 4 * 3 + 1)
                dve.wait_ge(s_c, 16 * 5)
                dve.memset(u[:, :, 0:2], 0.0).then_inc(s_u0, 1)
                dve.wait_ge(s_u0, 1)

                def body(c, last):
                    sent = [0]

                    def slot():
                        n = sent[0]
                        sent[0] += 1
                        dve.wait_ge(s_o[n % 5], 48 * c + 16 * (n // 5))
                        return stg[:, n % 5, :]

                    def staged(ins):
                        own(ins, s_st, NS - 1)

                    dve.wait_ge(s_rt, 2 * c + 1)
                    link(dve.reciprocal(rs[:], rs[:]))
                    for k in range(KT):
                        own(dve.scalar_tensor_tensor(aT[:, k], xb[:, k], gn[:, k:k + 1], rs[:], ALU.mult,
                                                     ALU.mult), s_a, KT)

                    def finish(n):
                        dve.wait_ge(s_nt, 6 * c + n + 1)
                        link(dve.reciprocal(rn[:, n % 2], rn[:, n % 2]))
                        staged(dve.scalar_tensor_tensor(slot(), zs[:, n % 2], gq[:, n:n + 1], rn[:, n % 2],
                                                        ALU.mult, ALU.mult))

                    for m, name in enumerate(ZT[:-1]):
                        dve.wait_ge(s_z, (len(ZT) - 1) * c + m + 1)
                        z = V(zp[m % 2])
                        if name in NORMED:
                            own(dve.tensor_copy(W(zs[:, m % 2]), z), s_zt, NZ)
                            own(dve.tensor_tensor(sqz[:, m % 2], zs[:, m % 2], zs[:, m % 2], ALU.mult), s_nq, 6)
                            if m:
                                finish(m - 1)
                        elif name in KVROW:
                            if m == 6:
                                finish(5)
                            o = slot()
                            own(dve.tensor_copy(W(o), z), s_zt, NZ)
                            staged(dve.nop())
                        elif name[:2] == "cc":
                            own(dve.tensor_copy(W(ccs[:]), z), s_zt, NZ)
                        elif name[:2] == "ch":
                            j = int(name[2])
                            own(dve.tensor_tensor(W(u[:, j, 2:CH + 2]), z, W(ccs[:]), ALU.mult), s_zt, NZ)
                            link(dve.tensor_scalar(cv[:], u[:, j, 2:CH + 2], cw[:, j, 2:3], None, ALU.mult))
                            link(dve.scalar_tensor_tensor(cv[:], u[:, j, 1:CH + 1], cw[:, j, 1:2], cv[:], ALU.mult, ALU.add))
                            link(dve.scalar_tensor_tensor(cv[:], u[:, j, 0:CH], cw[:, j, 0:1], cv[:], ALU.mult, ALU.add))
                            if last:
                                sc = cv[:, CH - NB:CH]
                                for i, past in enumerate((u[:, j, CH + 2 - NB:CH + 2], sst[:, j, 1], sst[:, j, 0])):
                                    wi = cw[:, j, 2 - i:3 - i]
                                    ins = dve.scalar_tensor_tensor(sc, past, wi, sc, ALU.mult, ALU.add) if i else \
                                        dve.tensor_scalar(sc, past, wi, None, ALU.mult)
                                    ins.then_inc(s_fix, 1)
                                    dve.wait_ge(s_fix, 3 * j + i + 1)
                            else:
                                own(dve.tensor_copy(u[:, j, 0:2], u[:, j, CH:CH + 2]), s_carry, 4)
                        else:
                            j = int(name[2])
                            own(dve.tensor_tensor(W(y[:, j]), z, W(cv[:]), ALU.mult), s_zt, NZ)
                    sent[0] += 1
                    dve.wait_ge(s_zt, (len(ZT) - 1) * (c + 1))
                    dve.wait_ge(s_gp, c + 1)
                    for j in range(4):
                        own(dve.tensor_tensor(aT[:, j], y[:, j], y[:, j], ALU.mult), s_ysq, 4)
                    dve.wait_ge(s_rt, 2 * c + 2)
                    link(dve.reciprocal(rn[:, 0], rn[:, 0]))
                    for j in range(4):
                        staged(dve.scalar_tensor_tensor(slot(), y[:, j], gy[:, j:j + 1], rn[:, 0], ALU.mult, ALU.mult))

                with dve.Fori(0, 3) as c:
                    own.iteration(c)
                    body(c, False)
                own.iteration(3)
                body(3, True)
                own.close()


def compress(nc, d, t):
    NPG = 32
    plain = t["plain"]
    with ExitStack() as ctx:
        sb = lambda n, s, dt=F32: ctx.enter_context(nc.sbuf_tensor(n, s, dt))
        pb = lambda n, s: ctx.enter_context(nc.psum_tensor(n, s, F32))
        sem = ctx.enter_context(semaphores(nc, "cp_"))
        wc = sb("w_cmp_sb", [128, 2, CB, 128])
        pe_t = sb("cmp_pe_sb", [128, 2, CB])
        cvec = sb("pe_compressed", [128, 2])
        gk = sb("k_norm_cmp", [128, 1])
        pg = [sb(f"pages{b}", [128, NPG, 2, PAGE]) for b in range(2)]
        ptab = sb("page_table_sb", [1, NB * NPAGE], I32)
        kcT, vcT = t["kcT"], sb("vcT", [128, NCP + NCS])
        cps = [pb(f"ps_cmp{b}", [128, 512]) for b in range(2)]
        sps = pb("ps_cmp_sum", [128, 512])
        tps = pb("ps_cmp_tr", [128, 4, 128])
        sq = pg[0][:, 0:2, :, :].rearrange("p a b c -> p (a b c)")
        rt = pg[0][:, 2:4, :, :].rearrange("p a b c -> p (a b c)")
        s_z, s_w, s_c, s_cv, s_cvd, s_done, s_ev, s_pr, s_sq, s_sum, s_rt, s_rc, s_kn, s_tr, s_te = (sem(n) for n in (
            "weights_cleared", "weights_loaded", "consts_loaded", "pe_summed", "pe_copied", "chunk_summed", "chunk_copied",
            "prompt_loaded", "squared", "squares_summed", "root", "reciprocal", "k_normed", "v_transposed", "v_copied"))
        s_k0 = sem("k_copied")
        s_pg = [sem(f"pages{b}") for b in range(2)]
        NCH = NB * NPAGE // NPG
        pieces = [(512 * i, 512) for i in range(4)] + [(2048, 64)]

        def load_pages(eng, b, idx_base):
            with eng.Fori(0, NPG) as j:
                page = eng.value_load(ptab[0:1, ds(idx_base + j, 1)], min_val=0, max_val=d["cache_cmp"].shape[0] - 1)
                eng.dma_start(pg[b][:, ds(j, 1)].rearrange("p a k n -> p (a k) n"),
                              d["cache_cmp"][ds(page, 1)].rearrange("a p k n -> (a p) k n")).then_inc(s_pg[b], 16)

        with nc.Block() as block:
            @block.gpsimd
            def _(pool):
                own = Own(pool)
                for kv in range(2):
                    own(pool.memset(wc[:, kv], 0.0), s_z, 2)

            @block.sync
            def _(sp):
                for a, b in ((pe_t, "cmp_pe"), (gk, "k_norm_cmp"), (ptab, "page_table")):
                    sp.dma_start(a[:], d[b]).then_inc(s_c, 16)
                sp.wait_ge(s_z, 2)
                for g in range(2):
                    for kv in range(2):
                        sp.dma_start(wc[64 * g:64 * g + 64, kv, :, 64 * g:64 * g + 64], d["w_cmp"][kv]).then_inc(s_w, 16)
                sp.wait_ge(s_c, 48)
                with sp.Fori(0, NCH // 2) as i:
                    sp.wait_ge(s_done, 2 * i)
                    plain(sp)
                    load_pages(sp, 0, i * (2 * NPG))
                sp.wait_ge(s_done, NCH)
                for kv in range(2):
                    sp.dma_start(pg[0][:, 0:SEQ // PAGE, kv, :],
                                 d["kvT"][kv, :, 0:SEQ].rearrange("p (a n) -> p a n", n=PAGE)).then_inc(s_pr, 16)

            @block.scalar
            def _(act):
                act.wait_ge(s_c, 48)
                with act.Fori(0, NCH // 2) as i:
                    act.wait_ge(s_done, 2 * i)
                    plain(act)
                    load_pages(act, 1, i * (2 * NPG) + NPG)
                for i, (a, n) in enumerate(pieces):
                    if i:
                        act.wait_ge(s_kn, i)
                    else:
                        act.wait_ge(s_ev, NCH + 1)
                    act.activation(sq[:, 0:n], kcT[:, a:a + n], ACT.Square).then_inc(s_sq, 1)
                    act.wait_ge(s_sum, i + 1)
                    act.activation(rt[:, 0:n], sps[:, 0:n], ACT.Sqrt, bias=t["eps"][:]).then_inc(s_rt, 1)

            @block.tensor
            def _(pe):
                pe.wait_ge(s_w, 64)
                pe.wait_ge(s_c, 48)
                for kv in range(2):
                    for l in range(CB):
                        mm = pe.matmul(sps[:, kv:kv + 1], wc[:, kv, l], pe_t[:, kv, l:l + 1], start=(l == 0), stop=(l == CB - 1))
                mm.then_inc(s_cv, 1)

                def chunk(b, np_):
                    for kv in range(2):
                        for l in range(CB):
                            mm = pe.matmul(cps[b][:, 128 * kv:128 * kv + 4 * np_], wc[:, kv, l],
                                           pg[b][:, 0:np_, kv, l::CB], start=(l == 0), stop=(l == CB - 1))
                    mm.then_inc(s_done, 1)
                with pe.Fori(0, NCH // 2) as i:
                    for b in range(2):
                        pe.wait_ge(s_pg[b], 16 * NPG * (i + 1))
                        pe.wait_ge(s_ev, 2 * i)
                        chunk(b, NPG)
                pe.wait_ge(s_pr, 32)
                pe.wait_ge(s_ev, NCH)
                chunk(0, SEQ // PAGE)
                for i, (a, n) in enumerate(pieces):
                    pe.wait_ge(s_sq, i + 1)
                    pe.wait_ge(s_cvd if i == 0 else s_rt, 1 if i == 0 else i)
                    pe.matmul(sps[:, 0:n], t["ones_hd"][:], sq[:, 0:n], start=True, stop=True).then_inc(s_sum, 1)
                for q in range(5):
                    if q:
                        pe.wait_ge(s_te, q)
                    if q < 4:
                        for j in range(4):
                            a = NCP + 512 * q + 128 * j
                            mm = pe.transpose(tps[:, j], vcT[:, a:a + 128], t["ident"][:])
                    else:
                        mm = pe.transpose(tps[0:NCP, 0], vcT[:, 0:NCP], t["ident"][:])
                    mm.then_inc(s_tr, 1)

            @block.vector
            def _(dve):
                dve.wait_ge(s_cv, 1)
                dve.tensor_copy(cvec[:], sps[:, 0:2]).then_inc(s_cvd, 1)
                dve.wait_ge(s_cvd, 1)

                def copy(b, a, n, done):
                    dve.tensor_scalar(kcT[:, a], cps[b][:, 0:n], cvec[:, 0:1], None, ALU.add).then_inc(s_k0, 1)
                    dve.tensor_scalar(vcT[:, a], cps[b][:, 128:128 + n], cvec[:, 1:2], None, ALU.add).then_inc(s_ev, 1)
                with dve.Fori(0, NCH // 2) as i:
                    for b in range(2):
                        dve.wait_ge(s_done, 2 * i + b + 1)
                        copy(b, ds(i * 256 + (NCP + 128 * b), 128), 128, None)
                dve.wait_ge(s_done, NCH + 1)
                copy(0, slice(0, NCP), NCP, None)
                dve.wait_ge(s_k0, NCH + 1)
                for i, (a, n) in enumerate(pieces):
                    dve.wait_ge(s_rt, i + 1)
                    dve.reciprocal(rt[:, 0:n], rt[:, 0:n]).then_inc(s_rc, 1)
                    dve.wait_ge(s_rc, i + 1)
                    dve.scalar_tensor_tensor(kcT[:, a:a + n], kcT[:, a:a + n], gk[:, 0:1], rt[:, 0:n], ALU.mult,
                                             ALU.mult).then_inc(s_kn, 1)
                    dve.wait_ge(s_kn, i + 1)
                for g in range(2):
                    r = slice(64 * g, 64 * g + 64)
                    o = slice(64 - 64 * g, 128 - 64 * g)
                    dve.tensor_copy(t["kcz"][r, g], kcT[r, 0:NCP])
                    dve.memset(t["kcz"][o, g], 0.0)
                for q in range(5):
                    dve.wait_ge(s_tr, q + 1)
                    if q < 4:
                        dve.tensor_copy(t["vcs"][:, 4 * q:4 * q + 4], tps[:]).then_inc(s_te, 1)
                    else:
                        dve.tensor_copy(t["vcp"][:], tps[0:NCP, 0]).then_inc(s_te, 1)


def prompt_keys(nc, d, t):
    with ExitStack() as ctx:
        sem = ctx.enter_context(semaphores(nc, "pk_"))
        vT = t["S"]
        ps = [ctx.enter_context(nc.psum_tensor(f"ps_vt{b}", [128, 4, 128], F32)) for b in range(2)]
        s_v, s_k, s_t, s_e, s_m = (sem(n) for n in ("v_loaded", "k_loaded", "v_transposed", "v_copied", "cleared"))
        with nc.Block() as block:
            @block.sync
            def _(sp):
                for i, n in enumerate(("vs", "vw")):
                    sp.dma_start(vT[:, i], d["kvT"][KVROW[n], :, 0:SEQ]).then_inc(s_v, 16)
                for n in ("ks", "kw"):
                    for g in range(2):
                        r = slice(64 * g, 64 * g + 64)
                        sp.dma_start(t[n][r, g], d["kvT"][KVROW[n], r, 0:SEQ]).then_inc(s_k, 16)
                for n in ("tri", "score_band", "att_gain"):
                    sp.dma_start(t[n][:], d[n]).then_inc(s_k, 16)
                sp.wait_ge(s_k, 16 * 7)

            @block.gpsimd
            def _(pool):
                own = Own(pool)
                for n in ("ks", "kw"):
                    for g in range(2):
                        own(pool.memset(t[n][64 - 64 * g:128 - 64 * g, g], 0.0), s_m, 5)
                own(pool.memset(t["half"][:], -0.5), s_m, 5)

            @block.tensor
            def _(pe):
                pe.wait_ge(s_v, 32)
                for q in range(8):
                    if q >= 2:
                        pe.wait_ge(s_e, q - 1)
                    for j in range(4):
                        k = 4 * (q % 4) + j
                        mm = pe.transpose(ps[q % 2][:, j], vT[:, q // 4, 128 * k:128 * k + 128], t["ident"][:])
                    mm.then_inc(s_t, 1)

            @block.vector
            def _(dve):
                dve.memset(t["cband"][:, :, 0:56], 0.0)
                dve.memset(t["cband"][:, :, 64:124], NEG)
                dve.tensor_copy(t["cband"][:, :, 56:64], t["band"][:, :, 415:415 + 32 * 7 + 1:32])
                for q in range(8):
                    dve.wait_ge(s_t, q + 1)
                    dst = t["vs" if q < 4 else "vw"]
                    dve.tensor_copy(dst[:, 4 * (q % 4):4 * (q % 4) + 4], ps[q % 2][:]).then_inc(s_e, 1)


def prompt(nc, d, t, cl):
    nk = cl + 1
    SC = HD ** -0.5
    items = [("cmp", 0)] + [("win", h) for h in range(NH)] + [("sel", h) for h in range(NH)]
    win_chunks = [(0, 512)] if cl == 0 else [(0, 512), (512, 128)]

    def chunks(item):
        return {"cmp": [(0, 512)], "win": win_chunks, "sel": [(512 * k, 512) for k in range(nk)]}[item[0]]

    def groups(item):
        return {"cmp": [4, 4], "win": [4] if cl == 0 else [4, 1], "sel": [4] * nk}[item[0]]
    NCK = sum(len(chunks(i)) for i in items)
    NG = sum(len(groups(i)) for i in items)
    first_group = [sum(len(groups(i)) for i in items[:j]) for j in range(len(items) + 1)]
    first_chunk = [sum(len(chunks(i)) for i in items[:j]) for j in range(len(items) + 1)]
    NI = len(items)
    BR = {"cmp": 0, "sel": 1, "win": 2}
    plain = t["plain"]

    with ExitStack() as ctx:
        pb = lambda n, s: ctx.enter_context(nc.psum_tensor(n, s, F32))
        sem = ctx.enter_context(semaphores(nc, f"pr{cl}_"))
        sp_ = [pb(f"ps_s{i}_{cl}", [128, 512]) for i in range(3)]
        tp_ = [pb(f"ps_p{i}_{cl}", [128, 4, 128]) for i in range(2)]
        O = [pb(f"ps_o{i}_{cl}", [128, NH, HD]) for i in range(3)]
        S, PT, q_, g_, gn = t["S"], t["PT"], t["q_tile"], t["g_tile"], t["gates_tok"]
        s_in, s_qk, s_ev, s_mx, s_exp, s_tp, s_pte, s_pv, s_gt, s_ge, s_comb, s_on, s_mo, s_cx, s_cp, s_dv, s_pw, s_ss, s_vr = \
            (sem(n) for n in (
                "tile_loaded", "scores_done", "scores_copied", "max_ready", "probs_ready", "probs_transposed",
                "transposed_copied", "values_done", "gates_transposed", "gates_copied", "outputs_read", "mix_normed", "mix_sent",
                "cmp_exp_done", "cmp_probs_ready", "dve_steps", "rstd_ready", "squares_summed", "variance_ready"))
        s_cs = sem("cmp_shifted")

        with nc.Block() as block:
            @block.sync
            def _(sp):
                with sp.Fori(0, 4) as i:
                    col = i * 128 + 512 * cl
                    sp.wait_ge(s_qk, NCK * i)
                    sp.wait_ge(s_gt, i)
                    sp.dma_start(q_[:], d["qT"][:, :, ds(col, 128)].rearrange("r p n -> p r n")).then_inc(s_in, 16)
                    sp.dma_start(g_[:], d["gT"][:, ds(col, 128)]).then_inc(s_in, 16)
                    sp.wait_ge(s_pte, (NG + 1) * (i + 1))
                    sp.dma_start(d["mixT"][0:4, :, ds(col, 128)].rearrange("r p n -> p r n"), t["mix_tile"][:]).then_inc(s_mo, 16)
                sp.wait_ge(s_mo, 64)

            @block.tensor
            def _(pe):
                with pe.Fori(0, 4) as i:
                    def scores(j):
                        kind, h = items[j]
                        g, r = h // 4, h % 4
                        for ci, (a, n) in enumerate(chunks(items[j])):
                            k = first_chunk[j] + ci
                            pe.wait_ge(s_ev, NCK * i + max(k - 2, 0))
                            if kind == "cmp":
                                for hh in range(NH):
                                    mm = pe.matmul(sp_[k % 3][:, 64 * hh:64 * hh + 64], q_[:, hh % 4], t["kcz"][:, hh // 4],
                                                   start=True, stop=True)
                            elif kind == "win" and cl:
                                keys = t["kw"][:, g, ds(i * 128 + (512 * cl - 512 + a), n)]
                                mm = pe.matmul(sp_[k % 3][:, 0:n], q_[:, r], keys, start=True, stop=True)
                            else:
                                keys = t["ks" if kind == "sel" else "kw"][:, g, a:a + n]
                                mm = pe.matmul(sp_[k % 3][:, 0:n], q_[:, r], keys, start=True, stop=True)
                            mm.then_inc(s_qk, 1)

                    def turn(q):
                        j = max(x for x in range(NI) if first_group[x] <= q)
                        kind, h = items[j]
                        gi = q - first_group[j]
                        if gi == 0:
                            if kind == "cmp":
                                pe.wait_ge(s_cp, i + 1)
                            else:
                                pe.wait_ge(s_exp, (NI - 1) * i + j)
                        free_bank(q)
                        plain(pe)
                        for y in range(groups(items[j])[gi]):
                            if kind == "cmp":
                                mm = pe.transpose(tp_[q % 2][0:64, y], S[:, j % 2, 256 * gi + 64 * y:256 * gi + 64 * y + 64],
                                                  t["ident"][:])
                            else:
                                a = 512 * gi + 128 * y
                                mm = pe.transpose(tp_[q % 2][:, y], S[:, j % 2, a:a + 128], t["ident"][:])
                        mm.then_inc(s_tp, 1)

                    def free_bank(q):
                        if q == 0:
                            pe.wait_ge(s_ge, i + 1)
                        else:
                            pe.wait_ge(s_pte, (NG + 1) * i + max(q - 1, 0))

                    def values(q):
                        j = max(x for x in range(NI) if first_group[x] <= q)
                        kind, h = items[j]
                        gi, g, n = q - first_group[j], h // 4, len(groups(items[j]))
                        pe.wait_ge(s_pte, (NG + 1) * i + q + 1)
                        if q == 0:
                            pe.wait_ge(s_comb, i)
                        for y in range(groups(items[j])[gi]):
                            if kind == "cmp":
                                hh = 4 * gi + y
                                mm = pe.matmul(O[0][:, hh], PT[0:64, q % 3, y], t["vcp"][:, 64 * gi:64 * gi + 64],
                                               start=True, stop=True)
                                continue
                            if kind == "win" and cl:
                                v = t["vw"][:, ds(i + (4 * cl - 4 + 4 * gi + y), 1), 64 * g:64 * g + 64].rearrange("p a n -> p (a n)")
                            else:
                                v = t["vs" if kind == "sel" else "vw"][:, 4 * gi + y, 64 * g:64 * g + 64]
                            mm = pe.matmul(O[BR[kind]][:, h], PT[:, q % 3, y], v, start=(gi == 0 and y == 0),
                                           stop=(gi == n - 1 and y == groups(items[j])[gi] - 1))
                        mm.then_inc(s_pv, 1)

                    pe.wait_ge(s_in, 32 * (i + 1))
                    pe.wait_ge(s_pte, (NG + 1) * i)
                    plain(pe)
                    pe.transpose(tp_[0][:, 0, 0:24], g_[:], t["ident"][0:24, 0:24]).then_inc(s_gt, 1)
                    scores(0)
                    for j in range(NI):
                        if j + 1 < NI:
                            scores(j + 1)
                        for q in range(first_group[j], first_group[j + 1]):
                            turn(q)
                            if q:
                                values(q - 1)
                    values(NG - 1)
                    pe.wait_ge(s_on, i + 1)
                    free_bank(NG)
                    for y in range(4):
                        mm = pe.transpose(tp_[NG % 2][:, y], t["o_att"][:, 128 * y:128 * y + 128], t["ident"][:])
                    mm.then_inc(s_tp, 1)

            @block.scalar
            def _(act):
                with act.Fori(0, 4) as i:
                    act.wait_ge(s_gt, i + 1)
                    act.wait_ge(s_comb, i)
                    act.activation(gn[:], tp_[0][:, 0, 0:24], ACT.Copy).then_inc(s_ge, 1)
                    act.wait_ge(s_cs, i + 1)
                    act.activation(S[:, 0, 0:512], S[:, 0, 0:512], ACT.Exp).then_inc(s_cx, 1)

                    def exp(j):
                        n = sum(c[1] for c in chunks(items[j]))
                        act.wait_ge(s_mx, (NI - 1) * i + j)
                        act.activation(S[:, j % 2, 0:n], S[:, j % 2, 0:n], ACT.Exp, bias=t["nmax"][:, j % 2:j % 2 + 1],
                                       accum_out=t["rsum"][:, j - 1:j]).then_inc(s_exp, 1)

                    def copy(q, n, rows):
                        act.wait_ge(s_tp, (NG + 1) * i + q + 1)
                        act.wait_ge(s_pv, NG * i + max(q - 2, 0))
                        act.activation(PT[0:rows, q % 3, 0:n], tp_[q % 2][0:rows, 0:n], ACT.Copy).then_inc(s_pte, 1)
                    for j in range(NI):
                        for gi, n in enumerate(groups(items[j])):
                            copy(first_group[j] + gi, n, 64 if j == 0 else 128)
                        if j + 1 < NI:
                            exp(j + 1)
                    act.wait_ge(s_tp, (NG + 1) * (i + 1))
                    act.wait_ge(s_mo, 16 * i)
                    for y in range(4):
                        ins = act.activation(t["mix_tile"][:, y], tp_[NG % 2][:, y], ACT.Copy, scale=t["att_gain"][:, y:y + 1])
                    ins.then_inc(s_pte, 1)

            @block.gpsimd
            def _(pool):
                with pool.Fori(0, 4) as i:
                    pool.wait_ge(s_vr, i + 1)
                    pool.tensor_tensor(t["rstd"][:], t["var"][:], t["half"][:], ALU.pow).then_inc(s_pw, 1)

            @block.vector
            def _(dve):
                own = Own(dve)
                step = lambda ins: own(ins, s_dv, 2 + 13 + NH + 8 + (2 * NH if cl else 0))
                bc = lambda a, n: a.rearrange("p (h o) -> p h o", o=1).to_broadcast([128, a.shape[1], n])
                with dve.Fori(0, 4) as i:
                    own.iteration(i)

                    def band(h, lo, n):
                        return t["band"][:, h, ds(i * -128 + (512 + lo), n)]

                    dve.wait_ge(s_qk, NCK * i + 1)
                    dve.wait_ge(s_tp, (NG + 1) * i)
                    p = S[:, 0, 0:512].rearrange("p (h n) -> p h n", n=64)
                    cb = t["cband"][:, :, ds(i * -4 + (60 - 16 * cl), 64)]
                    own(dve.scalar_tensor_tensor(p, sp_[0][:].rearrange("p (h n) -> p h n", n=64), SC, cb, ALU.mult, ALU.add),
                        s_ev, NCK)
                    m8, r8 = t["cmax"], t["csum"]
                    step(dve.tensor_reduce(m8[:], p, X, ALU.max))
                    step(dve.tensor_scalar(m8[:], m8[:], -1e20, None, ALU.max))
                    own(dve.tensor_tensor(p, p, bc(m8[:], 64), ALU.subtract), s_cs, 1)

                    def fetch(j):
                        kind, h = items[j]
                        g, b = h // 4, j % 2
                        n = sum(c[1] for c in chunks(items[j]))
                        dve.wait_ge(s_tp, (NG + 1) * i + (first_group[j - 1] if j >= 2 else 0))
                        for ci, (a, w) in enumerate(chunks(items[j])):
                            k = first_chunk[j] + ci
                            dve.wait_ge(s_qk, NCK * i + k + 1)
                            src, dst = sp_[k % 3][:, 0:w], S[:, b, a:a + w]
                            blocks = lambda z: z.rearrange("p (b k) -> p b k", k=64)
                            mask = bc(t["mask"][:, g, 8 * ci:8 * ci + 8], 64)
                            if kind == "win" and cl:
                                own(dve.scalar_tensor_tensor(dst, src, SC, t["band"][:, h, a:a + w], ALU.mult, ALU.add), s_ev, NCK)
                                if ci == 0:
                                    step(dve.tensor_tensor(S[:, b, 0:128], S[:, b, 0:128], t["tri"][:], ALU.add))
                            elif kind == "win" or ci == nk - 1:
                                own(dve.scalar_tensor_tensor(dst, src, SC, band(h, 0, 512), ALU.mult, ALU.add), s_ev, NCK)
                                if kind == "sel":
                                    step(dve.tensor_tensor(blocks(dst), blocks(dst), mask, ALU.add))
                            else:
                                own(dve.scalar_tensor_tensor(blocks(dst), blocks(src), SC, mask, ALU.mult, ALU.add), s_ev, NCK)
                                if ci == nk - 2:
                                    e = S[:, b, a + 384:a + 512]
                                    step(dve.tensor_tensor(e, e, band(h, -128, 128), ALU.add))
                        own(dve.tensor_reduce(t["nmax"][:, b:b + 1], S[:, b, 0:n], X, ALU.max, negate=True), s_mx, NI - 1)

                    fetch(1)
                    dve.wait_ge(s_cx, i + 1)
                    step(dve.tensor_reduce(r8[:], p, X, ALU.add))
                    step(dve.tensor_scalar(r8[:], r8[:], 1e-30, None, ALU.max))
                    step(dve.reciprocal(r8[:], r8[:]))
                    own(dve.tensor_tensor(p, p, bc(r8[:], 64), ALU.mult), s_cp, 1)
                    imp = t["imp"]
                    for g in range(2):
                        pv = S[:, 0, 256 * g:256 * g + 256].rearrange("p (r j w) -> p j r w", r=4, w=2)
                        step(dve.tensor_reduce(imp[:, g], pv, XY, ALU.add))
                    sbw = t["score_band"][:, ds(i * -2 + (30 - 8 * cl), 32)]
                    for g in range(2):
                        step(dve.tensor_tensor(imp[:, g], imp[:, g], sbw, ALU.add))
                    step(dve.tensor_scalar(imp[:, :, 0], imp[:, :, 0], 1e4, None, ALU.max))
                    for g in range(2):
                        plain(dve)
                        step(dve.max(t["top"][:, g], imp[:, g]))
                        plain(dve)
                        step(dve.match_replace(t["mask"][:, g], t["top"][:, g], imp[:, g], -2e30))
                    step(dve.tensor_scalar(t["mask"][:], t["mask"][:], -1.5e30, NEG, ALU.is_gt, ALU.mult))
                    for j in range(2, NI):
                        fetch(j)

                    dve.wait_ge(s_exp, (NI - 1) * (i + 1))
                    dve.wait_ge(s_ge, i + 1)
                    rs, o, o2 = t["rsum"], t["o_att"], t["o_tmp"]
                    step(dve.reciprocal(rs[:], rs[:]))
                    step(dve.tensor_tensor(rs[:, 0:8], rs[:, 0:8], gn[:, 16:24], ALU.mult))
                    step(dve.tensor_tensor(rs[:, 8:16], rs[:, 8:16], gn[:, 8:16], ALU.mult))
                    hv = lambda a: a.rearrange("p (h n) -> p h n", n=64)
                    dve.wait_ge(s_pv, NG * (i + 1))
                    step(dve.tensor_tensor(hv(o[:]), O[0][:], bc(gn[:, 0:8], 64), ALU.mult))
                    for br, cf in ((2, rs[:, 0:8]), (1, rs[:, 8:16])):
                        ins = dve.tensor_tensor(hv(o2[:]), O[br][:], bc(cf, 64), ALU.mult)
                        if br == 1:
                            own(ins, s_comb, 1)
                        else:
                            step(ins)
                        step(dve.tensor_tensor(o[:], o[:], o2[:], ALU.add))
                    own(dve.tensor_tensor(o2[:], o[:], o[:], ALU.mult), s_ss, 1)
                    step(dve.tensor_reduce(t["var"][:], o2[:], X, ALU.add))
                    own(dve.tensor_scalar(t["var"][:], t["var"][:], 1 / 512, EPS, ALU.mult, ALU.add), s_vr, 1)
                    dve.wait_ge(s_pw, i + 1)
                    own(dve.tensor_scalar(o[:], o[:], t["rstd"][:, 0:1], None, ALU.mult), s_on, 1)
                own.close()


def sample(nc, d, t):
    ROWS = NB * NH
    with ExitStack() as ctx:
        sb = lambda n, s, dt=F32: ctx.enter_context(nc.sbuf_tensor(n, s, dt))
        pb = lambda n, s: ctx.enter_context(nc.psum_tensor(n, s, F32))
        sem = ctx.enter_context(semaphores(nc, "sm_"))
        wk, wv = sb("win_k", [128, NB, 512]), sb("win_v", [128, NB, 4, 128])
        kg, vg = sb("sel_k", [64, NB, 2, 8, 64]), sb("sel_v", [128, NB, 2, 4, 64])
        ksn = sb("new_ks", [64, 2, NB])
        kwn = sb("new_kw", [128, NB])
        qz, qs = sb("q_padded", [128, NH, NB]), sb("q_groups", [64, 2, 4, NB])
        gr = sb("gate_rows", [ROWS, 3])
        bias = {"cmp": sb("bias_cmp", [ROWS, 256]), "win": sb("bias_win", [ROWS, 512]), "sel": sb("bias_sel", [ROWS, 512])}
        near = sb("bias_near", [ROWS, 64])
        pti, pb2 = sb("pages_int", [ROWS, NPAGE], I32), sb("phys_block", [ROWS, NPAGE, 2])
        iota, own4, own8 = sb("iota", [ROWS, 128]), sb("same_group", [ROWS, ROWS]), sb("same_token", [ROWS, ROWS])
        side = sb("group_rows", [ROWS, 2])
        gain = sb("gain_rows", [ROWS, HD])
        sT, R = sb("scores_T", [128, 4, ROWS]), {k: sb("rows_" + k, [ROWS, n]) for k, n in (("cmp", 256), ("win", 512), ("sel", 512))}
        pT = {k: sb("probs_T_" + k, [128, n, ROWS]) for k, n in (("cmp", 2), ("win", 4), ("sel", 4))}
        imp, junk = sb("importance", [ROWS, 128]), sb("picked", [ROWS, 128])
        top, idx, idf, ind = sb("top", [ROWS, 8]), sb("top_index", [ROWS, 8], U32), sb("top_float", [ROWS, 8]), sb("is_last", [ROWS, 8])
        ph, phi, prow = sb("phys", [ROWS, 7]), sb("phys_int", [ROWS, 7], I32), sb("phys_row", [1, ROWS * 7], I32)
        mx, rsm = sb("row_max", [ROWS, 3]), sb("row_sum", [ROWS, 3])
        aw, dd, o = sb("out_cmp_win", [128, ROWS]), sb("out_sel", [64, ROWS]), sb("o_rows", [ROWS, HD])
        o2, ss, sd = sb("o_scratch", [ROWS, HD]), sb("o_sumsq", [ROWS, 1]), sb("o_std", [ROWS, 1])
        om = sb("o_heads", [HD, NH, NB])
        psS, psR, psP = pb("ps_sT", [128, 4, ROWS]), pb("ps_rows", [ROWS, 4, 128]), pb("ps_pT", [128, 4, ROWS])
        psI, psA, psD, psX = pb("ps_imp", [ROWS, 128]), pb("ps_aw", [128, ROWS]), pb("ps_sel_o", [64, ROWS]), pb("ps_turn", [64, 256])
        s_z, s_c, s_n, s_wo, s_ph, s_pr, s_sel, s_mm, s_dv, s_ac, s_mo = (sem(n) for n in (
            "cleared", "inputs_loaded", "new_token_placed", "window_out", "phys_stored", "phys_loaded", "selected_loaded",
            "pe_steps", "dve_steps", "act_steps", "mix_sent"))
        s_wl = sem("window_loaded")
        col = slice(SEQ, NTOK)
        PE = ["sT_cmp", "R_cmp", "imp", "pT_cmp", "sT_win", "R_win", "pT_win", "sT_sel", "R_sel", "pT_sel", "aw", "sel_o",
              "turn", "token_sum", "heads"]
        pe_at = {n: i + 1 for i, n in enumerate(PE)}
        DV = ["sc_cmp", "s_cmp", "nm_cmp", "rec_cmp", "p_cmp", "pair_sum", "imp", "top", "index", "float", "plus_one", "pages_f", "even", "odd",
              "pick0", "pick1", "pick2", "pick3", "pick4", "ph1", "ph2", "phys_int", "gated_cmp", "c_pT_cmp",
              "new_kw", "new_ks", "sc_win", "s_win", "nm_win", "rec_win", "p_win", "c_pT_win",
              "is_last", "b3", "b4", "b5", "b6", "b7", "sc_sel", "s_sel", "nm_sel", "rec_sel", "p_sel", "c_pT_sel",
              "c_aw", "c_dd", "o_a", "o_b", "o_c", "o_sq", "o_ss", "std_r", "o_n", "o_g", "c_heads"]
        dv_at = {n: i + 1 for i, n in enumerate(DV)}
        n_in = 5 + 2 + 4 + 8 * (1 + 1 + 1 + 3 + 1 + 1)

        with nc.Block() as block:
            @block.gpsimd
            def _(pool):
                own = Own(pool)
                for a, v in ((qz[:], 0.0), (kg[:, :, :, 0], 0.0), (vg[0:64, :, :, 0], 0.0), (bias["cmp"][:], 0.0),
                             (bias["sel"][:, 0:64], NEG), (bias["sel"][:, 64:128], 0.0)):
                    own(pool.memset(a, v), s_z, 6)

            @block.sync
            def _(sp):
                ld = lambda a, b: sp.dma_start(a, b).then_inc(s_c, 16)
                for b in range(NB):
                    sp.dma_start(wk[:, b, 0:511], d["win_k"][b, :, 1:512]).then_inc(s_wl, 16)
                    for ti in range(4):
                        n = 127 if ti == 3 else 128
                        sp.dma_start(wv[0:n, b, ti], d["win_v"][b, 128 * ti + 1:128 * ti + 1 + n]).then_inc(s_wl, 16)
                with nc.allow_non_contiguous_dma(reason="one new token"):
                    for b in range(NB):
                        sp.dma_start(wv[127:128, b, 3], d["kvT"][KVROW["vw"], :, SEQ + b:SEQ + b + 1].rearrange("p n -> n p")).then_inc(s_wl, 16)
                ld(kwn[:], d["kvT"][KVROW["kw"], :, col])
                for a, n in ((iota, "iota"), (own4, "same_group"), (own8, "same_token"), (side, "group_rows")):
                    ld(a[:], d[n])
                for g in range(2):
                    ld(ksn[:, g], d["kvT"][KVROW["ks"], 64 * g:64 * g + 64, col])
                sp.wait_ge(s_z, 6)
                for g in range(2):
                    r = slice(64 * g, 64 * g + 64)
                    ld(qz[r, 4 * g:4 * g + 4], d["qT"][:, r, col].rearrange("r p n -> p r n"))
                    ld(qs[:, g], d["qT"][:, r, col].rearrange("r p n -> p r n"))
                with nc.allow_non_contiguous_dma(reason="a few values per row"):
                    for b in range(NB):
                        r = slice(NH * b, NH * b + NH)
                        for g in range(2):
                            src = d["kvT"][KVROW["vs"], 64 * g:64 * g + 64, SEQ + b:SEQ + b + 1].rearrange("p n -> n p")
                            sp.dma_start(vg[0:1, b, g, 0], src).then_inc(s_n, 16)
                        ld(gr[r], d["gT"][:, SEQ + b:SEQ + b + 1].rearrange("(k h) n -> h (k n)", k=3))
                        ld(bias["cmp"][r, 252:256], d["line"][:, 543:640:32])
                        ld(bias["win"][r], d["line"][:, 129:641])
                        ld(bias["sel"][r, 0:1], d["line"][:, 640:641])
                        ld(bias["sel"][r, 128:192], d["line"][:, 576:640])
                        ld(near[r], d["line"][:, 512:576])
                        ld(pti[r], d["page_table"][0:1, NPAGE * b:NPAGE * (b + 1)].to_broadcast([NH, NPAGE]))
                        ld(gain[r], d["out_gain"])
                sp.dma_start(d["conv_prev"], d["state_conv"][:, :, 1]).then_inc(s_wo, 16)
                sp.wait_ge(s_dv, dv_at["new_kw"])
                sp.wait_ge(s_wl, 16 * 6 * NB)
                sp.dma_start(d["win_k_out"].rearrange("b p n -> p b n"), wk[:]).then_inc(s_wo, 16)
                sp.dma_start(d["win_v_out"].rearrange("b (t p) n -> p b t n", p=128), wv[:]).then_inc(s_wo, 16)
                sp.wait_ge(s_dv, dv_at["phys_int"])
                sp.dma_start(d["phys"], phi[:]).then_inc(s_ph, 16)
                sp.wait_ge(s_ph, 16)
                sp.dma_start(prow[:], d["phys"].rearrange("r s -> (r s)").rearrange("(o n) -> o n", o=1)).then_inc(s_pr, 16)
                sp.wait_ge(s_pr, 16)
                with sp.Fori(0, NB) as b:
                    for g in range(2):
                        for s in range(7):
                            v = sp.value_load(prow[0:1, ds(b * 56 + (28 * g + s), 1)], min_val=0, max_val=d["sel_k"].shape[0] - 1)
                            sp.dma_start(kg[:, ds(b, 1), g, s + 1].rearrange("p a n -> p (a n)"),
                                         d["sel_k"][ds(v, 1), g].rearrange("a p n -> (a p) n")).then_inc(s_sel, 16)
                sp.wait_ge(s_dv, dv_at["c_heads"])
                dst = d["mixT"][0:4].rearrange("j (a d) n -> d (j a) n", a=2)[:, :, col]
                sp.dma_start(dst, om[:]).then_inc(s_mo, 16)
                sp.wait_ge(s_mo, 16)
                sp.wait_ge(s_wo, 48)

            @block.tensor
            def _(pe):
                def done(mm):
                    mm.then_inc(s_mm, 1)

                def rows(k, n):
                    for y in range(n):
                        mm = pe.transpose(psR[:, y], sT[:, y], t["ident"][:])
                    done(mm)

                def probs(k, n):
                    for y in range(n):
                        mm = pe.transpose(psP[:, y], R[k][:, 128 * y:128 * y + 128], t["ident"][0:ROWS, 0:ROWS])
                    done(mm)
                pe.wait_ge(s_c, 16 * n_in)
                for b in range(NB):
                    for y in range(2):
                        a = NCP + 256 * b + 128 * y
                        mm = pe.matmul(psS[:, y, NH * b:NH * b + NH], t["kcT"][:, a:a + 128], qz[:, :, b], start=True, stop=True)
                done(mm)
                pe.wait_ge(s_dv, dv_at["sc_cmp"])
                rows("cmp", 2)
                pe.wait_ge(s_dv, dv_at["pair_sum"])
                done(pe.matmul(psI[:], own4[:], junk[:], start=True, stop=True))
                pe.wait_ge(s_dv, dv_at["gated_cmp"])
                probs("cmp", 2)
                pe.wait_ge(s_dv, dv_at["new_kw"])
                for b in range(NB):
                    for y in range(4):
                        mm = pe.matmul(psS[:, y, NH * b:NH * b + NH], wk[:, b, 128 * y:128 * y + 128], qz[:, :, b],
                                       start=True, stop=True)
                done(mm)
                pe.wait_ge(s_dv, dv_at["sc_win"])
                rows("win", 4)
                pe.wait_ge(s_dv, dv_at["p_win"])
                probs("win", 4)
                pe.wait_ge(s_sel, 16 * 2 * 2 * 7 * NB)
                pe.wait_ge(s_n, 16 * 2 * NB)
                for b in range(NB):
                    for g in range(2):
                        for y in range(4):
                            a = NH * b + 4 * g
                            mm = pe.matmul(psS[:, y, a:a + 4], kg[:, b, g, 2 * y:2 * y + 2].rearrange("p s n -> p (s n)"),
                                           qs[:, g, :, b], start=True, stop=True)
                done(mm)
                pe.wait_ge(s_dv, dv_at["sc_sel"])
                rows("sel", 4)
                pe.wait_ge(s_dv, dv_at["p_sel"])
                probs("sel", 4)
                pe.wait_ge(s_dv, dv_at["c_pT_sel"])
                for b in range(NB):
                    a = NH * b
                    for y in range(2):
                        pe.matmul(psA[:, a:a + NH], t["vcs"][:, 2 * b + y], pT["cmp"][:, y, a:a + NH], start=(y == 0), stop=False)
                    for y in range(4):
                        mm = pe.matmul(psA[:, a:a + NH], wv[:, b, y], pT["win"][:, y, a:a + NH], start=False, stop=(y == 3))
                done(mm)
                for b in range(NB):
                    for g in range(2):
                        a = NH * b + 4 * g
                        for y in range(4):
                            mm = pe.matmul(psD[:, a:a + 4], vg[:, b, g, y], pT["sel"][:, y, a:a + 4], start=(y == 0), stop=(y == 3))
                done(mm)
                pe.wait_ge(s_dv, dv_at["c_dd"])
                pe.transpose(psX[:, 0:128], aw[:], t["ident"][:])
                done(pe.transpose(psX[:, 128:192], dd[:], t["ident"][0:64, 0:64]))
                pe.wait_ge(s_dv, dv_at["o_ss"])
                done(pe.matmul(psI[:, 0:1], own8[:], ss[:], start=True, stop=True))
                pe.wait_ge(s_dv, dv_at["o_g"])
                done(pe.transpose(psX[:, 192:256], o[:], t["ident"][0:64, 0:64]))

            @block.scalar
            def _(act):
                def exp(k, i):
                    act.wait_ge(s_dv, dv_at["nm_" + k])
                    act.activation(R[k][:], R[k][:], ACT.Exp, bias=mx[:, i:i + 1], accum_out=rsm[:, i:i + 1]).then_inc(s_ac, 1)
                exp("cmp", 0)
                act.wait_ge(s_pr, 16)
                with act.Fori(0, NB) as b:
                    for g in range(2):
                        for s in range(7):
                            v = act.value_load(prow[0:1, ds(b * 56 + (28 * g + s), 1)], min_val=0, max_val=d["sel_k"].shape[0] - 1)
                            q = 64 * ((s + 1) % 2)
                            act.dma_start(vg[q:q + 64, ds(b, 1), g, (s + 1) // 2].rearrange("p a n -> p (a n)"),
                                          d["sel_v"][ds(v, 1), g].rearrange("a p n -> (a p) n")).then_inc(s_sel, 16)
                exp("win", 1)
                exp("sel", 2)
                act.wait_ge(s_mm, pe_at["token_sum"])
                act.activation(sd[:], psI[:, 0:1], ACT.Sqrt, bias=t["eps"][0:ROWS]).then_inc(s_ac, 1)

            @block.vector
            def _(dve):
                n = [0]

                def step(name, ins):
                    assert DV[n[0]] == name, (DV[n[0]], name)
                    n[0] += 1
                    ins.then_inc(s_dv, 1)
                    dve.wait_ge(s_dv, n[0])
                SC = HD ** -0.5

                def scores(k, tiles):
                    dve.wait_ge(s_mm, pe_at["sT_" + k])
                    step("sc_" + k, dve.tensor_copy(sT[:, 0:tiles], psS[:, 0:tiles]))
                    dve.wait_ge(s_mm, pe_at["R_" + k])
                    src = psR[:, 0:tiles].rearrange("p a b -> p (a b)")
                    step("s_" + k, dve.scalar_tensor_tensor(R[k][:], src, SC, bias[k][:], ALU.mult, ALU.add))
                    i = "cmp win sel".split().index(k)
                    step("nm_" + k, dve.tensor_reduce(mx[:, i:i + 1], R[k][:], X, ALU.max, negate=True))
                    dve.wait_ge(s_ac, i + 1)

                dve.wait_ge(s_c, 16 * n_in)
                scores("cmp", 2)
                p = R["cmp"]
                step("rec_cmp", dve.reciprocal(rsm[:, 0:1], rsm[:, 0:1]))
                step("p_cmp", dve.tensor_scalar(p[:], p[:], rsm[:, 0:1], None, ALU.mult))
                pv = p[:].rearrange("p (j w) -> p j w", w=2)
                step("pair_sum", dve.scalar_tensor_tensor(junk[:], pv[:, :, 0], 1.0, pv[:, :, 1], ALU.mult, ALU.add))
                dve.wait_ge(s_mm, pe_at["imp"])
                step("imp", dve.tensor_copy(imp[:], psI[:]))
                step("top", dve.max(top[:], imp[:, 1:127]))
                step("index", dve.max_index(idx[:], top[:], imp[:, 1:127]))
                step("float", dve.tensor_copy(idf[:], idx[:]))
                step("plus_one", dve.tensor_scalar(idf[:], idf[:], 1.0, None, ALU.add))
                step("pages_f", dve.tensor_copy(pb2[:, :, 1], pti[:]))
                step("even", dve.tensor_scalar(pb2[:, :, 0], pb2[:, :, 1], 2.0, None, ALU.mult))
                step("odd", dve.tensor_scalar(pb2[:, :, 1], pb2[:, :, 0], 1.0, None, ALU.add))
                blocks = pb2[:].rearrange("p a b -> p (a b)")
                for k in range(5):
                    step(f"pick{k}", dve.scalar_tensor_tensor(junk[:], iota[:], idf[:, k:k + 1], blocks, ALU.is_equal, ALU.mult,
                                                              accum_out=ph[:, 2 + k:3 + k]))
                step("ph1", dve.tensor_copy(ph[:, 0:1], blocks[:, 0:1]))
                step("ph2", dve.tensor_copy(ph[:, 1:2], blocks[:, 127:128]))
                step("phys_int", dve.tensor_copy(phi[:], ph[:]))
                step("gated_cmp", dve.tensor_scalar(p[:], p[:], gr[:, 0:1], None, ALU.mult))
                dve.wait_ge(s_mm, pe_at["pT_cmp"])
                step("c_pT_cmp", dve.tensor_copy(pT["cmp"][:], psP[:, 0:2]))
                dve.wait_ge(s_wl, 16 * 6 * NB)
                step("new_kw", dve.tensor_copy(wk[:, :, 511], kwn[:]))
                step("new_ks", dve.tensor_copy(kg[:, :, :, 0, 0].rearrange("p b g -> p g b"), ksn[:]))

                def weigh(k, i, g):
                    step("p_" + k, dve.tensor_scalar(R[k][:], R[k][:], rsm[:, i:i + 1], gr[:, g:g + 1], ALU.mult, ALU.mult))
                scores("win", 4)
                step("rec_win", dve.reciprocal(rsm[:, 1:2], rsm[:, 1:2]))
                weigh("win", 1, 2)
                dve.wait_ge(s_mm, pe_at["pT_win"])
                step("c_pT_win", dve.tensor_copy(pT["win"][:], psP[:]))
                step("is_last", dve.tensor_scalar(ind[:], idf[:], 126.0, None, ALU.is_equal))
                for k in range(5):
                    step(f"b{3 + k}", dve.tensor_scalar(bias["sel"][:, 64 * (3 + k):64 * (4 + k)], near[:], ind[:, k:k + 1], None, ALU.mult))
                scores("sel", 4)
                step("rec_sel", dve.reciprocal(rsm[:, 2:3], rsm[:, 2:3]))
                weigh("sel", 2, 1)
                dve.wait_ge(s_mm, pe_at["pT_sel"])
                step("c_pT_sel", dve.tensor_copy(pT["sel"][:], psP[:]))
                dve.wait_ge(s_mm, pe_at["aw"])
                step("c_aw", dve.tensor_copy(aw[:], psA[:]))
                dve.wait_ge(s_mm, pe_at["sel_o"])
                step("c_dd", dve.tensor_copy(dd[:], psD[:]))
                dve.wait_ge(s_mm, pe_at["turn"])
                step("o_a", dve.tensor_scalar(o2[:], psX[:, 0:64], side[:, 0:1], None, ALU.mult))
                step("o_b", dve.scalar_tensor_tensor(o[:], psX[:, 64:128], side[:, 1:2], o2[:], ALU.mult, ALU.add))
                step("o_c", dve.tensor_tensor(o[:], o[:], psX[:, 128:192], ALU.add))
                step("o_sq", dve.tensor_tensor(o2[:], o[:], o[:], ALU.mult))
                step("o_ss", dve.tensor_reduce(ss[:], o2[:], X, ALU.add))
                dve.wait_ge(s_ac, 4)
                step("std_r", dve.reciprocal(sd[:], sd[:]))
                step("o_n", dve.tensor_scalar(o[:], o[:], sd[:, 0:1], None, ALU.mult))
                step("o_g", dve.tensor_tensor(o[:], o[:], gain[:], ALU.mult))
                dve.wait_ge(s_mm, pe_at["heads"])
                step("c_heads", dve.tensor_copy(om[:], psX[:, 192:256].rearrange("p (b h) -> p h b", h=NH)))
                assert n[0] == len(DV)


def tail(nc, d, t):
    NU = 8 + 32 + 32 + 8 + 2
    RING = 6
    with ExitStack() as ctx:
        sb = lambda n, s, dt=F32: ctx.enter_context(nc.sbuf_tensor(n, s, dt))
        pb = lambda n, s: ctx.enter_context(nc.psum_tensor(n, s, F32))
        sem = ctx.enter_context(semaphores(nc, "tl_"))
        h = sb("h", [128, KT, CH])
        mx = sb("mix_chunk", [128, KT, CH])
        pT = sb("p_chunk", [128, 2, CH])
        ff = sb("ff", [128, FT, CH])
        sq = sb("h_square", [128, 2, CH])
        rs = sb("rstd_h", [128, CH])
        gate = sb("gate", [128, 2, CH])
        wr = sb("w_ring", [128, RING, 8, 128])
        gm = sb("norm_mlp_sb", [128, KT])
        gp = sb("norm_ple_sb", [128, KT])
        zp = [pb(f"ps_t{i}", [128, 2, 512]) for i in range(3)]
        ssp = pb("ps_hs", [128, 2, 512])
        V = lambda ps: ps[:, :, 0:HF]
        W = lambda a: a.rearrange("p (h n) -> p h n", h=2)
        s_c, s_in, s_o, s_wu, s_o1, s_h1, s_sq, s_sqf, s_rs, s_a, s_u, s_ut, s_f, s_dn, s_h2, s_g, s_gs, s_pj, s_y, s_rt = \
            (sem(n) for n in (
                "consts_loaded", "inputs_loaded", "y_sent", "unit_used", "wout_done", "h1_ready", "h_squared",
                "h_square_summed", "rstd_ready", "a_ready", "up_done", "up_taken", "ff_ready", "down_done", "h2_ready", "gate_done",
                "gate_ready", "proj_done", "y_ready", "roots_taken"))
        s_w = [sem(f"w{i}") for i in range(RING)]
        per_slot = [len(range(s, NU, RING)) for s in range(RING)]

        with nc.Block() as block:
            @block.sync
            def _(sp):
                sp.dma_start(gm[:], d["norm_mlp"]).then_inc(s_c, 16)
                sp.dma_start(gp[:], d["norm_ple"]).then_inc(s_c, 16)

                def load_unit(un):
                    sp.dma_start(wr[:, un % RING], d["w_tail"][un]).then_inc(s_w[un % RING], 16)

                def load_in(c):
                    sp.dma_start(h[:], d["xT"][:, :, ds(c * CH, CH)].rearrange("k p n -> p k n")).then_inc(s_in, 16)
                    sp.dma_start(mx[:], d["mixT"][:, :, ds(c * CH, CH)].rearrange("k p n -> p k n")).then_inc(s_in, 16)
                    sp.dma_start(pT[:], d["pT"][:, :, ds(c * CH, CH)].rearrange("k p n -> p k n")).then_inc(s_in, 16)

                load_in(0)
                for un in range(RING):
                    load_unit(un)

                def body(c, last):
                    for un in range(RING, NU):
                        sp.wait_ge(s_wu, NU * c + un - RING + 1)
                        load_unit(un)
                    if not last:
                        for un in range(RING):
                            before = max(range(un, NU, RING))
                            sp.wait_ge(s_wu, NU * c + before + 1)
                            load_unit(un)
                    for k in range(KT):
                        sp.wait_ge(s_y, KT * c + k + 1)
                        sp.dma_start(d["yT"][k, :, ds(c * CH, CH)], h[:, k]).then_inc(s_o, 16)
                    if not last:
                        sp.wait_ge(s_o, 16 * KT * (c + 1))
                        load_in(c + 1)
                with sp.Fori(0, 3) as c:
                    body(c, False)
                body(3, True)
                sp.wait_ge(s_o, 16 * KT * 4)

            @block.tensor
            def _(pe):
                with pe.Fori(0, 4) as c:
                    un = [0]

                    def unit():
                        n = un[0]
                        pe.wait_ge(s_w[n % RING], 16 * (per_slot[n % RING] * c + n // RING + 1))
                        return wr[:, n % RING]

                    def used(mm):
                        mm.then_inc(s_wu, 1)
                        un[0] += 1

                    def sums(k0):
                        for k in range(KT):
                            pe.wait_ge(s_sq, 2 * KT * c + k0 + k + 1)
                            for hh in range(2):
                                mm = pe.matmul(ssp[:, hh, 0:HF], t["ones_d"][:], sq[:, k % 2, hh * HF:(hh + 1) * HF],
                                               start=(k == 0), stop=(k == KT - 1))
                            mm.then_inc(s_sqf, 1)

                    def tile(zi, src, ks, w, first=True, final=True):
                        for hh in range(2):
                            for i, k in enumerate(ks):
                                mm = pe.matmul(zp[zi][:, hh, 0:HF], w[:, i], src[:, k, hh * HF:(hh + 1) * HF],
                                               start=(first and i == 0), stop=(final and i == len(ks) - 1),
                                               skip_group_check=True)
                        return mm

                    pe.wait_ge(s_in, 48 * c + 48)
                    for m in range(KT):
                        w = unit()
                        if m >= 3:
                            pe.wait_ge(s_h1, KT * c + m - 2)
                        used(tile(m % 3, mx, range(KT), w))
                    sums(0)
                    pe.wait_ge(s_a, 2 * KT * c + KT)
                    for m in range(FT):
                        w = unit()
                        if m >= 3:
                            pe.wait_ge(s_ut, FT * c + m - 2)
                        used(tile(m % 3, mx, range(KT), w))
                    pe.wait_ge(s_f, FT * (c + 1))
                    for m in range(KT):
                        if m >= 3:
                            pe.wait_ge(s_h2, KT * c + m - 2)
                        for g in range(4):
                            w = unit()
                            used(tile(m % 3, ff, range(8 * g, 8 * g + 8), w, g == 0, g == 3))
                    sums(KT)
                    pe.wait_ge(s_a, 2 * KT * (c + 1))
                    for m in range(KT):
                        w = unit()
                        if m >= 2:
                            pe.wait_ge(s_gs, KT * c + m - 1)
                        used(tile(m % 2, mx, range(KT), w))
                    for m in range(KT):
                        if m % 4 == 0:
                            w = unit()
                        if m >= 1:
                            pe.wait_ge(s_y, KT * c + m)
                        mm = tile(2, pT, range(2), w[:, 2 * (m % 4):2 * (m % 4) + 2])
                        if m % 4 == 3:
                            used(mm)
                        else:
                            mm.then_inc(s_pj, 1)

            @block.scalar
            def _(act):
                with act.Fori(0, 4) as c:
                    for r in range(2):
                        for k in range(KT):
                            if r == 0:
                                act.wait_ge(s_h1, KT * c + k + 1)
                            else:
                                act.wait_ge(s_h2, KT * c + k + 1)
                            if k >= 2:
                                act.wait_ge(s_sqf, 2 * KT * c + KT * r + k - 1)
                            act.activation(sq[:, k % 2], h[:, k], ACT.Square).then_inc(s_sq, 1)
                        act.wait_ge(s_sqf, 2 * KT * c + KT * (r + 1))
                        act.activation(W(rs[:]), V(ssp), ACT.Sqrt, bias=t["eps"][:]).then_inc(s_rt, 1)
                        if r == 0:
                            for m in range(FT):
                                act.wait_ge(s_wu, NU * c + KT + m + 1)
                                act.activation(W(ff[:, m]), V(zp[m % 3]), ACT.Relu).then_inc(s_ut, 1)
                    for m in range(KT):
                        act.wait_ge(s_wu, NU * c + KT + 2 * FT + m + 1)
                        act.activation(W(ff[:, m]), V(zp[m % 2]), ACT.Sigmoid).then_inc(s_gs, 1)

            @block.vector
            def _(dve):
                dve.wait_ge(s_c, 32)
                own = Own(dve)
                with dve.Fori(0, 4) as c:
                    own.iteration(c)
                    dve.wait_ge(s_in, 48 * c + 48)
                    for m in range(KT):
                        dve.wait_ge(s_wu, NU * c + m + 1)
                        own(dve.tensor_tensor(W(h[:, m]), V(zp[m % 3]), W(h[:, m]), ALU.add), s_h1, KT)

                    def norm(r, gain):
                        dve.wait_ge(s_rt, 2 * c + r + 1)
                        own(dve.reciprocal(rs[:], rs[:]), s_rs, 2)
                        for k in range(KT):
                            own(dve.scalar_tensor_tensor(mx[:, k], h[:, k], gain[:, k:k + 1], rs[:], ALU.mult,
                                                         ALU.mult), s_a, 2 * KT)
                    norm(0, gm)
                    for m in range(FT):
                        dve.wait_ge(s_ut, FT * c + m + 1)
                        own(dve.tensor_tensor(ff[:, m], ff[:, m], ff[:, m], ALU.mult), s_f, FT)
                    for m in range(KT):
                        dve.wait_ge(s_wu, NU * c + KT + FT + 4 * (m + 1))
                        own(dve.tensor_tensor(W(h[:, m]), V(zp[m % 3]), W(h[:, m]), ALU.add), s_h2, KT)
                    norm(1, gp)
                    for m in range(KT):
                        dve.wait_ge(s_gs, KT * c + m + 1)
                        if m % 4 == 3:
                            dve.wait_ge(s_wu, NU * c + 2 * KT + 2 * FT + m // 4 + 1)
                        else:
                            dve.wait_ge(s_pj, 6 * c + 3 * (m // 4) + m % 4 + 1)
                        own(dve.tensor_tensor(W(ff[:, m]), V(zp[2]), W(ff[:, m]), ALU.mult), s_g, KT)
                        own(dve.tensor_tensor(h[:, m], h[:, m], ff[:, m], ALU.add), s_y, KT)


def build(nc, d):
    with ExitStack() as ctx:
        sb = lambda n, s, dt=F32: ctx.enter_context(nc.sbuf_tensor(n, s, dt))
        t = {n: sb(n, [128, 128]) for n in ("ident", "ones_d", "ones_w", "ones_hd")}
        t["eps"] = sb("eps", [128, 1])
        s_k = ctx.enter_context(nc.semaphore("matrices_loaded"))
        live = ctx.enter_context(nc.semaphore("waits_passed"))

        def plain(eng):
            eng.sem_inc(live, 1)
        t["plain"] = plain
        with nc.Block() as block:
            @block.sync
            def _(sp):
                for i, n in enumerate(("ident", "ones_d", "ones_w", "ones_hd")):
                    sp.dma_start(t[n][:], d["matrices"][i]).then_inc(s_k, 16)
                sp.wait_ge(s_k, 64)

            @block.gpsimd
            def _(pool):
                pool.memset(t["eps"][:], EPS)
        project(nc, d, t)
        with ExitStack() as held:
            keep = lambda n, s, dt=F32: t.__setitem__(n, held.enter_context(nc.sbuf_tensor(n + "_sb", s, dt)))
            keep("band", [128, NH, BANDW])
            keep("kcT", [128, NCP + NCS])
            keep("kcz", [128, 2, NCP])
            keep("vcp", [NCP, 128])
            keep("vcs", [128, 2 * NB, 128])
            setup(nc, d, t)
            compress(nc, d, t)
            with ExitStack() as inner:
                keep = lambda n, s, dt=F32: t.__setitem__(n, inner.enter_context(nc.sbuf_tensor(n + "_pr", s, dt)))
                for n in ("ks", "kw"):
                    keep(n, [128, 2, SEQ])
                for n in ("vs", "vw"):
                    keep(n, [128, SEQ // 128, 128])
                for n, shape in (("S", [128, 2, SEQ]), ("PT", [128, 3, 4, 128]), ("cband", [128, NH, 124]),
                                 ("score_band", [128, 64]), ("tri", [128, 128]), ("half", [128, 1]), ("att_gain", [128, 4]),
                                 ("q_tile", [128, 4, 128]), ("g_tile", [24, 128]), ("gates_tok", [128, 24]),
                                 ("mix_tile", [128, 4, 128]), ("nmax", [128, 2]), ("rsum", [128, 16]), ("cmax", [128, NH]),
                                 ("csum", [128, NH]), ("imp", [128, 2, 32]), ("top", [128, 2, 8]), ("mask", [128, 2, 32]),
                                 ("o_att", [128, 512]), ("o_tmp", [128, 512]), ("var", [128, 1]), ("rstd", [128, 1])):
                    keep(n, shape)
                prompt_keys(nc, d, t)
                for cl in range(4):
                    prompt(nc, d, t, cl)
            sample(nc, d, t)
        tail(nc, d, t)


def constants():
    p = np.arange(128)
    ident = np.eye(128, dtype=np.float32)
    blk = (p[:, None] // HD == p[None, :] // HD).astype(np.float32) / HD
    mats = np.stack([ident, np.full((128, 128), 1 / D), np.full((128, 128), 1 / 512), blk]).astype(np.float32)
    dist = 640 - np.arange(LINEW)
    n = np.maximum(dist, 1).astype(np.float32)
    large = 16 + (np.log(n / 16) / np.float32(np.log(8.0)) * 16).astype(np.int32)
    bucket = np.where(dist < 16, np.maximum(dist, 0), np.minimum(large, 31))
    onehot = (np.arange(32)[:, None] == bucket[None]).astype(np.float32)
    onehot[31] -= 1.0
    onehot[:, dist < 0] = 0
    rel = np.arange(BANDW) - 512
    cmask = np.where(rel[None] > p[:, None], NEG, 0).astype(np.float32)
    tri = np.where(p[None] > p[:, None], 0, NEG).astype(np.float32)
    r = np.arange(NB * NH)
    rel_blk, cur = np.arange(64)[None] - 30, (p >= 64).astype(int)[:, None]
    score = np.where(rel_blk > cur, NEG, np.where(rel_blk >= cur - 1, 1e4, 0)).astype(np.float32)
    return {"matrices": mats, "onehot": onehot, "cmask": cmask, "tri": tri, "score_band": score,
            "iota": np.broadcast_to(np.arange(128, dtype=np.float32), (NB * NH, 128)).copy(),
            "same_group": (r[:, None] // 4 == r[None] // 4).astype(np.float32),
            "same_token": ((r[:, None] // NH == r[None] // NH) / 512).astype(np.float32),
            "group_rows": np.stack([r % NH < 4, r % NH >= 4], axis=1).astype(np.float32)}


def lay_out(x):
    a = {k: np.asarray(v) for k, v in x.items()}
    A = np.ascontiguousarray
    feat = lambda v, n: v.reshape(-1, n * 128).T.reshape(n, 128, -1)
    tok = lambda p, s, n: A(np.concatenate([feat(p, n), feat(s, n)], axis=2))
    tiles = lambda w: w.reshape(w.shape[0] // 128, 128, -1, 128).transpose(2, 1, 0, 3)
    w = a["w_in"][0]
    o = 512
    cols = {k: np.arange(o + 128 * i, o + 128 * (i + 1)) for i, k in enumerate(("kc", "vc", "ks", "vs", "kw", "vw"))}
    for j in range(4):
        cols[f"q{j}"] = np.r_[HD * j:HD * (j + 1), HD * (4 + j):HD * (5 + j)]
        for i, k in enumerate(("cb", "cc", "ch")):
            s = 512 + 768 + 24 + 512 * i + 128 * j
            cols[f"{k}{j}"] = np.arange(s, s + 128)
    order = np.concatenate([cols[k] for k in ZT[:-1]])
    r = {"xT": tok(a["x_prompt"], a["x_sample"], 8), "pT": tok(a["p_prompt"], a["p_sample"], 2)}
    r["w_in"] = A(tiles(w[:, order]))
    r["w_gates"] = A(w[:, 1280:1304].reshape(8, 128, 24).transpose(1, 0, 2))
    vec = lambda v: A(v.reshape(-1, 128).T)
    r["norm_mix"], r["norm_mlp"], r["norm_ple"] = (vec(a[k]) for k in ("norm_mix", "norm_mlp", "norm_ple"))
    on = vec(a["out_norm"])
    r["att_gain"], r["conv_gain"] = A(on[:, 0:4]), A(on[:, 4:8])
    two = lambda v: np.concatenate([v, v])
    r["qk_gain"] = A(np.stack([two(a["q_norm"][0])] * 4 + [two(a["k_norm"][0, 1]), two(a["k_norm"][0, 2])], axis=1))
    r["conv_w"] = A(a["conv_w"][0].reshape(3, 4, 128).transpose(2, 1, 0))
    r["state_conv"] = A(a["state_conv"][0].reshape(NB, 2, 4, 128).transpose(3, 2, 1, 0))
    r["rel_bias"] = a["rel_bias"]
    r["cache_cmp"] = A(a["cache_cmp_kv"][0].transpose(0, 3, 4, 2, 1).reshape(-1, 128, 2, PAGE))
    r["page_table"] = A(a["page_table"].reshape(1, -1))
    r["w_cmp"] = A(a["w_cmp"][0].transpose(0, 2, 1, 3))
    r["cmp_pe"] = A(np.concatenate([a["cmp_pe"][0].transpose(2, 0, 1)] * 2))
    sel = a["cache_sel_kv"][0].reshape(-1, 64, 2, 2, HD)
    r["sel_k"], r["sel_v"] = A(sel[:, :, 0].transpose(0, 2, 3, 1)), A(sel[:, :, 1].transpose(0, 2, 1, 3))
    w = a["state_win_kv"][0].reshape(NB, 512, 2, 128)
    r["win_k"], r["win_v"] = A(w[:, :, 0].transpose(0, 2, 1)), A(w[:, :, 1])
    r["out_gain"] = A(a["out_norm"][0, :512].reshape(NH, HD))
    r["k_norm_cmp"] = A(two(a["k_norm"][0, 0])[:, None])
    up, down, out_, gate = tiles(a["w_up"][0]), tiles(a["w_down"][0]), tiles(a["w_out"][0]), tiles(a["w_ple_gate"][0])
    down = down.reshape(8, 128, 4, 8, 128).transpose(0, 2, 1, 3, 4).reshape(32, 128, 8, 128)
    proj = tiles(a["w_ple_proj"][0]).reshape(2, 4, 128, 2, 128).transpose(0, 2, 1, 3, 4).reshape(2, 128, 8, 128)
    r["w_tail"] = A(np.concatenate([out_, up, down, gate, proj]))
    return r


OUTS = {"yT": [8, 128, NTOK], "kvT": [6, 128, NTOK], "uT": [4, 128, NB + 2],
        "win_k_out": [NB, 128, 512], "win_v_out": [NB, 512, 128], "conv_prev": [128, 4, NB]}
SCRATCH = {"qT": [4, 128, NTOK], "mixT": [8, 128, NTOK], "gT": [24, NTOK], "line": [NH, LINEW],
           "skew": [128, NH * LINEW], "phys": [NB * NH, 7]}


def kernel(**inputs):
    import concourse.bacc as bacc
    from concourse.bass_utils import run_bass_kernel_spmd

    nc = bacc.Bacc("TRN2", target_bir_lowering=False, num_devices=1)
    arrays = {**lay_out(inputs), **constants()}
    d = {n: nc.dram_tensor("in_" + n, v.shape, mybir.dt.from_np(v.dtype), kind="ExternalInput").ap()
         for n, v in arrays.items()}
    for n, s in OUTS.items():
        d[n] = nc.dram_tensor("out_" + n, s, F32, kind="ExternalOutput").ap()
    for n, s in SCRATCH.items():
        d[n] = nc.dram_tensor("scratch_" + n, s, I32 if n == "phys" else F32, kind="Internal").ap()
    build(nc, d)
    r = run_bass_kernel_spmd(nc, [{"in_" + n: v for n, v in arrays.items()}], core_ids=[0]).results[0]
    g = {n: r["out_" + n] for n in OUTS}
    y = g["yT"].reshape(D, NTOK).T
    kv = g["kvT"].reshape(6, 128, NTOK).transpose(2, 0, 1).reshape(NTOK, 3, 2, 2, HD)
    uT = g["uT"].reshape(512, NB + 2).T
    p, s = kv[:SEQ], kv[SEQ:]
    wk, wv = g["win_k_out"].transpose(0, 2, 1).reshape(NB, 512, 2, HD), g["win_v_out"].reshape(NB, 512, 2, HD)
    wk = np.stack([wk, wv], axis=2)[None]
    prev = g["conv_prev"].transpose(2, 1, 0).reshape(NB, 512)
    sc = np.stack([prev, uT[2:]], axis=1)[None]
    return (y[None, :SEQ].copy(), y[SEQ:, None].copy(), p[None, None, :, 0].copy(), p[None, None, :, 1].copy(),
            p[None, None, -512:, 2].copy(), uT[None, None, 0:2].copy(), s[None, :, None, 0].copy(),
            s[None, :, None, 1].copy(), wk, sc)
```

```python
from contextlib import ExitStack

import numpy as np

import concourse.bass as bass
from concourse import mybir

ALU = mybir.AluOpType
ACT = mybir.ActivationFunctionType
F32 = mybir.dt.float32
I32 = mybir.dt.int32
U32 = mybir.dt.uint32
X = mybir.AxisListType.X
XY = mybir.AxisListType.XY

D = 1024
SEQ = 2048
NB = 8
NTOK = SEQ + NB
CH = NTOK // 4
HF = CH // 2
NEG = -1e30
EPS = 1e-6
HD = 64
NH = 8
KT = D // 128
FT = 4 * D // 128
PAST = 8192
PAGE = 128
NPAGE = PAST // PAGE
CB = 32
BANDW = 1024
LINEW = 1152
NCP = SEQ // CB
NCS = NB * PAST // CB
ZT = ["q0", "q1", "q2", "q3", "ks", "kw", "kc", "vc", "vs", "vw"] + \
     [f"{a}{j}" for j in range(4) for a in ("cc", "ch", "cb")] + ["g"]
NORMED = ZT[:6]
KVROW = {"kc": 0, "vc": 1, "ks": 2, "vs": 3, "kw": 4, "vw": 5}


class Own:

    def __init__(self, eng, start=0):
        self.eng, self.i, self.count, self.start = eng, 0, {}, start

    def iteration(self, i):
        self.close()
        self.i, self.count = i, {}

    def close(self):
        for name, (n, per) in self.count.items():
            assert n == per, (name, n, per)
        self.count = {}

    def __call__(self, ins, sem, per):
        n = self.count.get(sem.name, (0, per))[0] + 1
        self.count[sem.name] = (n, per)
        ins.then_inc(sem, 1)
        self.eng.wait_ge(sem, per * self.i + n + self.start)


ONE = 1


class semaphores:

    def __init__(self, nc, prefix):
        self.nc, self.prefix, self.taken = nc, prefix, []

    def __call__(self, name):
        self.taken.append(self.nc.alloc_semaphore(name=self.prefix + name))
        return self.taken[-1]

    def start_at_one(self):
        for s in self.taken:
            self.nc.sync.sem_inc(s, ONE)
        self.nc.all_engine_barrier()

    def __enter__(self):
        return self

    def __exit__(self, *_):
        self.nc.clear_and_free_semaphores(self.taken)
        self.nc.all_engine_barrier()


def ds(a, n):
    return bass.ds(a, n)


def setup(nc, d, t):
    with ExitStack() as ctx:
        sb = lambda n, s, dt=F32: ctx.enter_context(nc.sbuf_tensor(n, s, dt))
        sem = ctx.enter_context(semaphores(nc, "st_"))
        relb = sb("relb", [32, NH])
        oneh = sb("oneh", [32, LINEW])
        line = sb("line_sb", [NH, LINEW])
        cmask = sb("cmask", [128, BANDW])
        ps = ctx.enter_context(nc.psum_tensor("ps_line", [NH, 3, 512], F32))
        s_in, s_mm, s_line, s_ld, s_st, s_band, s_out = (sem(n) for n in (
            "inputs", "line_matmul", "line_copied", "consts", "line_stored", "band_loaded", "band_masked"))
        with nc.Block() as block:
            @block.sync
            def _(sp):
                sp.dma_start(relb[:], d["rel_bias"]).then_inc(s_in, 16)
                sp.dma_start(oneh[:], d["onehot"]).then_inc(s_in, 16)
                sp.dma_start(cmask[:], d["cmask"]).then_inc(s_ld, 16)
                sp.wait_ge(s_line, 3)
                sp.dma_start(d["line"], line[:]).then_inc(s_st, 16)
                sp.wait_ge(s_st, 16)
                every = bass.AP(tensor=d["line"].tensor, offset=0, ap=[[0, 128], [1, NH * LINEW]])
                sp.dma_start(d["skew"], every).then_inc(s_st, 16)
                sp.wait_ge(s_st, 32)
                src = bass.AP(tensor=d["skew"].tensor, offset=128,
                              ap=[[NH * LINEW - 1, 128], [LINEW, NH], [1, BANDW]])
                sp.dma_start(t["band"][:], src).then_inc(s_band, 16)

            @block.tensor
            def _(pe):
                pe.wait_ge(s_in, 32)
                for i, (a, n) in enumerate(((0, 512), (512, 512), (1024, 128))):
                    pe.matmul(ps[:, i, 0:n], relb[:], oneh[:, a:a + n], start=True, stop=True).then_inc(s_mm, 1)

            @block.vector
            def _(dve):
                for i, (a, n) in enumerate(((0, 512), (512, 512), (1024, 128))):
                    dve.wait_ge(s_mm, i + 1)
                    dve.tensor_copy(line[:, a:a + n], ps[:, i, 0:n]).then_inc(s_line, 1)
                dve.wait_ge(s_band, 16)
                dve.wait_ge(s_ld, 16)
                for h in range(NH):
                    dve.scalar_tensor_tensor(t["band"][:, h, :], t["band"][:, h, :], HD ** 0.5, cmask[:], ALU.mult,
                                             ALU.add).then_inc(s_out, 1)


def project(nc, d, t):
    with ExitStack() as ctx:
        sb = lambda n, s, dt=F32: ctx.enter_context(nc.sbuf_tensor(n, s, dt))
        pb = lambda n, s: ctx.enter_context(nc.psum_tensor(n, s, F32))
        sem = ctx.enter_context(semaphores(nc, "pj_"))
        win = sb("w_in_sb", [128, len(ZT) - 1, KT, 128])
        wg = sb("w_gates_sb", [128, KT, 24])
        xb = sb("x_chunk", [128, KT, CH])
        aT = sb("a_chunk", [128, KT, CH])
        sqx = sb("x_squares", [128, 2, CH])
        rs = sb("rstd_x", [128, CH])
        zs = sb("z_copy", [128, 2, CH])
        sqz = sb("z_square", [128, 2, CH])
        rn = sb("rstd_z", [128, 2, CH])
        ccs = sb("cc_copy", [128, CH])
        cv = sb("conv_sum", [128, CH])
        u = sb("u", [128, 4, CH + 2])
        y = sb("y_conv", [128, 4, CH])
        stg = sb("stage", [128, 5, CH])
        sst = sb("state_conv_sb", [128, 4, 2, NB])
        gn = sb("norm_mix_sb", [128, KT])
        gq = sb("qk_gain", [128, 6])
        gy = sb("conv_gain", [128, 4])
        cw = sb("conv_w_sb", [128, 4, 3])
        zp = [pb("ps_z0", [128, 2, 512]), pb("ps_z1", [128, 2, 512])]
        ssp = pb("ps_ssq", [128, 2, 512])
        nsp = pb("ps_nsq", [128, 2, 512])
        V = lambda ps: ps[:, :, 0:HF]
        W = lambda a: a.rearrange("p (h n) -> p h n", h=2)

        s_w, s_c, s_x, s_sq, s_sqf, s_ss, s_a, s_z, s_zt, s_nq, s_nd, s_nt, s_ysq, s_ys = (sem(n) for n in (
            "w_loaded", "consts_loaded", "x_loaded", "x_squared", "x_square_used", "x_summed", "a_ready", "z_done", "z_taken",
            "z_squared", "z_summed", "z_sum_taken", "y_squared", "y_summed"))
        s_st, s_gp, s_gs, s_chain, s_uo, s_rt = (sem(n) for n in (
            "staged", "gates_done", "gates_staged", "dve_steps", "u_out", "roots_taken"))
        s_u0, s_carry, s_fix = sem("u_cleared"), sem("u_carried"), sem("sample_conv")
        s_o = [sem(f"stage{i}_out") for i in range(5)]
        sends = [("q", j) for j in range(4)] + [("kv", KVROW[k]) for k in ("ks", "kw", "kc", "vc", "vs", "vw")] + \
                [("g", 0)] + [("mix", 4 + j) for j in range(4)]
        NS = len(sends)
        sem.start_at_one()

        with nc.Block() as block:
            @block.sync
            def _(sp):
                def load_x(c):
                    sp.dma_start(xb[:], d["xT"][:, :, ds(c * CH, CH)].rearrange("k p n -> p k n")).then_inc(s_x, 16)

                load_x(0)
                for a, b in ((gn, "norm_mix"), (gq, "qk_gain"), (gy, "conv_gain"), (cw, "conv_w"), (sst, "state_conv")):
                    sp.dma_start(a[:], d[b]).then_inc(s_c, 16)
                for m in range(len(ZT) - 1):
                    sp.dma_start(win[:, m], d["w_in"][m]).then_inc(s_w, 16)
                sp.dma_start(wg[:], d["w_gates"]).then_inc(s_w, 16)

                def body(c, last):
                    for n, (what, row) in enumerate(sends):
                        sl = n % 5
                        if n == 10 and not last:
                            sp.wait_ge(s_a, ONE + KT * (c + 1))
                            load_x(c + 1)
                        if what == "g":
                            sp.wait_ge(s_gs, ONE + c + 1)
                        else:
                            sp.wait_ge(s_st, ONE + (NS - 1) * c + n + (n < 10))
                        dst = d["gT"][:, ds(c * CH, CH)] if what == "g" else \
                            d[{"q": "qT", "kv": "kvT", "mix": "mixT"}[what]][row, :, ds(c * CH, CH)]
                        src = stg[0:24, sl, :] if what == "g" else stg[:, sl, :]
                        sp.dma_start(dst, src).then_inc(s_o[sl], 16)
                with sp.Fori(0, 3) as c:
                    body(c, False)
                body(3, True)
                sp.dma_start(d["uT"].rearrange("j p n -> p j n"), u[:, :, CH - NB:CH + 2]).then_inc(s_uo, 16)
                sp.wait_ge(s_uo, ONE + 16)
                for sl in range(5):
                    sp.wait_ge(s_o[sl], ONE + 16 * 4 * NS // 5)

            @block.scalar
            def _(act):
                with act.Fori(0, 4) as c:
                    act.wait_ge(s_x, ONE + 16 * c + 16)
                    for k in range(KT):
                        if k >= 2:
                            act.wait_ge(s_sqf, ONE + KT * c + k - 1)
                        act.activation(sqx[:, k % 2], xb[:, k], ACT.Square).then_inc(s_sq, 1)
                    act.wait_ge(s_sqf, ONE + KT * (c + 1))
                    act.activation(W(rs[:]), V(ssp), ACT.Sqrt, bias=t["eps"][:]).then_inc(s_rt, 1)
                    for n in range(6):
                        act.wait_ge(s_nd, ONE + 6 * c + n + 1)
                        act.activation(W(rn[:, n % 2]), V(nsp), ACT.Sqrt, bias=t["eps"][:]).then_inc(s_nt, 1)
                    act.wait_ge(s_gp, ONE + c + 1)
                    act.wait_ge(s_o[0], ONE + 16 * 3 * c + 32)
                    act.activation(W(stg[0:24, 0, :]), V(zp[0])[0:24], ACT.Sigmoid).then_inc(s_gs, 1)
                    act.wait_ge(s_ys, ONE + c + 1)
                    act.activation(W(rn[:, 0]), V(nsp), ACT.Sqrt, bias=t["eps"][:]).then_inc(s_rt, 1)

            @block.tensor
            def _(pe):
                with pe.Fori(0, 4) as c:
                    for k in range(KT):
                        pe.wait_ge(s_sq, ONE + KT * c + k + 1)
                        for h in range(2):
                            mm = pe.matmul(ssp[:, h, 0:HF], t["ones_d"][:], sqx[:, k % 2, h * HF:(h + 1) * HF],
                                           start=(k == 0), stop=(k == KT - 1))
                        mm.then_inc(s_sqf, 1)

                    def norm(n):
                        pe.wait_ge(s_nq, ONE + 6 * c + n + 1)
                        if n:
                            pe.wait_ge(s_nt, ONE + 6 * c + n)
                        for h in range(2):
                            mm = pe.matmul(nsp[:, h, 0:HF], t["ones_hd"][:], sqz[:, n % 2, h * HF:(h + 1) * HF],
                                           start=True, stop=True)
                        mm.then_inc(s_nd, 1)
                    for m, name in enumerate(ZT):
                        if m == 0:
                            pe.wait_ge(s_a, ONE + KT * (c + 1))
                            pe.wait_ge(s_w, ONE + 16 * len(ZT))
                        if m >= 2:
                            pe.wait_ge(s_zt, ONE + (len(ZT) - 1) * c + m - 1)
                        for h in range(2):
                            for k in range(KT):
                                o = zp[m % 2][0:24, h, 0:HF] if name == "g" else zp[m % 2][:, h, 0:HF]
                                mm = pe.matmul(o, wg[:, k] if name == "g" else win[:, m, k],
                                               aT[:, k, h * HF:(h + 1) * HF], start=(k == 0), stop=(k == KT - 1))
                        mm.then_inc(s_gp if name == "g" else s_z, 1)
                        if 1 <= m <= 6:
                            norm(m - 1)
                    for j in range(4):
                        pe.wait_ge(s_ysq, ONE + 4 * c + j + 1)
                        for h in range(2):
                            mm = pe.matmul(nsp[:, h, 0:HF], t["ones_w"][:], aT[:, j, h * HF:(h + 1) * HF],
                                           start=(j == 0), stop=(j == 3))
                    mm.then_inc(s_ys, 1)

            @block.vector
            def _(dve):
                own = Own(dve, ONE)
                NZ = len(ZT) - 1
                link = lambda ins: own(ins, s_chain, 1 + 6 + 4 * 3 + 1)
                dve.wait_ge(s_c, ONE + 16 * 5)
                dve.memset(u[:, :, 0:2], 0.0).then_inc(s_u0, 1)
                dve.wait_ge(s_u0, ONE + 1)

                def body(c, last):
                    sent = [0]

                    def slot():
                        n = sent[0]
                        sent[0] += 1
                        dve.wait_ge(s_o[n % 5], ONE + 48 * c + 16 * (n // 5))
                        return stg[:, n % 5, :]

                    def staged(ins):
                        own(ins, s_st, NS - 1)

                    dve.wait_ge(s_rt, ONE + 2 * c + 1)
                    link(dve.reciprocal(rs[:], rs[:]))
                    for k in range(KT):
                        own(dve.scalar_tensor_tensor(aT[:, k], xb[:, k], gn[:, k:k + 1], rs[:], ALU.mult,
                                                     ALU.mult), s_a, KT)

                    def finish(n):
                        dve.wait_ge(s_nt, ONE + 6 * c + n + 1)
                        link(dve.reciprocal(rn[:, n % 2], rn[:, n % 2]))
                        staged(dve.scalar_tensor_tensor(slot(), zs[:, n % 2], gq[:, n:n + 1], rn[:, n % 2],
                                                        ALU.mult, ALU.mult))

                    for m, name in enumerate(ZT[:-1]):
                        dve.wait_ge(s_z, ONE + (len(ZT) - 1) * c + m + 1)
                        z = V(zp[m % 2])
                        if name in NORMED:
                            own(dve.tensor_copy(W(zs[:, m % 2]), z), s_zt, NZ)
                            own(dve.tensor_tensor(sqz[:, m % 2], zs[:, m % 2], zs[:, m % 2], ALU.mult), s_nq, 6)
                            if m:
                                finish(m - 1)
                        elif name in KVROW:
                            if m == 6:
                                finish(5)
                            o = slot()
                            own(dve.tensor_copy(W(o), z), s_zt, NZ)
                            staged(dve.nop())
                        elif name[:2] == "cc":
                            own(dve.tensor_copy(W(ccs[:]), z), s_zt, NZ)
                        elif name[:2] == "ch":
                            j = int(name[2])
                            own(dve.tensor_tensor(W(u[:, j, 2:CH + 2]), z, W(ccs[:]), ALU.mult), s_zt, NZ)
                            link(dve.tensor_scalar(cv[:], u[:, j, 2:CH + 2], cw[:, j, 2:3], None, ALU.mult))
                            link(dve.scalar_tensor_tensor(cv[:], u[:, j, 1:CH + 1], cw[:, j, 1:2], cv[:], ALU.mult, ALU.add))
                            link(dve.scalar_tensor_tensor(cv[:], u[:, j, 0:CH], cw[:, j, 0:1], cv[:], ALU.mult, ALU.add))
                            if last:
                                sc = cv[:, CH - NB:CH]
                                for i, past in enumerate((u[:, j, CH + 2 - NB:CH + 2], sst[:, j, 1], sst[:, j, 0])):
                                    wi = cw[:, j, 2 - i:3 - i]
                                    ins = dve.scalar_tensor_tensor(sc, past, wi, sc, ALU.mult, ALU.add) if i else \
                                        dve.tensor_scalar(sc, past, wi, None, ALU.mult)
                                    ins.then_inc(s_fix, 1)
                                    dve.wait_ge(s_fix, ONE + 3 * j + i + 1)
                            else:
                                own(dve.tensor_copy(u[:, j, 0:2], u[:, j, CH:CH + 2]), s_carry, 4)
                        else:
                            j = int(name[2])
                            own(dve.tensor_tensor(W(y[:, j]), z, W(cv[:]), ALU.mult), s_zt, NZ)
                    sent[0] += 1
                    dve.wait_ge(s_zt, ONE + (len(ZT) - 1) * (c + 1))
                    dve.wait_ge(s_gp, ONE + c + 1)
                    for j in range(4):
                        own(dve.tensor_tensor(aT[:, j], y[:, j], y[:, j], ALU.mult), s_ysq, 4)
                    dve.wait_ge(s_rt, ONE + 2 * c + 2)
                    link(dve.reciprocal(rn[:, 0], rn[:, 0]))
                    for j in range(4):
                        staged(dve.scalar_tensor_tensor(slot(), y[:, j], gy[:, j:j + 1], rn[:, 0], ALU.mult, ALU.mult))

                with dve.Fori(0, 3) as c:
                    own.iteration(c)
                    body(c, False)
                own.iteration(3)
                body(3, True)
                own.close()


def compress(nc, d, t):
    NPG = 32
    plain = t["plain"]
    with ExitStack() as ctx:
        sb = lambda n, s, dt=F32: ctx.enter_context(nc.sbuf_tensor(n, s, dt))
        pb = lambda n, s: ctx.enter_context(nc.psum_tensor(n, s, F32))
        sem = ctx.enter_context(semaphores(nc, "cp_"))
        wc = sb("w_cmp_sb", [128, 2, CB, 128])
        pe_t = sb("cmp_pe_sb", [128, 2, CB])
        cvec = sb("pe_compressed", [128, 2])
        gk = sb("k_norm_cmp", [128, 1])
        pg = [sb(f"pages{b}", [128, NPG, 2, PAGE]) for b in range(2)]
        ptab = sb("page_table_sb", [1, NB * NPAGE], I32)
        kcT, vcT = t["kcT"], sb("vcT", [128, NCP + NCS])
        cps = [pb(f"ps_cmp{b}", [128, 512]) for b in range(2)]
        sps = pb("ps_cmp_sum", [128, 512])
        tps = pb("ps_cmp_tr", [128, 4, 128])
        sq = pg[0][:, 0:2, :, :].rearrange("p a b c -> p (a b c)")
        rt = pg[0][:, 2:4, :, :].rearrange("p a b c -> p (a b c)")
        s_z, s_w, s_c, s_cv, s_cvd, s_pr, s_sq, s_sum, s_rt, s_rc, s_kn, s_tr, s_te = (sem(n) for n in (
            "weights_cleared", "weights_loaded", "consts_loaded", "pe_summed", "pe_copied",
            "prompt_loaded", "squared", "squares_summed", "root", "reciprocal", "k_normed", "v_transposed", "v_copied"))
        s_k0 = sem("k_copied")
        s_pg, s_done, s_ev = ([sem(f"{n}{b}") for b in range(2)] for n in ("pages", "chunk_summed", "chunk_copied"))
        sem.start_at_one()
        NCH = NB * NPAGE // NPG
        pieces = [(512 * i, 512) for i in range(4)] + [(2048, 64)]

        def load_pages(eng, b, idx_base):
            with eng.Fori(0, NPG // 4) as j4:
                pages = [eng.value_load(ptab[0:1, ds(idx_base + (j4 * 4 + jj), 1)], min_val=0, max_val=d["cache_cmp"].shape[0] - 1) for jj in range(4)]
                for jj in range(4):
                    eng.dma_start(pg[b][:, ds(j4 * 4 + jj, 1)].rearrange("p a k n -> p (a k) n"),
                              d["cache_cmp"][ds(pages[jj], 1)].rearrange("a p k n -> (a p) k n")).then_inc(s_pg[b], 16)

        with nc.Block() as block:
            @block.gpsimd
            def _(pool):
                own = Own(pool, ONE)
                for kv in range(2):
                    own(pool.memset(wc[:, kv], 0.0), s_z, 2)

            @block.sync
            def _(sp):
                for a, b in ((pe_t, "cmp_pe"), (gk, "k_norm_cmp"), (ptab, "page_table")):
                    sp.dma_start(a[:], d[b]).then_inc(s_c, 16)
                sp.wait_ge(s_z, ONE + 2)
                for g in range(2):
                    for kv in range(2):
                        sp.dma_start(wc[64 * g:64 * g + 64, kv, :, 64 * g:64 * g + 64], d["w_cmp"][kv]).then_inc(s_w, 16)
                sp.wait_ge(s_c, ONE + 48)
                with sp.Fori(0, NCH // 2) as i:
                    sp.wait_ge(s_done[0], ONE + i)
                    plain(sp)
                    load_pages(sp, 0, i * (2 * NPG))
                sp.wait_ge(s_done[0], ONE + NCH // 2)
                for kv in range(2):
                    sp.dma_start(pg[0][:, 0:SEQ // PAGE, kv, :],
                                 d["kvT"][kv, :, 0:SEQ].rearrange("p (a n) -> p a n", n=PAGE)).then_inc(s_pr, 16)

            @block.scalar
            def _(act):
                act.wait_ge(s_c, ONE + 48)
                with act.Fori(0, NCH // 2) as i:
                    act.wait_ge(s_done[1], ONE + i)
                    plain(act)
                    load_pages(act, 1, i * (2 * NPG) + NPG)
                for i, (a, n) in enumerate(pieces):
                    if i:
                        act.wait_ge(s_kn, ONE + i)
                    else:
                        act.wait_ge(s_ev[0], ONE + NCH // 2 + 1)
                        act.wait_ge(s_ev[1], ONE + NCH // 2)
                    act.activation(sq[:, 0:n], kcT[:, a:a + n], ACT.Square).then_inc(s_sq, 1)
                    act.wait_ge(s_sum, ONE + i + 1)
                    act.activation(rt[:, 0:n], sps[:, 0:n], ACT.Sqrt, bias=t["eps"][:]).then_inc(s_rt, 1)

            @block.tensor
            def _(pe):
                pe.wait_ge(s_w, ONE + 64)
                pe.wait_ge(s_c, ONE + 48)
                for kv in range(2):
                    for l in range(CB):
                        mm = pe.matmul(sps[:, kv:kv + 1], wc[:, kv, l], pe_t[:, kv, l:l + 1], start=(l == 0), stop=(l == CB - 1))
                mm.then_inc(s_cv, 1)

                def chunk(b, np_):
                    for kv in range(2):
                        for l in range(CB):
                            mm = pe.matmul(cps[b][:, 128 * kv:128 * kv + 4 * np_], wc[:, kv, l],
                                           pg[b][:, 0:np_, kv, l::CB], start=(l == 0), stop=(l == CB - 1))
                    mm.then_inc(s_done[b], 1)
                with pe.Fori(0, NCH // 2) as i:
                    for b in range(2):
                        pe.wait_ge(s_pg[b], ONE + 16 * NPG * (i + 1))
                        pe.wait_ge(s_ev[b], ONE + i)
                        chunk(b, NPG)
                pe.wait_ge(s_pr, ONE + 32)
                pe.wait_ge(s_ev[0], ONE + NCH // 2)
                chunk(0, SEQ // PAGE)
                for i, (a, n) in enumerate(pieces):
                    pe.wait_ge(s_sq, ONE + i + 1)
                    if i:
                        pe.wait_ge(s_rt, ONE + i)
                    else:
                        pe.wait_ge(s_cvd, ONE + 1)
                    pe.matmul(sps[:, 0:n], t["ones_hd"][:], sq[:, 0:n], start=True, stop=True).then_inc(s_sum, 1)
                for q in range(5):
                    if q:
                        pe.wait_ge(s_te, ONE + q)
                    if q < 4:
                        for j in range(4):
                            a = NCP + 512 * q + 128 * j
                            mm = pe.transpose(tps[:, j], vcT[:, a:a + 128], t["ident"][:])
                    else:
                        mm = pe.transpose(tps[0:NCP, 0], vcT[:, 0:NCP], t["ident"][:])
                    mm.then_inc(s_tr, 1)

            @block.vector
            def _(dve):
                dve.wait_ge(s_cv, ONE + 1)
                dve.tensor_copy(cvec[:], sps[:, 0:2]).then_inc(s_cvd, 1)
                dve.wait_ge(s_cvd, ONE + 1)

                def copy(b, a, n):
                    dve.tensor_scalar(kcT[:, a], cps[b][:, 0:n], cvec[:, 0:1], None, ALU.add).then_inc(s_k0, 1)
                    dve.tensor_scalar(vcT[:, a], cps[b][:, 128:128 + n], cvec[:, 1:2], None, ALU.add).then_inc(s_ev[b], 1)
                with dve.Fori(0, NCH // 2) as i:
                    for b in range(2):
                        dve.wait_ge(s_done[b], ONE + i + 1)
                        copy(b, ds(i * 256 + (NCP + 128 * b), 128), 128)
                dve.wait_ge(s_done[0], ONE + NCH // 2 + 1)
                copy(0, slice(0, NCP), NCP)
                dve.wait_ge(s_k0, ONE + NCH + 1)
                for i, (a, n) in enumerate(pieces):
                    dve.wait_ge(s_rt, ONE + i + 1)
                    dve.reciprocal(rt[:, 0:n], rt[:, 0:n]).then_inc(s_rc, 1)
                    dve.wait_ge(s_rc, ONE + i + 1)
                    dve.scalar_tensor_tensor(kcT[:, a:a + n], kcT[:, a:a + n], gk[:, 0:1], rt[:, 0:n], ALU.mult,
                                             ALU.mult).then_inc(s_kn, 1)
                    dve.wait_ge(s_kn, ONE + i + 1)
                for g in range(2):
                    r = slice(64 * g, 64 * g + 64)
                    o = slice(64 - 64 * g, 128 - 64 * g)
                    dve.tensor_copy(t["kcz"][r, g], kcT[r, 0:NCP])
                    dve.memset(t["kcz"][o, g], 0.0)
                for q in range(5):
                    dve.wait_ge(s_tr, ONE + q + 1)
                    if q < 4:
                        dve.tensor_copy(t["vcs"][:, 4 * q:4 * q + 4], tps[:]).then_inc(s_te, 1)
                    else:
                        dve.tensor_copy(t["vcp"][:], tps[0:NCP, 0]).then_inc(s_te, 1)


def prompt_keys(nc, d, t):
    with ExitStack() as ctx:
        sem = ctx.enter_context(semaphores(nc, "pk_"))
        vT = t["S"]
        ps = [ctx.enter_context(nc.psum_tensor(f"ps_vt{b}", [128, 4, 128], F32)) for b in range(2)]
        s_wb = sem("window_band")
        s_v, s_k, s_t, s_e, s_m = (sem(n) for n in ("v_loaded", "k_loaded", "v_transposed", "v_copied", "cleared"))
        with nc.Block() as block:
            @block.sync
            def _(sp):
                for i, n in enumerate(("vs", "vw")):
                    sp.dma_start(vT[:, i], d["kvT"][KVROW[n], :, 0:SEQ]).then_inc(s_v, 16)
                for n in ("ks", "kw"):
                    for g in range(2):
                        r = slice(64 * g, 64 * g + 64)
                        sp.dma_start(t[n][r, g], d["kvT"][KVROW[n], r, 0:SEQ]).then_inc(s_k, 16)
                for n in ("tri", "score_band", "att_gain"):
                    sp.dma_start(t[n][:], d[n]).then_inc(s_k, 16)
                sp.wait_ge(s_k, 16 * 7)

            @block.gpsimd
            def _(pool):
                own = Own(pool)
                for n in ("ks", "kw"):
                    for g in range(2):
                        own(pool.memset(t[n][64 - 64 * g:128 - 64 * g, g], 0.0), s_m, 5)
                own(pool.memset(t["half"][:], -0.5), s_m, 5)

            @block.tensor
            def _(pe):
                pe.wait_ge(s_v, 32)
                for q in range(8):
                    if q >= 2:
                        pe.wait_ge(s_e, q - 1)
                    for j in range(4):
                        k = 4 * (q % 4) + j
                        mm = pe.transpose(ps[q % 2][:, j], vT[:, q // 4, 128 * k:128 * k + 128], t["ident"][:])
                    mm.then_inc(s_t, 1)

            @block.vector
            def _(dve):
                dve.memset(t["cband"][:, :, 0:56], 0.0)
                dve.memset(t["cband"][:, :, 64:124], NEG)
                dve.wait_ge(s_k, 16 * 7)
                for h in range(NH):
                    dve.tensor_copy(t["wband"][:, h], t["band"][:, h, 0:640]).then_inc(s_wb, 1)
                    dve.wait_ge(s_wb, 2 * h + 1)
                    dve.tensor_tensor(t["wband"][:, h, 0:128], t["wband"][:, h, 0:128], t["tri"][:], ALU.add).then_inc(s_wb, 1)
                    dve.wait_ge(s_wb, 2 * h + 2)
                dve.tensor_copy(t["cband"][:, :, 56:64], t["band"][:, :, 415:415 + 32 * 7 + 1:32])
                for q in range(8):
                    dve.wait_ge(s_t, q + 1)
                    dst = t["vs" if q < 4 else "vw"]
                    dve.tensor_copy(dst[:, 4 * (q % 4):4 * (q % 4) + 4], ps[q % 2][:]).then_inc(s_e, 1)


def prompt(nc, d, t, cl):
    nk = cl + 1
    SC = HD ** -0.5
    items = [("cmp", 0)] + [("win", h) for h in range(NH)] + [("sel", h) for h in range(NH)]
    win_chunks = [(0, 512)] if cl == 0 else [(0, 512), (512, 128)]
    far = 512 * cl - 128
    sel_chunks = ([(a, min(512, far - a)) for a in range(0, far, 512)] + [(far, 128)] if cl else []) + [(512 * cl, 512)]

    def chunks(item):
        return {"cmp": [(0, 512)], "win": win_chunks, "sel": sel_chunks}[item[0]]

    def groups(item):
        return {"cmp": [4, 4], "win": [4] if cl == 0 else [4, 1], "sel": [4] * nk}[item[0]]
    NCK = sum(len(chunks(i)) for i in items)
    NG = sum(len(groups(i)) for i in items)
    first_group = [sum(len(groups(i)) for i in items[:j]) for j in range(len(items) + 1)]
    first_chunk = [sum(len(chunks(i)) for i in items[:j]) for j in range(len(items) + 1)]
    NI = len(items)
    BR = {"cmp": 0, "sel": 1, "win": 2}
    plain = t["plain"]
    bc = lambda a, n: a.rearrange("p (h o) -> p h o", o=1).to_broadcast([128, a.shape[1], n])

    with ExitStack() as ctx:
        pb = lambda n, s: ctx.enter_context(nc.psum_tensor(n, s, F32))
        sem = ctx.enter_context(semaphores(nc, f"pr{cl}_"))
        sp_ = [pb(f"ps_s{i}_{cl}", [128, 512]) for i in range(3)]
        tp_ = [pb(f"ps_p{i}_{cl}", [128, 4, 128]) for i in range(2)]
        O = [pb(f"ps_o{i}_{cl}", [128, NH, HD]) for i in range(3)]
        S, PT, q_, g_, gn = t["S"], t["PT"], t["q_tile"], t["g_tile"], t["gates_tok"]
        s_in, s_qk, s_ev, s_mx, s_exp, s_tp, s_pte, s_pv, s_gt, s_ge, s_comb, s_on, s_mo, s_cx, s_cp, s_dv, s_pw, s_ss, s_vr = \
            (sem(n) for n in (
                "tile_loaded", "scores_done", "scores_copied", "max_ready", "probs_ready", "probs_transposed",
                "transposed_copied", "values_done", "gates_transposed", "gates_copied", "outputs_read", "mix_normed", "mix_sent",
                "cmp_exp_done", "cmp_probs_ready", "dve_steps", "rstd_ready", "squares_summed", "variance_ready"))
        s_cs, s_mb, s_mk, s_cf = sem("cmp_shifted"), sem("bias_mixed"), sem("mask_ready"), sem("coefficients_ready")
        sem.start_at_one()
        MIXED = [j for j, it in enumerate(items) if it[0] == "sel" or (it[0] == "win" and cl == 0)]

        with nc.Block() as block:
            @block.sync
            def _(sp):
                with sp.Fori(0, 4) as i:
                    col = i * 128 + 512 * cl
                    sp.wait_ge(s_qk, ONE + NCK * i)
                    plain(sp)
                    sp.wait_ge(s_gt, ONE + i)
                    plain(sp)
                    sp.dma_start(q_[:], d["qT"][:, :, ds(col, 128)].rearrange("r p n -> p r n")).then_inc(s_in, 16)
                    sp.dma_start(g_[:], d["gT"][:, ds(col, 128)]).then_inc(s_in, 16)
                    sp.wait_ge(s_pte, ONE + (NG + 1) * (i + 1))
                    plain(sp)
                    sp.dma_start(d["mixT"][0:4, :, ds(col, 128)].rearrange("r p n -> p r n"), t["mix_tile"][:]).then_inc(s_mo, 16)
                sp.wait_ge(s_mo, ONE + 64)

            @block.tensor
            def _(pe):
                with pe.Fori(0, 4) as i:
                    def scores(j):
                        kind, h = items[j]
                        g, r = h // 4, h % 4
                        for ci, (a, n) in enumerate(chunks(items[j])):
                            k = first_chunk[j] + ci
                            pe.wait_ge(s_ev, ONE + NCK * i + max(k - 2, 0))
                            if kind == "cmp":
                                for hh in range(NH):
                                    mm = pe.matmul(sp_[k % 3][:, 64 * hh:64 * hh + 64], q_[:, hh % 4], t["kcz"][:, hh // 4],
                                                   start=True, stop=True)
                            elif kind == "win" and cl:
                                keys = t["kw"][:, g, ds(i * 128 + (512 * cl - 512 + a), n)]
                                mm = pe.matmul(sp_[k % 3][:, 0:n], q_[:, r], keys, start=True, stop=True)
                            else:
                                keys = t["ks" if kind == "sel" else "kw"][:, g, a:a + n]
                                mm = pe.matmul(sp_[k % 3][:, 0:n], q_[:, r], keys, start=True, stop=True)
                            mm.then_inc(s_qk, 1)

                    def turn(q):
                        j = max(x for x in range(NI) if first_group[x] <= q)
                        kind, h = items[j]
                        gi = q - first_group[j]
                        if gi == 0:
                            if kind == "cmp":
                                pe.wait_ge(s_cp, ONE + i + 1)
                            else:
                                pe.wait_ge(s_exp, ONE + (NI - 1) * i + j)
                        free_bank(q)
                        plain(pe)
                        for y in range(groups(items[j])[gi]):
                            if kind == "cmp":
                                mm = pe.transpose(tp_[q % 2][0:64, y], S[:, j % 3, 256 * gi + 64 * y:256 * gi + 64 * y + 64],
                                                  t["ident"][:])
                            else:
                                a = 512 * gi + 128 * y
                                mm = pe.transpose(tp_[q % 2][:, y], S[:, j % 3, a:a + 128], t["ident"][:])
                        mm.then_inc(s_tp, 1)

                    def free_bank(q):
                        if q == 0:
                            pe.wait_ge(s_ge, ONE + i + 1)
                        else:
                            pe.wait_ge(s_pte, ONE + (NG + 1) * i + max(q - 1, 0))

                    def values(q):
                        j = max(x for x in range(NI) if first_group[x] <= q)
                        kind, h = items[j]
                        gi, g, n = q - first_group[j], h // 4, len(groups(items[j]))
                        pe.wait_ge(s_pte, ONE + (NG + 1) * i + q + 1)
                        if q == 0:
                            pe.wait_ge(s_comb, ONE + i)
                        for y in range(groups(items[j])[gi]):
                            if kind == "cmp":
                                hh = 4 * gi + y
                                mm = pe.matmul(O[0][:, hh], PT[0:64, q % 3, y], t["vcp"][:, 64 * gi:64 * gi + 64],
                                               start=True, stop=True)
                                continue
                            if kind == "win" and cl:
                                v = t["vw"][:, ds(i + (4 * cl - 4 + 4 * gi + y), 1), 64 * g:64 * g + 64].rearrange("p a n -> p (a n)")
                            else:
                                v = t["vs" if kind == "sel" else "vw"][:, 4 * gi + y, 64 * g:64 * g + 64]
                            mm = pe.matmul(O[BR[kind]][:, h], PT[:, q % 3, y], v, start=(gi == 0 and y == 0),
                                           stop=(gi == n - 1 and y == groups(items[j])[gi] - 1))
                        mm.then_inc(s_pv, 1)

                    pe.wait_ge(s_in, ONE + 32 * (i + 1))
                    pe.wait_ge(s_pte, ONE + (NG + 1) * i)
                    plain(pe)
                    pe.transpose(tp_[0][:, 0, 0:24], g_[:], t["ident"][0:24, 0:24]).then_inc(s_gt, 1)
                    scores(0)
                    scores(1)
                    for j in range(NI):
                        if j + 2 < NI:
                            scores(j + 2)
                        for q in range(first_group[j], first_group[j + 1]):
                            turn(q)
                            if q:
                                values(q - 1)
                    values(NG - 1)
                    pe.wait_ge(s_on, ONE + i + 1)
                    free_bank(NG)
                    for y in range(4):
                        mm = pe.transpose(tp_[NG % 2][:, y], t["o_att"][:, 128 * y:128 * y + 128], t["ident"][:])
                    mm.then_inc(s_tp, 1)

            @block.scalar
            def _(act):
                with act.Fori(0, 4) as i:
                    act.wait_ge(s_gt, ONE + i + 1)
                    act.wait_ge(s_cf, ONE + i)
                    act.activation(gn[:], tp_[0][:, 0, 0:24], ACT.Copy).then_inc(s_ge, 1)
                    act.wait_ge(s_cs, ONE + i + 1)
                    act.activation(S[:, 0, 0:512], S[:, 0, 0:512], ACT.Exp, scale=SC).then_inc(s_cx, 1)

                    def exp(j):
                        n = sum(c[1] for c in chunks(items[j]))
                        act.wait_ge(s_mx, ONE + (NI - 1) * i + j)
                        act.activation(S[:, j % 3, 0:n], S[:, j % 3, 0:n], ACT.Exp, bias=t["nmax"][:, j % 3:j % 3 + 1],
                                       accum_out=t["rsum"][:, j - 1:j]).then_inc(s_exp, 1)

                    def copy(q, n, rows):
                        act.wait_ge(s_tp, ONE + (NG + 1) * i + q + 1)
                        act.wait_ge(s_pv, ONE + NG * i + max(q - 2, 0))
                        act.activation(PT[0:rows, q % 3, 0:n], tp_[q % 2][0:rows, 0:n], ACT.Copy).then_inc(s_pte, 1)
                    for j in range(NI):
                        if j + 1 < NI:
                            exp(j + 1)
                        for gi, n in enumerate(groups(items[j])):
                            copy(first_group[j] + gi, n, 64 if j == 0 else 128)
                    act.wait_ge(s_tp, ONE + (NG + 1) * (i + 1))
                    act.wait_ge(s_mo, ONE + 16 * i)
                    for y in range(4):
                        ins = act.activation(t["mix_tile"][:, y], tp_[NG % 2][:, y], ACT.Copy, scale=t["att_gain"][:, y:y + 1])
                    ins.then_inc(s_pte, 1)

            @block.gpsimd
            def _(pool):
                own = Own(pool, ONE)
                with pool.Fori(0, 4) as i:
                    own.iteration(i)
                    for m, j in enumerate(MIXED):
                        kind, h = items[j]
                        pool.wait_ge(s_ev, ONE + NCK * i + (first_chunk[MIXED[m - 3] + 1] if m >= 3 else 0))
                        plain(pool)
                        if kind == "win":
                            own(pool.tensor_copy(t["mix_bias"][:, m % 3, 128:640], t["band"][:, h, ds(i * -128 + 512, 512)]),
                                s_mb, len(MIXED))
                            continue
                        pool.wait_ge(s_mk, ONE + i + 1)
                        plain(pool)
                        lo = 128 if cl == 0 else 0
                        blocks = lambda z: z.rearrange("p (b k) -> p b k", k=64)
                        own(pool.tensor_tensor(blocks(t["mix_bias"][:, m % 3, lo:640]),
                                               blocks(t["band"][:, h, ds(i * -128 + (384 + lo), 640 - lo)]),
                                               bc(t["mask"][:, h // 4, 8 * cl - 2 + lo // 64:8 * cl + 8], 64), ALU.add),
                            s_mb, len(MIXED))
                    pool.wait_ge(s_vr, ONE + i + 1)
                    own(pool.tensor_tensor(t["rstd"][:], t["var"][:], t["half"][:], ALU.pow), s_pw, 1)
                own.close()

            @block.vector
            def _(dve):
                own = Own(dve, ONE)
                step = lambda ins: own(ins, s_dv, 21)
                with dve.Fori(0, 4) as i:
                    own.iteration(i)
                    dve.wait_ge(s_qk, ONE + NCK * i + 1)
                    dve.wait_ge(s_tp, ONE + (NG + 1) * i)
                    p = S[:, 0, 0:512].rearrange("p (h n) -> p h n", n=64)
                    cb = t["cband"][:, :, ds(i * -4 + (60 - 16 * cl), 64)]
                    own(dve.tensor_tensor(p, sp_[0][:].rearrange("p (h n) -> p h n", n=64), cb, ALU.add), s_ev, NCK)
                    m8, r8 = t["cmax"], t["csum"]
                    step(dve.tensor_reduce(m8[:], p, X, ALU.max))
                    step(dve.tensor_scalar(m8[:], m8[:], -1e20, None, ALU.max))
                    own(dve.tensor_tensor(p, p, bc(m8[:], 64), ALU.subtract), s_cs, 1)

                    def fetch(j):
                        kind, h = items[j]
                        g, b = h // 4, j % 3
                        cs = chunks(items[j])
                        dve.wait_ge(s_tp, ONE + (NG + 1) * i + (first_group[j - 2] if j >= 3 else 0))
                        if j in MIXED:
                            m = MIXED.index(j)
                            dve.wait_ge(s_mb, ONE + len(MIXED) * i + m + 1)
                        for ci, (a, w) in enumerate(cs):
                            k = first_chunk[j] + ci
                            dve.wait_ge(s_qk, ONE + NCK * i + k + 1)
                            src, dst = sp_[k % 3][:, 0:w], S[:, b, a:a + w]
                            if kind == "win" and cl:
                                add = t["wband"][:, h, a:a + w]
                            elif j in MIXED and a >= far:
                                add = t["mix_bias"][:, m % 3, a - far:a - far + w]
                            else:
                                blocks = lambda z: z.rearrange("p (b k) -> p b k", k=64)
                                src, dst, add = blocks(src), blocks(dst), bc(t["mask"][:, g, a // 64:(a + w) // 64], 64)
                            plain(dve)
                            own(dve.tensor_tensor_reduce(dst, src, add, SC, -3e38, ALU.add, ALU.max,
                                                         t["chunk_max"][:, b, ci:ci + 1]), s_ev, NCK)
                        own(dve.tensor_reduce(t["nmax"][:, b:b + 1], t["chunk_max"][:, b, 0:len(cs)], X, ALU.max, negate=True),
                            s_mx, NI - 1)

                    fetch(1)
                    dve.wait_ge(s_cx, ONE + i + 1)
                    step(dve.tensor_reduce(r8[:], p, X, ALU.add))
                    step(dve.tensor_scalar(r8[:], r8[:], 1e-30, None, ALU.max))
                    step(dve.reciprocal(r8[:], r8[:]))
                    own(dve.tensor_tensor(p, p, bc(r8[:], 64), ALU.mult), s_cp, 1)
                    imp = t["imp"]
                    for g in range(2):
                        pv = S[:, 0, 256 * g:256 * g + 256].rearrange("p (r j w) -> p j r w", r=4, w=2)
                        step(dve.tensor_reduce(imp[:, g], pv, XY, ALU.add))
                    fetch(2)
                    fetch(3)
                    sbw = t["score_band"][:, ds(i * -2 + (30 - 8 * cl), 32)]
                    for g in range(2):
                        step(dve.tensor_tensor(imp[:, g], imp[:, g], sbw, ALU.add))
                    step(dve.tensor_scalar(imp[:, :, 0], imp[:, :, 0], 1e4, None, ALU.max))
                    for g in range(2):
                        plain(dve)
                        step(dve.max(t["top"][:, g], imp[:, g]))
                        plain(dve)
                        step(dve.match_replace(t["mask"][:, g], t["top"][:, g], imp[:, g], -2e30))
                    own(dve.tensor_scalar(t["mask"][:], t["mask"][:], -1.5e30, NEG, ALU.is_gt, ALU.mult), s_mk, 1)
                    for j in range(4, NI):
                        fetch(j)

                    dve.wait_ge(s_exp, ONE + (NI - 1) * (i + 1))
                    dve.wait_ge(s_ge, ONE + i + 1)
                    rs, cf, o, o2 = t["rsum"], t["coef"], t["o_att"], t["o_tmp"]
                    hv = lambda a: a.rearrange("p (h n) -> p h n", n=64)
                    dve.wait_ge(s_pv, ONE + NG * i + 2)
                    step(dve.tensor_tensor(hv(o[:]), O[0][:], bc(gn[:, 0:8], 64), ALU.mult))
                    step(dve.reciprocal(cf[:], rs[:]))
                    step(dve.tensor_tensor(cf[:, 0:8], cf[:, 0:8], gn[:, 16:24], ALU.mult))
                    own(dve.tensor_tensor(cf[:, 8:16], cf[:, 8:16], gn[:, 8:16], ALU.mult), s_cf, 1)
                    for br, c0 in ((2, 0), (1, 8)):
                        dve.wait_ge(s_pv, ONE + NG * i + (first_group[1 + NH] if br == 2 else NG))
                        ins = dve.tensor_tensor(hv(o2[:]), O[br][:], bc(cf[:, c0:c0 + 8], 64), ALU.mult)
                        if br == 1:
                            own(ins, s_comb, 1)
                        else:
                            step(ins)
                        step(dve.tensor_tensor(o[:], o[:], o2[:], ALU.add))
                    own(dve.tensor_tensor(o2[:], o[:], o[:], ALU.mult), s_ss, 1)
                    step(dve.tensor_reduce(t["var"][:], o2[:], X, ALU.add))
                    own(dve.tensor_scalar(t["var"][:], t["var"][:], 1 / 512, EPS, ALU.mult, ALU.add), s_vr, 1)
                    dve.wait_ge(s_pw, ONE + i + 1)
                    own(dve.tensor_scalar(o[:], o[:], t["rstd"][:, 0:1], None, ALU.mult), s_on, 1)
                own.close()


def sample(nc, d, t):
    ROWS = NB * NH
    with ExitStack() as ctx:
        sb = lambda n, s, dt=F32: ctx.enter_context(nc.sbuf_tensor(n, s, dt))
        pb = lambda n, s: ctx.enter_context(nc.psum_tensor(n, s, F32))
        sem = ctx.enter_context(semaphores(nc, "sm_"))
        wk, wv = sb("win_k", [128, NB, 512]), sb("win_v", [128, NB, 4, 128])
        kg, vg = sb("sel_k", [64, NB, 2, 8, 64]), sb("sel_v", [128, NB, 2, 4, 64])
        ksn = sb("new_ks", [64, 2, NB])
        kwn = sb("new_kw", [128, NB])
        qz, qs = sb("q_padded", [128, NH, NB]), sb("q_groups", [64, 2, 4, NB])
        gr = sb("gate_rows", [ROWS, 3])
        bias = {"cmp": sb("bias_cmp", [ROWS, 256]), "win": sb("bias_win", [ROWS, 512]), "sel": sb("bias_sel", [ROWS, 512])}
        near = sb("bias_near", [ROWS, 64])
        pti, pb2 = sb("pages_int", [ROWS, NPAGE], I32), sb("phys_block", [ROWS, NPAGE, 2])
        iota, own4, own8 = sb("iota", [ROWS, 128]), sb("same_group", [ROWS, ROWS]), sb("same_token", [ROWS, ROWS])
        side = sb("group_rows", [ROWS, 2])
        gain = sb("gain_rows", [ROWS, HD])
        sT, R = sb("scores_T", [128, 4, ROWS]), {k: sb("rows_" + k, [ROWS, n]) for k, n in (("cmp", 256), ("win", 512), ("sel", 512))}
        pT = {k: sb("probs_T_" + k, [128, n, ROWS]) for k, n in (("cmp", 2), ("win", 4), ("sel", 4))}
        imp, junk = sb("importance", [ROWS, 128]), sb("picked", [ROWS, 128])
        top, idx, idf, ind = sb("top", [ROWS, 8]), sb("top_index", [ROWS, 8], U32), sb("top_float", [ROWS, 8]), sb("is_last", [ROWS, 8])
        ph, phi, prow = sb("phys", [ROWS, 7]), sb("phys_int", [ROWS, 7], I32), sb("phys_row", [1, ROWS * 7], I32)
        mx, rsm = sb("row_max", [ROWS, 3]), sb("row_sum", [ROWS, 3])
        aw, dd, o = sb("out_cmp_win", [128, ROWS]), sb("out_sel", [64, ROWS]), sb("o_rows", [ROWS, HD])
        o2, ss, sd = sb("o_scratch", [ROWS, HD]), sb("o_sumsq", [ROWS, 1]), sb("o_std", [ROWS, 1])
        om = sb("o_heads", [HD, NH, NB])
        psS, psR, psP = pb("ps_sT", [128, 4, ROWS]), pb("ps_rows", [ROWS, 4, 128]), pb("ps_pT", [128, 4, ROWS])
        psI, psA, psD, psX = pb("ps_imp", [ROWS, 128]), pb("ps_aw", [128, ROWS]), pb("ps_sel_o", [64, ROWS]), pb("ps_turn", [64, 256])
        s_z, s_c, s_n, s_wo, s_ph, s_pr, s_sel, s_mm, s_dv, s_ac, s_mo = (sem(n) for n in (
            "cleared", "inputs_loaded", "new_token_placed", "window_out", "phys_stored", "phys_loaded", "selected_loaded",
            "pe_steps", "dve_steps", "act_steps", "mix_sent"))
        s_wl = sem("window_loaded")
        col = slice(SEQ, NTOK)
        PE = ["sT_cmp", "R_cmp", "imp", "pT_cmp", "sT_win", "R_win", "pT_win", "sT_sel", "R_sel", "pT_sel", "aw", "sel_o",
              "turn", "token_sum", "heads"]
        pe_at = {n: i + 1 for i, n in enumerate(PE)}
        DV = ["sc_cmp", "s_cmp", "nm_cmp", "rec_cmp", "p_cmp", "pair_sum", "imp", "top", "index", "float", "plus_one", "pages_f", "even", "odd",
              "pick0", "pick1", "pick2", "pick3", "pick4", "ph1", "ph2", "phys_int", "gated_cmp", "c_pT_cmp",
              "new_kw", "new_ks", "sc_win", "s_win", "nm_win", "rec_win", "p_win", "c_pT_win",
              "is_last", "b3", "b4", "b5", "b6", "b7", "sc_sel", "s_sel", "nm_sel", "rec_sel", "p_sel", "c_pT_sel",
              "c_aw", "c_dd", "o_a", "o_b", "o_c", "o_sq", "o_ss", "std_r", "o_n", "o_g", "c_heads"]
        dv_at = {n: i + 1 for i, n in enumerate(DV)}
        n_in = 5 + 2 + 4 + 8 * (1 + 1 + 1 + 3 + 1 + 1)

        with nc.Block() as block:
            @block.gpsimd
            def _(pool):
                own = Own(pool)
                for a, v in ((qz[:], 0.0), (kg[:, :, :, 0], 0.0), (vg[0:64, :, :, 0], 0.0), (bias["cmp"][:], 0.0),
                             (bias["sel"][:, 0:64], NEG), (bias["sel"][:, 64:128], 0.0)):
                    own(pool.memset(a, v), s_z, 6)

            @block.sync
            def _(sp):
                ld = lambda a, b: sp.dma_start(a, b).then_inc(s_c, 16)
                for b in range(NB):
                    sp.dma_start(wk[:, b, 0:511], d["win_k"][b, :, 1:512]).then_inc(s_wl, 16)
                    for ti in range(4):
                        n = 127 if ti == 3 else 128
                        sp.dma_start(wv[0:n, b, ti], d["win_v"][b, 128 * ti + 1:128 * ti + 1 + n]).then_inc(s_wl, 16)
                with nc.allow_non_contiguous_dma(reason="one new token"):
                    for b in range(NB):
                        sp.dma_start(wv[127:128, b, 3], d["kvT"][KVROW["vw"], :, SEQ + b:SEQ + b + 1].rearrange("p n -> n p")).then_inc(s_wl, 16)
                ld(kwn[:], d["kvT"][KVROW["kw"], :, col])
                for a, n in ((iota, "iota"), (own4, "same_group"), (own8, "same_token"), (side, "group_rows")):
                    ld(a[:], d[n])
                for g in range(2):
                    ld(ksn[:, g], d["kvT"][KVROW["ks"], 64 * g:64 * g + 64, col])
                sp.wait_ge(s_z, 6)
                for g in range(2):
                    r = slice(64 * g, 64 * g + 64)
                    ld(qz[r, 4 * g:4 * g + 4], d["qT"][:, r, col].rearrange("r p n -> p r n"))
                    ld(qs[:, g], d["qT"][:, r, col].rearrange("r p n -> p r n"))
                with nc.allow_non_contiguous_dma(reason="a few values per row"):
                    for b in range(NB):
                        r = slice(NH * b, NH * b + NH)
                        for g in range(2):
                            src = d["kvT"][KVROW["vs"], 64 * g:64 * g + 64, SEQ + b:SEQ + b + 1].rearrange("p n -> n p")
                            sp.dma_start(vg[0:1, b, g, 0], src).then_inc(s_n, 16)
                        ld(gr[r], d["gT"][:, SEQ + b:SEQ + b + 1].rearrange("(k h) n -> h (k n)", k=3))
                        ld(bias["cmp"][r, 252:256], d["line"][:, 543:640:32])
                        ld(bias["win"][r], d["line"][:, 129:641])
                        ld(bias["sel"][r, 0:1], d["line"][:, 640:641])
                        ld(bias["sel"][r, 128:192], d["line"][:, 576:640])
                        ld(near[r], d["line"][:, 512:576])
                        ld(pti[r], d["page_table"][0:1, NPAGE * b:NPAGE * (b + 1)].to_broadcast([NH, NPAGE]))
                        ld(gain[r], d["out_gain"])
                sp.dma_start(d["conv_prev"], d["state_conv"][:, :, 1]).then_inc(s_wo, 16)
                sp.wait_ge(s_dv, dv_at["new_kw"])
                sp.wait_ge(s_wl, 16 * 6 * NB)
                sp.dma_start(d["win_k_out"].rearrange("b p n -> p b n"), wk[:]).then_inc(s_wo, 16)
                sp.dma_start(d["win_v_out"].rearrange("b (t p) n -> p b t n", p=128), wv[:]).then_inc(s_wo, 16)
                sp.wait_ge(s_dv, dv_at["phys_int"])
                sp.dma_start(d["phys"], phi[:]).then_inc(s_ph, 16)
                sp.wait_ge(s_ph, 16)
                sp.dma_start(prow[:], d["phys"].rearrange("r s -> (r s)").rearrange("(o n) -> o n", o=1)).then_inc(s_pr, 16)
                sp.wait_ge(s_pr, 16)
                with sp.Fori(0, NB) as b:
                    for g in range(2):
                        for s in range(7):
                            v = sp.value_load(prow[0:1, ds(b * 56 + (28 * g + s), 1)], min_val=0, max_val=d["sel_k"].shape[0] - 1)
                            sp.dma_start(kg[:, ds(b, 1), g, s + 1].rearrange("p a n -> p (a n)"),
                                         d["sel_k"][ds(v, 1), g].rearrange("a p n -> (a p) n")).then_inc(s_sel, 16)
                sp.wait_ge(s_dv, dv_at["c_heads"])
                dst = d["mixT"][0:4].rearrange("j (a d) n -> d (j a) n", a=2)[:, :, col]
                sp.dma_start(dst, om[:]).then_inc(s_mo, 16)
                sp.wait_ge(s_mo, 16)
                sp.wait_ge(s_wo, 48)

            @block.tensor
            def _(pe):
                def done(mm):
                    mm.then_inc(s_mm, 1)

                def rows(k, n):
                    for y in range(n):
                        mm = pe.transpose(psR[:, y], sT[:, y], t["ident"][:])
                    done(mm)

                def probs(k, n):
                    for y in range(n):
                        mm = pe.transpose(psP[:, y], R[k][:, 128 * y:128 * y + 128], t["ident"][0:ROWS, 0:ROWS])
                    done(mm)
                pe.wait_ge(s_c, 16 * n_in)
                for b in range(NB):
                    for y in range(2):
                        a = NCP + 256 * b + 128 * y
                        mm = pe.matmul(psS[:, y, NH * b:NH * b + NH], t["kcT"][:, a:a + 128], qz[:, :, b], start=True, stop=True)
                done(mm)
                pe.wait_ge(s_dv, dv_at["sc_cmp"])
                rows("cmp", 2)
                pe.wait_ge(s_dv, dv_at["pair_sum"])
                done(pe.matmul(psI[:], own4[:], junk[:], start=True, stop=True))
                pe.wait_ge(s_dv, dv_at["gated_cmp"])
                probs("cmp", 2)
                pe.wait_ge(s_dv, dv_at["new_kw"])
                for b in range(NB):
                    for y in range(4):
                        mm = pe.matmul(psS[:, y, NH * b:NH * b + NH], wk[:, b, 128 * y:128 * y + 128], qz[:, :, b],
                                       start=True, stop=True)
                done(mm)
                pe.wait_ge(s_dv, dv_at["sc_win"])
                rows("win", 4)
                pe.wait_ge(s_dv, dv_at["p_win"])
                probs("win", 4)
                pe.wait_ge(s_sel, 16 * 2 * 2 * 7 * NB)
                pe.wait_ge(s_n, 16 * 2 * NB)
                for b in range(NB):
                    for g in range(2):
                        for y in range(4):
                            a = NH * b + 4 * g
                            mm = pe.matmul(psS[:, y, a:a + 4], kg[:, b, g, 2 * y:2 * y + 2].rearrange("p s n -> p (s n)"),
                                           qs[:, g, :, b], start=True, stop=True)
                done(mm)
                pe.wait_ge(s_dv, dv_at["sc_sel"])
                rows("sel", 4)
                pe.wait_ge(s_dv, dv_at["p_sel"])
                probs("sel", 4)
                pe.wait_ge(s_dv, dv_at["c_pT_sel"])
                for b in range(NB):
                    a = NH * b
                    for y in range(2):
                        pe.matmul(psA[:, a:a + NH], t["vcs"][:, 2 * b + y], pT["cmp"][:, y, a:a + NH], start=(y == 0), stop=False)
                    for y in range(4):
                        mm = pe.matmul(psA[:, a:a + NH], wv[:, b, y], pT["win"][:, y, a:a + NH], start=False, stop=(y == 3))
                done(mm)
                for b in range(NB):
                    for g in range(2):
                        a = NH * b + 4 * g
                        for y in range(4):
                            mm = pe.matmul(psD[:, a:a + 4], vg[:, b, g, y], pT["sel"][:, y, a:a + 4], start=(y == 0), stop=(y == 3))
                done(mm)
                pe.wait_ge(s_dv, dv_at["c_dd"])
                pe.transpose(psX[:, 0:128], aw[:], t["ident"][:])
                done(pe.transpose(psX[:, 128:192], dd[:], t["ident"][0:64, 0:64]))
                pe.wait_ge(s_dv, dv_at["o_ss"])
                done(pe.matmul(psI[:, 0:1], own8[:], ss[:], start=True, stop=True))
                pe.wait_ge(s_dv, dv_at["o_g"])
                done(pe.transpose(psX[:, 192:256], o[:], t["ident"][0:64, 0:64]))

            @block.scalar
            def _(act):
                def exp(k, i):
                    act.wait_ge(s_dv, dv_at["nm_" + k])
                    act.activation(R[k][:], R[k][:], ACT.Exp, bias=mx[:, i:i + 1], accum_out=rsm[:, i:i + 1]).then_inc(s_ac, 1)
                exp("cmp", 0)
                act.wait_ge(s_pr, 16)
                with act.Fori(0, NB) as b:
                    for g in range(2):
                        for s in range(7):
                            v = act.value_load(prow[0:1, ds(b * 56 + (28 * g + s), 1)], min_val=0, max_val=d["sel_k"].shape[0] - 1)
                            q = 64 * ((s + 1) % 2)
                            act.dma_start(vg[q:q + 64, ds(b, 1), g, (s + 1) // 2].rearrange("p a n -> p (a n)"),
                                          d["sel_v"][ds(v, 1), g].rearrange("a p n -> (a p) n")).then_inc(s_sel, 16)
                exp("win", 1)
                exp("sel", 2)
                act.wait_ge(s_mm, pe_at["token_sum"])
                act.activation(sd[:], psI[:, 0:1], ACT.Sqrt, bias=t["eps"][0:ROWS]).then_inc(s_ac, 1)

            @block.vector
            def _(dve):
                n = [0]

                def step(name, ins):
                    assert DV[n[0]] == name, (DV[n[0]], name)
                    n[0] += 1
                    ins.then_inc(s_dv, 1)
                    dve.wait_ge(s_dv, n[0])
                SC = HD ** -0.5

                def scores(k, tiles):
                    dve.wait_ge(s_mm, pe_at["sT_" + k])
                    step("sc_" + k, dve.tensor_copy(sT[:, 0:tiles], psS[:, 0:tiles]))
                    dve.wait_ge(s_mm, pe_at["R_" + k])
                    src = psR[:, 0:tiles].rearrange("p a b -> p (a b)")
                    step("s_" + k, dve.scalar_tensor_tensor(R[k][:], src, SC, bias[k][:], ALU.mult, ALU.add))
                    i = "cmp win sel".split().index(k)
                    step("nm_" + k, dve.tensor_reduce(mx[:, i:i + 1], R[k][:], X, ALU.max, negate=True))
                    dve.wait_ge(s_ac, i + 1)

                dve.wait_ge(s_c, 16 * n_in)
                scores("cmp", 2)
                p = R["cmp"]
                step("rec_cmp", dve.reciprocal(rsm[:, 0:1], rsm[:, 0:1]))
                step("p_cmp", dve.tensor_scalar(p[:], p[:], rsm[:, 0:1], None, ALU.mult))
                pv = p[:].rearrange("p (j w) -> p j w", w=2)
                step("pair_sum", dve.scalar_tensor_tensor(junk[:], pv[:, :, 0], 1.0, pv[:, :, 1], ALU.mult, ALU.add))
                dve.wait_ge(s_mm, pe_at["imp"])
                step("imp", dve.tensor_copy(imp[:], psI[:]))
                step("top", dve.max(top[:], imp[:, 1:127]))
                step("index", dve.max_index(idx[:], top[:], imp[:, 1:127]))
                step("float", dve.tensor_copy(idf[:], idx[:]))
                step("plus_one", dve.tensor_scalar(idf[:], idf[:], 1.0, None, ALU.add))
                step("pages_f", dve.tensor_copy(pb2[:, :, 1], pti[:]))
                step("even", dve.tensor_scalar(pb2[:, :, 0], pb2[:, :, 1], 2.0, None, ALU.mult))
                step("odd", dve.tensor_scalar(pb2[:, :, 1], pb2[:, :, 0], 1.0, None, ALU.add))
                blocks = pb2[:].rearrange("p a b -> p (a b)")
                for k in range(5):
                    step(f"pick{k}", dve.scalar_tensor_tensor(junk[:], iota[:], idf[:, k:k + 1], blocks, ALU.is_equal, ALU.mult,
                                                              accum_out=ph[:, 2 + k:3 + k]))
                step("ph1", dve.tensor_copy(ph[:, 0:1], blocks[:, 0:1]))
                step("ph2", dve.tensor_copy(ph[:, 1:2], blocks[:, 127:128]))
                step("phys_int", dve.tensor_copy(phi[:], ph[:]))
                step("gated_cmp", dve.tensor_scalar(p[:], p[:], gr[:, 0:1], None, ALU.mult))
                dve.wait_ge(s_mm, pe_at["pT_cmp"])
                step("c_pT_cmp", dve.tensor_copy(pT["cmp"][:], psP[:, 0:2]))
                dve.wait_ge(s_wl, 16 * 6 * NB)
                step("new_kw", dve.tensor_copy(wk[:, :, 511], kwn[:]))
                step("new_ks", dve.tensor_copy(kg[:, :, :, 0, 0].rearrange("p b g -> p g b"), ksn[:]))

                def weigh(k, i, g):
                    step("p_" + k, dve.tensor_scalar(R[k][:], R[k][:], rsm[:, i:i + 1], gr[:, g:g + 1], ALU.mult, ALU.mult))
                scores("win", 4)
                step("rec_win", dve.reciprocal(rsm[:, 1:2], rsm[:, 1:2]))
                weigh("win", 1, 2)
                dve.wait_ge(s_mm, pe_at["pT_win"])
                step("c_pT_win", dve.tensor_copy(pT["win"][:], psP[:]))
                step("is_last", dve.tensor_scalar(ind[:], idf[:], 126.0, None, ALU.is_equal))
                for k in range(5):
                    step(f"b{3 + k}", dve.tensor_scalar(bias["sel"][:, 64 * (3 + k):64 * (4 + k)], near[:], ind[:, k:k + 1], None, ALU.mult))
                scores("sel", 4)
                step("rec_sel", dve.reciprocal(rsm[:, 2:3], rsm[:, 2:3]))
                weigh("sel", 2, 1)
                dve.wait_ge(s_mm, pe_at["pT_sel"])
                step("c_pT_sel", dve.tensor_copy(pT["sel"][:], psP[:]))
                dve.wait_ge(s_mm, pe_at["aw"])
                step("c_aw", dve.tensor_copy(aw[:], psA[:]))
                dve.wait_ge(s_mm, pe_at["sel_o"])
                step("c_dd", dve.tensor_copy(dd[:], psD[:]))
                dve.wait_ge(s_mm, pe_at["turn"])
                step("o_a", dve.tensor_scalar(o2[:], psX[:, 0:64], side[:, 0:1], None, ALU.mult))
                step("o_b", dve.scalar_tensor_tensor(o[:], psX[:, 64:128], side[:, 1:2], o2[:], ALU.mult, ALU.add))
                step("o_c", dve.tensor_tensor(o[:], o[:], psX[:, 128:192], ALU.add))
                step("o_sq", dve.tensor_tensor(o2[:], o[:], o[:], ALU.mult))
                step("o_ss", dve.tensor_reduce(ss[:], o2[:], X, ALU.add))
                dve.wait_ge(s_ac, 4)
                step("std_r", dve.reciprocal(sd[:], sd[:]))
                step("o_n", dve.tensor_scalar(o[:], o[:], sd[:, 0:1], None, ALU.mult))
                step("o_g", dve.tensor_tensor(o[:], o[:], gain[:], ALU.mult))
                dve.wait_ge(s_mm, pe_at["heads"])
                step("c_heads", dve.tensor_copy(om[:], psX[:, 192:256].rearrange("p (b h) -> p h b", h=NH)))
                assert n[0] == len(DV)


def tail(nc, d, t):
    NU = 8 + 32 + 32 + 8 + 2
    RING = 6
    with ExitStack() as ctx:
        sb = lambda n, s, dt=F32: ctx.enter_context(nc.sbuf_tensor(n, s, dt))
        pb = lambda n, s: ctx.enter_context(nc.psum_tensor(n, s, F32))
        sem = ctx.enter_context(semaphores(nc, "tl_"))
        h = sb("h", [128, KT, CH])
        mx = sb("mix_chunk", [128, KT, CH])
        pT = sb("p_chunk", [128, 2, CH])
        ff = sb("ff", [128, FT, CH])
        sq = sb("h_square", [128, 2, CH])
        rs = sb("rstd_h", [128, CH])
        gate = sb("gate", [128, 2, CH])
        wr = sb("w_ring", [128, RING, 8, 128])
        gm = sb("norm_mlp_sb", [128, KT])
        gp = sb("norm_ple_sb", [128, KT])
        zp = [pb(f"ps_t{i}", [128, 2, 512]) for i in range(3)]
        ssp = pb("ps_hs", [128, 2, 512])
        V = lambda ps: ps[:, :, 0:HF]
        W = lambda a: a.rearrange("p (h n) -> p h n", h=2)
        s_c, s_in, s_o, s_wu, s_o1, s_h1, s_sq, s_sqf, s_rs, s_a, s_u, s_ut, s_f, s_dn, s_h2, s_g, s_gs, s_pj, s_y, s_rt = \
            (sem(n) for n in (
                "consts_loaded", "inputs_loaded", "y_sent", "unit_used", "wout_done", "h1_ready", "h_squared",
                "h_square_summed", "rstd_ready", "a_ready", "up_done", "up_taken", "ff_ready", "down_done", "h2_ready", "gate_done",
                "gate_ready", "proj_done", "y_ready", "roots_taken"))
        s_w = [sem(f"w{i}") for i in range(RING)]
        per_slot = [len(range(s, NU, RING)) for s in range(RING)]

        with nc.Block() as block:
            @block.sync
            def _(sp):
                sp.dma_start(gm[:], d["norm_mlp"]).then_inc(s_c, 16)
                sp.dma_start(gp[:], d["norm_ple"]).then_inc(s_c, 16)

                def load_unit(un):
                    sp.dma_start(wr[:, un % RING], d["w_tail"][un]).then_inc(s_w[un % RING], 16)

                def load_in(c):
                    sp.dma_start(h[:], d["xT"][:, :, ds(c * CH, CH)].rearrange("k p n -> p k n")).then_inc(s_in, 16)
                    sp.dma_start(mx[:], d["mixT"][:, :, ds(c * CH, CH)].rearrange("k p n -> p k n")).then_inc(s_in, 16)
                    sp.dma_start(pT[:], d["pT"][:, :, ds(c * CH, CH)].rearrange("k p n -> p k n")).then_inc(s_in, 16)

                load_in(0)
                for un in range(RING):
                    load_unit(un)

                def body(c, last):
                    for un in range(RING, NU):
                        sp.wait_ge(s_wu, NU * c + un - RING + 1)
                        load_unit(un)
                    if not last:
                        for un in range(RING):
                            before = max(range(un, NU, RING))
                            sp.wait_ge(s_wu, NU * c + before + 1)
                            load_unit(un)
                    for k in range(KT):
                        sp.wait_ge(s_y, KT * c + k + 1)
                        sp.dma_start(d["yT"][k, :, ds(c * CH, CH)], h[:, k]).then_inc(s_o, 16)
                    if not last:
                        sp.wait_ge(s_o, 16 * KT * (c + 1))
                        load_in(c + 1)
                with sp.Fori(0, 3) as c:
                    body(c, False)
                body(3, True)
                sp.wait_ge(s_o, 16 * KT * 4)

            @block.tensor
            def _(pe):
                with pe.Fori(0, 4) as c:
                    un = [0]

                    def unit():
                        n = un[0]
                        pe.wait_ge(s_w[n % RING], 16 * (per_slot[n % RING] * c + n // RING + 1))
                        return wr[:, n % RING]

                    def used(mm):
                        mm.then_inc(s_wu, 1)
                        un[0] += 1

                    def sums(k0):
                        for k in range(KT):
                            pe.wait_ge(s_sq, 2 * KT * c + k0 + k + 1)
                            for hh in range(2):
                                mm = pe.matmul(ssp[:, hh, 0:HF], t["ones_d"][:], sq[:, k % 2, hh * HF:(hh + 1) * HF],
                                               start=(k == 0), stop=(k == KT - 1))
                            mm.then_inc(s_sqf, 1)

                    def tile(zi, src, ks, w, first=True, final=True):
                        for hh in range(2):
                            for i, k in enumerate(ks):
                                mm = pe.matmul(zp[zi][:, hh, 0:HF], w[:, i], src[:, k, hh * HF:(hh + 1) * HF],
                                               start=(first and i == 0), stop=(final and i == len(ks) - 1),
                                               skip_group_check=True)
                        return mm

                    pe.wait_ge(s_in, 48 * c + 48)
                    for m in range(KT):
                        w = unit()
                        if m >= 3:
                            pe.wait_ge(s_h1, KT * c + m - 2)
                        used(tile(m % 3, mx, range(KT), w))
                    sums(0)
                    pe.wait_ge(s_a, 2 * KT * c + KT)
                    for m in range(FT):
                        w = unit()
                        if m >= 3:
                            pe.wait_ge(s_ut, FT * c + m - 2)
                        used(tile(m % 3, mx, range(KT), w))
                    pe.wait_ge(s_f, FT * (c + 1))
                    for m in range(KT):
                        if m >= 3:
                            pe.wait_ge(s_h2, KT * c + m - 2)
                        for g in range(4):
                            w = unit()
                            used(tile(m % 3, ff, range(8 * g, 8 * g + 8), w, g == 0, g == 3))
                    sums(KT)
                    pe.wait_ge(s_a, 2 * KT * (c + 1))
                    for m in range(KT):
                        w = unit()
                        if m >= 2:
                            pe.wait_ge(s_gs, KT * c + m - 1)
                        used(tile(m % 2, mx, range(KT), w))
                    for m in range(KT):
                        if m % 4 == 0:
                            w = unit()
                        if m >= 1:
                            pe.wait_ge(s_y, KT * c + m)
                        mm = tile(2, pT, range(2), w[:, 2 * (m % 4):2 * (m % 4) + 2])
                        if m % 4 == 3:
                            used(mm)
                        else:
                            mm.then_inc(s_pj, 1)

            @block.scalar
            def _(act):
                with act.Fori(0, 4) as c:
                    for r in range(2):
                        for k in range(KT):
                            if r == 0:
                                act.wait_ge(s_h1, KT * c + k + 1)
                            else:
                                act.wait_ge(s_h2, KT * c + k + 1)
                            if k >= 2:
                                act.wait_ge(s_sqf, 2 * KT * c + KT * r + k - 1)
                            act.activation(sq[:, k % 2], h[:, k], ACT.Square).then_inc(s_sq, 1)
                        act.wait_ge(s_sqf, 2 * KT * c + KT * (r + 1))
                        act.activation(W(rs[:]), V(ssp), ACT.Sqrt, bias=t["eps"][:]).then_inc(s_rt, 1)
                        if r == 0:
                            for m in range(FT):
                                act.wait_ge(s_wu, NU * c + KT + m + 1)
                                act.activation(W(ff[:, m]), V(zp[m % 3]), ACT.Relu).then_inc(s_ut, 1)
                    for m in range(KT):
                        act.wait_ge(s_wu, NU * c + KT + 2 * FT + m + 1)
                        act.activation(W(ff[:, m]), V(zp[m % 2]), ACT.Sigmoid).then_inc(s_gs, 1)

            @block.vector
            def _(dve):
                dve.wait_ge(s_c, 32)
                own = Own(dve)
                with dve.Fori(0, 4) as c:
                    own.iteration(c)
                    dve.wait_ge(s_in, 48 * c + 48)
                    for m in range(KT):
                        dve.wait_ge(s_wu, NU * c + m + 1)
                        own(dve.tensor_tensor(W(h[:, m]), V(zp[m % 3]), W(h[:, m]), ALU.add), s_h1, KT)

                    def norm(r, gain):
                        dve.wait_ge(s_rt, 2 * c + r + 1)
                        own(dve.reciprocal(rs[:], rs[:]), s_rs, 2)
                        for k in range(KT):
                            own(dve.scalar_tensor_tensor(mx[:, k], h[:, k], gain[:, k:k + 1], rs[:], ALU.mult,
                                                         ALU.mult), s_a, 2 * KT)
                    norm(0, gm)
                    for m in range(FT):
                        dve.wait_ge(s_ut, FT * c + m + 1)
                        own(dve.tensor_tensor(ff[:, m], ff[:, m], ff[:, m], ALU.mult), s_f, FT)
                    for m in range(KT):
                        dve.wait_ge(s_wu, NU * c + KT + FT + 4 * (m + 1))
                        own(dve.tensor_tensor(W(h[:, m]), V(zp[m % 3]), W(h[:, m]), ALU.add), s_h2, KT)
                    norm(1, gp)
                    for m in range(KT):
                        dve.wait_ge(s_gs, KT * c + m + 1)
                        if m % 4 == 3:
                            dve.wait_ge(s_wu, NU * c + 2 * KT + 2 * FT + m // 4 + 1)
                        else:
                            dve.wait_ge(s_pj, 6 * c + 3 * (m // 4) + m % 4 + 1)
                        own(dve.tensor_tensor(W(ff[:, m]), V(zp[2]), W(ff[:, m]), ALU.mult), s_g, KT)
                        own(dve.tensor_tensor(h[:, m], h[:, m], ff[:, m], ALU.add), s_y, KT)


def build(nc, d):
    with ExitStack() as ctx:
        sb = lambda n, s, dt=F32: ctx.enter_context(nc.sbuf_tensor(n, s, dt))
        t = {n: sb(n, [128, 128]) for n in ("ident", "ones_d", "ones_w", "ones_hd")}
        t["eps"] = sb("eps", [128, 1])
        s_k = ctx.enter_context(nc.semaphore("matrices_loaded"))
        live = ctx.enter_context(nc.semaphore("waits_passed"))

        def plain(eng):
            eng.sem_inc(live, 1)
        t["plain"] = plain
        with nc.Block() as block:
            @block.sync
            def _(sp):
                for i, n in enumerate(("ident", "ones_d", "ones_w", "ones_hd")):
                    sp.dma_start(t[n][:], d["matrices"][i]).then_inc(s_k, 16)
                sp.wait_ge(s_k, 64)

            @block.gpsimd
            def _(pool):
                pool.memset(t["eps"][:], EPS)
        project(nc, d, t)
        with ExitStack() as held:
            keep = lambda n, s, dt=F32: t.__setitem__(n, held.enter_context(nc.sbuf_tensor(n + "_sb", s, dt)))
            keep("band", [128, NH, BANDW])
            keep("kcT", [128, NCP + NCS])
            keep("kcz", [128, 2, NCP])
            keep("vcp", [NCP, 128])
            keep("vcs", [128, 2 * NB, 128])
            setup(nc, d, t)
            compress(nc, d, t)
            with ExitStack() as inner:
                keep = lambda n, s, dt=F32: t.__setitem__(n, inner.enter_context(nc.sbuf_tensor(n + "_pr", s, dt)))
                for n in ("ks", "kw"):
                    keep(n, [128, 2, SEQ])
                for n in ("vs", "vw"):
                    keep(n, [128, SEQ // 128, 128])
                for n, shape in (("S", [128, 3, SEQ]), ("mix_bias", [128, 3, 640]), ("wband", [128, NH, 640]), ("chunk_max", [128, 3, 8]),
                                 ("PT", [128, 3, 4, 128]), ("cband", [128, NH, 124]),
                                 ("score_band", [128, 64]), ("tri", [128, 128]), ("half", [128, 1]), ("att_gain", [128, 4]),
                                 ("q_tile", [128, 4, 128]), ("g_tile", [24, 128]), ("gates_tok", [128, 24]),
                                 ("mix_tile", [128, 4, 128]), ("nmax", [128, 3]), ("rsum", [128, 16]), ("coef", [128, 16]), ("cmax", [128, NH]),
                                 ("csum", [128, NH]), ("imp", [128, 2, 32]), ("top", [128, 2, 8]), ("mask", [128, 2, 32]),
                                 ("o_att", [128, 512]), ("o_tmp", [128, 512]), ("var", [128, 1]), ("rstd", [128, 1])):
                    keep(n, shape)
                prompt_keys(nc, d, t)
                for cl in range(4):
                    prompt(nc, d, t, cl)
            sample(nc, d, t)
        tail(nc, d, t)


def constants():
    p = np.arange(128)
    ident = np.eye(128, dtype=np.float32)
    blk = (p[:, None] // HD == p[None, :] // HD).astype(np.float32) / HD
    mats = np.stack([ident, np.full((128, 128), 1 / D), np.full((128, 128), 1 / 512), blk]).astype(np.float32)
    dist = 640 - np.arange(LINEW)
    n = np.maximum(dist, 1).astype(np.float32)
    large = 16 + (np.log(n / 16) / np.float32(np.log(8.0)) * 16).astype(np.int32)
    bucket = np.where(dist < 16, np.maximum(dist, 0), np.minimum(large, 31))
    onehot = (np.arange(32)[:, None] == bucket[None]).astype(np.float32)
    onehot[31] -= 1.0
    onehot[:, dist < 0] = 0
    rel = np.arange(BANDW) - 512
    cmask = np.where(rel[None] > p[:, None], NEG, 0).astype(np.float32)
    tri = np.where(p[None] > p[:, None], 0, NEG).astype(np.float32)
    r = np.arange(NB * NH)
    rel_blk, cur = np.arange(64)[None] - 30, (p >= 64).astype(int)[:, None]
    score = np.where(rel_blk > cur, NEG, np.where(rel_blk >= cur - 1, 1e4, 0)).astype(np.float32)
    return {"matrices": mats, "onehot": onehot, "cmask": cmask, "tri": tri, "score_band": score,
            "iota": np.broadcast_to(np.arange(128, dtype=np.float32), (NB * NH, 128)).copy(),
            "same_group": (r[:, None] // 4 == r[None] // 4).astype(np.float32),
            "same_token": ((r[:, None] // NH == r[None] // NH) / 512).astype(np.float32),
            "group_rows": np.stack([r % NH < 4, r % NH >= 4], axis=1).astype(np.float32)}


def lay_out(x):
    a = {k: np.asarray(v) for k, v in x.items()}
    A = np.ascontiguousarray
    feat = lambda v, n: v.reshape(-1, n * 128).T.reshape(n, 128, -1)
    tok = lambda p, s, n: A(np.concatenate([feat(p, n), feat(s, n)], axis=2))
    tiles = lambda w: w.reshape(w.shape[0] // 128, 128, -1, 128).transpose(2, 1, 0, 3)
    w = a["w_in"][0]
    o = 512
    cols = {k: np.arange(o + 128 * i, o + 128 * (i + 1)) for i, k in enumerate(("kc", "vc", "ks", "vs", "kw", "vw"))}
    for j in range(4):
        cols[f"q{j}"] = np.r_[HD * j:HD * (j + 1), HD * (4 + j):HD * (5 + j)]
        for i, k in enumerate(("cb", "cc", "ch")):
            s = 512 + 768 + 24 + 512 * i + 128 * j
            cols[f"{k}{j}"] = np.arange(s, s + 128)
    order = np.concatenate([cols[k] for k in ZT[:-1]])
    r = {"xT": tok(a["x_prompt"], a["x_sample"], 8), "pT": tok(a["p_prompt"], a["p_sample"], 2)}
    r["w_in"] = A(tiles(w[:, order]))
    r["w_gates"] = A(w[:, 1280:1304].reshape(8, 128, 24).transpose(1, 0, 2))
    vec = lambda v: A(v.reshape(-1, 128).T)
    r["norm_mix"], r["norm_mlp"], r["norm_ple"] = (vec(a[k]) for k in ("norm_mix", "norm_mlp", "norm_ple"))
    on = vec(a["out_norm"])
    r["att_gain"], r["conv_gain"] = A(on[:, 0:4]), A(on[:, 4:8])
    two = lambda v: np.concatenate([v, v])
    r["qk_gain"] = A(np.stack([two(a["q_norm"][0])] * 4 + [two(a["k_norm"][0, 1]), two(a["k_norm"][0, 2])], axis=1))
    r["conv_w"] = A(a["conv_w"][0].reshape(3, 4, 128).transpose(2, 1, 0))
    r["state_conv"] = A(a["state_conv"][0].reshape(NB, 2, 4, 128).transpose(3, 2, 1, 0))
    r["rel_bias"] = a["rel_bias"]
    r["cache_cmp"] = A(a["cache_cmp_kv"][0].transpose(0, 3, 4, 2, 1).reshape(-1, 128, 2, PAGE))
    r["page_table"] = A(a["page_table"].reshape(1, -1))
    r["w_cmp"] = A(a["w_cmp"][0].transpose(0, 2, 1, 3))
    r["cmp_pe"] = A(np.concatenate([a["cmp_pe"][0].transpose(2, 0, 1)] * 2))
    sel = a["cache_sel_kv"][0].reshape(-1, 64, 2, 2, HD)
    r["sel_k"], r["sel_v"] = A(sel[:, :, 0].transpose(0, 2, 3, 1)), A(sel[:, :, 1].transpose(0, 2, 1, 3))
    w = a["state_win_kv"][0].reshape(NB, 512, 2, 128)
    r["win_k"], r["win_v"] = A(w[:, :, 0].transpose(0, 2, 1)), A(w[:, :, 1])
    r["out_gain"] = A(a["out_norm"][0, :512].reshape(NH, HD))
    r["k_norm_cmp"] = A(two(a["k_norm"][0, 0])[:, None])
    up, down, out_, gate = tiles(a["w_up"][0]), tiles(a["w_down"][0]), tiles(a["w_out"][0]), tiles(a["w_ple_gate"][0])
    down = down.reshape(8, 128, 4, 8, 128).transpose(0, 2, 1, 3, 4).reshape(32, 128, 8, 128)
    proj = tiles(a["w_ple_proj"][0]).reshape(2, 4, 128, 2, 128).transpose(0, 2, 1, 3, 4).reshape(2, 128, 8, 128)
    r["w_tail"] = A(np.concatenate([out_, up, down, gate, proj]))
    return r


OUTS = {"yT": [8, 128, NTOK], "kvT": [6, 128, NTOK], "uT": [4, 128, NB + 2],
        "win_k_out": [NB, 128, 512], "win_v_out": [NB, 512, 128], "conv_prev": [128, 4, NB]}
SCRATCH = {"qT": [4, 128, NTOK], "mixT": [8, 128, NTOK], "gT": [24, NTOK], "line": [NH, LINEW],
           "skew": [128, NH * LINEW], "phys": [NB * NH, 7]}


def kernel(**inputs):
    import concourse.bacc as bacc
    from concourse.bass_utils import run_bass_kernel_spmd

    nc = bacc.Bacc("TRN2", target_bir_lowering=False, num_devices=1)
    arrays = {**lay_out(inputs), **constants()}
    d = {n: nc.dram_tensor("in_" + n, v.shape, mybir.dt.from_np(v.dtype), kind="ExternalInput").ap()
         for n, v in arrays.items()}
    for n, s in OUTS.items():
        d[n] = nc.dram_tensor("out_" + n, s, F32, kind="ExternalOutput").ap()
    for n, s in SCRATCH.items():
        d[n] = nc.dram_tensor("scratch_" + n, s, I32 if n == "phys" else F32, kind="Internal").ap()
    build(nc, d)
    r = run_bass_kernel_spmd(nc, [{"in_" + n: v for n, v in arrays.items()}], core_ids=[0]).results[0]
    g = {n: r["out_" + n] for n in OUTS}
    y = g["yT"].reshape(D, NTOK).T
    kv = g["kvT"].reshape(6, 128, NTOK).transpose(2, 0, 1).reshape(NTOK, 3, 2, 2, HD)
    uT = g["uT"].reshape(512, NB + 2).T
    p, s = kv[:SEQ], kv[SEQ:]
    wk, wv = g["win_k_out"].transpose(0, 2, 1).reshape(NB, 512, 2, HD), g["win_v_out"].reshape(NB, 512, 2, HD)
    wk = np.stack([wk, wv], axis=2)[None]
    prev = g["conv_prev"].transpose(2, 1, 0).reshape(NB, 512)
    sc = np.stack([prev, uT[2:]], axis=1)[None]
    return (y[None, :SEQ].copy(), y[SEQ:, None].copy(), p[None, None, :, 0].copy(), p[None, None, :, 1].copy(),
            p[None, None, -512:, 2].copy(), uT[None, None, 0:2].copy(), s[None, :, None, 0].copy(),
            s[None, :, None, 1].copy(), wk, sc)
```

```python
from contextlib import ExitStack

import numpy as np

import concourse.bass as bass
from concourse import mybir

ALU = mybir.AluOpType
ACT = mybir.ActivationFunctionType
F32 = mybir.dt.float32
I32 = mybir.dt.int32
U32 = mybir.dt.uint32
X = mybir.AxisListType.X
XY = mybir.AxisListType.XY

D = 1024
SEQ = 2048
NB = 8
NTOK = SEQ + NB
CH = NTOK // 4
HF = CH // 2
NEG = -1e30
EPS = 1e-6
HD = 64
NH = 8
KT = D // 128
FT = 4 * D // 128
PAST = 8192
PAGE = 128
NPAGE = PAST // PAGE
CB = 32
BANDW = 1024
LINEW = 1152
NCP = SEQ // CB
NCS = NB * PAST // CB
ZT = ["q0", "q1", "q2", "q3", "ks", "kw", "kc", "vc", "vs", "vw"] + \
     [f"{a}{j}" for j in range(4) for a in ("cc", "ch", "cb")] + ["g"]
NORMED = ZT[:6]
KVROW = {"kc": 0, "vc": 1, "ks": 2, "vs": 3, "kw": 4, "vw": 5}


class Own:

    def __init__(self, eng, start=0):
        self.eng, self.i, self.count, self.before, self.looping, self.start = eng, 0, {}, {}, False, start

    def iteration(self, i):
        if self.looping:
            self.close()
        else:
            self.before = {name: n for name, (n, _) in self.count.items()}
        self.looping, self.i, self.count = True, i, {}

    def close(self):
        for name, (n, per) in self.count.items():
            assert n == per, (name, n, per)
        self.count = {}

    def post(self, ins, sem, per):
        n = self.count.get(sem.name, (0, per))[0] + 1
        self.count[sem.name] = (n, per)
        ins.then_inc(sem, 1)

    def settle(self, sem, per):
        self.eng.wait_ge(sem, per * self.i + (self.count[sem.name][0] + self.start + self.before.get(sem.name, 0)))

    def __call__(self, ins, sem, per):
        self.post(ins, sem, per)
        self.settle(sem, per)


ONE = 1


class semaphores:

    def __init__(self, nc, prefix):
        self.nc, self.prefix, self.taken = nc, prefix, []

    def __call__(self, name):
        self.taken.append(self.nc.alloc_semaphore(name=self.prefix + name))
        return self.taken[-1]

    def start_at_one(self):
        for s in self.taken:
            self.nc.sync.sem_inc(s, ONE)
        self.nc.all_engine_barrier()

    def __enter__(self):
        return self

    def __exit__(self, *_):
        self.nc.clear_and_free_semaphores(self.taken)
        self.nc.all_engine_barrier()


def ds(a, n):
    return bass.ds(a, n)


def project(nc, d, t):
    with ExitStack() as ctx:
        sb = lambda n, s, dt=F32: ctx.enter_context(nc.sbuf_tensor(n, s, dt))
        pb = lambda n, s: ctx.enter_context(nc.psum_tensor(n, s, F32))
        sem = ctx.enter_context(semaphores(nc, "pj_"))
        win = sb("w_in_sb", [128, len(ZT) - 1, KT, 128])
        wg = sb("w_gates_sb", [128, KT, 24])
        xb = sb("x_chunk", [128, KT, CH])
        aT = sb("a_chunk", [128, KT, CH])
        sqx = sb("x_squares", [128, 2, CH])
        rs = sb("rstd_x", [128, CH])
        zs = sb("z_copy", [128, 2, CH])
        sqz = sb("z_square", [128, 2, CH])
        rn = sb("rstd_z", [128, 2, CH])
        ccs = sb("cc_copy", [128, CH])
        cv = sb("conv_sum", [128, CH])
        u = sb("u", [128, 4, CH + 2])
        y = sb("y_conv", [128, 4, CH])
        stg = sb("stage", [128, 5, CH])
        sst = sb("state_conv_sb", [128, 4, 2, NB])
        gn = sb("norm_mix_sb", [128, KT])
        gq = sb("qk_gain", [128, 6])
        gy = sb("conv_gain", [128, 4])
        cw = sb("conv_w_sb", [128, 4, 3])
        zp = [pb("ps_z0", [128, 2, 512]), pb("ps_z1", [128, 2, 512])]
        ssp = pb("ps_ssq", [128, 2, 512])
        nsp = pb("ps_nsq", [128, 2, 512])
        V = lambda ps: ps[:, :, 0:HF]
        W = lambda a: a.rearrange("p (h n) -> p h n", h=2)

        s_w, s_c, s_x, s_sq, s_sqf, s_a, s_z, s_zt, s_nq, s_nd, s_nt, s_ysq, s_ys = (sem(n) for n in (
            "w_loaded", "consts_loaded", "x_loaded", "x_squared", "x_square_used", "a_ready", "z_done", "z_taken",
            "z_squared", "z_summed", "z_sum_taken", "y_squared", "y_summed"))
        s_st, s_gp, s_gs, s_chain, s_uo, s_rt = (sem(n) for n in (
            "staged", "gates_done", "gates_staged", "dve_steps", "u_out", "roots_taken"))
        s_u0, s_carry, s_fix = sem("u_cleared"), sem("u_carried"), sem("sample_conv")
        s_o = [sem(f"stage{i}_out") for i in range(5)]
        sends = [("q", j) for j in range(4)] + [("kv", KVROW[k]) for k in ("ks", "kw", "kc", "vc", "vs", "vw")] + \
                [("g", 0)] + [("mix", 4 + j) for j in range(4)]
        NS = len(sends)
        sem.start_at_one()

        with nc.Block() as block:
            @block.sync
            def _(sp):
                def load_x(c):
                    sp.dma_start(xb[:], d["xT"][:, :, ds(c * CH, CH)].rearrange("k p n -> p k n")).then_inc(s_x, 16)

                load_x(0)
                for a, b in ((gn, "norm_mix"), (gq, "qk_gain"), (gy, "conv_gain"), (cw, "conv_w"), (sst, "state_conv")):
                    sp.dma_start(a[:], d[b]).then_inc(s_c, 16)
                for m in range(len(ZT) - 1):
                    sp.dma_start(win[:, m], d["w_in"][m]).then_inc(s_w, 16)
                sp.dma_start(wg[:], d["w_gates"]).then_inc(s_w, 16)

                def body(c, last):
                    for n, (what, row) in enumerate(sends):
                        sl = n % 5
                        if n == 10 and not last:
                            sp.wait_ge(s_a, ONE + KT * (c + 1))
                            load_x(c + 1)
                        if what == "g":
                            sp.wait_ge(s_gs, ONE + c + 1)
                        else:
                            sp.wait_ge(s_st, ONE + (NS - 1) * c + n + (n < 10))
                        dst = d["gT"][:, ds(c * CH, CH)] if what == "g" else \
                            d[{"q": "qT", "kv": "kvT", "mix": "mixT"}[what]][row, :, ds(c * CH, CH)]
                        src = stg[0:24, sl, :] if what == "g" else stg[:, sl, :]
                        sp.dma_start(dst, src).then_inc(s_o[sl], 16)
                with sp.Fori(0, 3) as c:
                    body(c, False)
                body(3, True)
                sp.dma_start(d["uT"].rearrange("j p n -> p j n"), u[:, :, CH - NB:CH + 2]).then_inc(s_uo, 16)
                sp.wait_ge(s_uo, ONE + 16)
                for sl in range(5):
                    sp.wait_ge(s_o[sl], ONE + 16 * 4 * NS // 5)

            @block.scalar
            def _(act):
                with act.Fori(0, 4) as c:
                    act.wait_ge(s_x, ONE + 16 * c + 16)
                    for k in range(KT):
                        if k >= 2:
                            act.wait_ge(s_sqf, ONE + KT * c + k - 1)
                        act.activation(sqx[:, k % 2], xb[:, k], ACT.Square).then_inc(s_sq, 1)
                    act.wait_ge(s_sqf, ONE + KT * (c + 1))
                    act.activation(W(rs[:]), V(ssp), ACT.Sqrt, bias=t["eps"][:]).then_inc(s_rt, 1)
                    for n in range(6):
                        act.wait_ge(s_nd, ONE + 6 * c + n + 1)
                        act.activation(W(rn[:, n % 2]), V(nsp), ACT.Sqrt, bias=t["eps"][:]).then_inc(s_nt, 1)
                    act.wait_ge(s_gp, ONE + c + 1)
                    act.wait_ge(s_o[0], ONE + 16 * 3 * c + 32)
                    act.activation(W(stg[0:24, 0, :]), V(zp[0])[0:24], ACT.Sigmoid).then_inc(s_gs, 1)
                    act.wait_ge(s_ys, ONE + c + 1)
                    act.activation(W(rn[:, 0]), V(nsp), ACT.Sqrt, bias=t["eps"][:]).then_inc(s_rt, 1)

            @block.tensor
            def _(pe):
                with pe.Fori(0, 4) as c:
                    for k in range(KT):
                        pe.wait_ge(s_sq, ONE + KT * c + k + 1)
                        for h in range(2):
                            mm = pe.matmul(ssp[:, h, 0:HF], t["ones_d"][:], sqx[:, k % 2, h * HF:(h + 1) * HF],
                                           start=(k == 0), stop=(k == KT - 1))
                        mm.then_inc(s_sqf, 1)

                    def norm(n):
                        pe.wait_ge(s_nq, ONE + 6 * c + n + 1)
                        if n:
                            pe.wait_ge(s_nt, ONE + 6 * c + n)
                        for h in range(2):
                            mm = pe.matmul(nsp[:, h, 0:HF], t["ones_hd"][:], sqz[:, n % 2, h * HF:(h + 1) * HF],
                                           start=True, stop=True)
                        mm.then_inc(s_nd, 1)
                    for m, name in enumerate(ZT):
                        if m == 0:
                            pe.wait_ge(s_a, ONE + KT * (c + 1))
                            pe.wait_ge(s_w, ONE + 16 * len(ZT))
                        if m >= 2:
                            pe.wait_ge(s_zt, ONE + (len(ZT) - 1) * c + m - 1)
                        for h in range(2):
                            for k in range(KT):
                                o = zp[m % 2][0:24, h, 0:HF] if name == "g" else zp[m % 2][:, h, 0:HF]
                                mm = pe.matmul(o, wg[:, k] if name == "g" else win[:, m, k],
                                               aT[:, k, h * HF:(h + 1) * HF], start=(k == 0), stop=(k == KT - 1))
                        mm.then_inc(s_gp if name == "g" else s_z, 1)
                        if 1 <= m <= 6:
                            norm(m - 1)
                    for j in range(4):
                        pe.wait_ge(s_ysq, ONE + 4 * c + j + 1)
                        for h in range(2):
                            mm = pe.matmul(nsp[:, h, 0:HF], t["ones_w"][:], aT[:, j, h * HF:(h + 1) * HF],
                                           start=(j == 0), stop=(j == 3))
                    mm.then_inc(s_ys, 1)

            @block.vector
            def _(dve):
                own = Own(dve, ONE)
                NZ = len(ZT) - 1
                link = lambda ins: own(ins, s_chain, 1 + 6 + 4 * 3 + 1)
                dve.wait_ge(s_c, ONE + 16 * 5)
                dve.memset(u[:, :, 0:2], 0.0).then_inc(s_u0, 1)
                dve.wait_ge(s_u0, ONE + 1)

                def body(c, last):
                    sent = [0]

                    def slot():
                        n = sent[0]
                        sent[0] += 1
                        dve.wait_ge(s_o[n % 5], ONE + 48 * c + 16 * (n // 5))
                        return stg[:, n % 5, :]

                    def staged(ins):
                        own(ins, s_st, NS - 1)

                    dve.wait_ge(s_rt, ONE + 2 * c + 1)
                    link(dve.reciprocal(rs[:], rs[:]))
                    for k in range(KT):
                        own(dve.scalar_tensor_tensor(aT[:, k], xb[:, k], gn[:, k:k + 1], rs[:], ALU.mult,
                                                     ALU.mult), s_a, KT)

                    def finish(n):
                        dve.wait_ge(s_nt, ONE + 6 * c + n + 1)
                        link(dve.reciprocal(rn[:, n % 2], rn[:, n % 2]))
                        staged(dve.scalar_tensor_tensor(slot(), zs[:, n % 2], gq[:, n:n + 1], rn[:, n % 2],
                                                        ALU.mult, ALU.mult))

                    for m, name in enumerate(ZT[:-1]):
                        dve.wait_ge(s_z, ONE + (len(ZT) - 1) * c + m + 1)
                        z = V(zp[m % 2])
                        if name in NORMED:
                            own(dve.tensor_copy(W(zs[:, m % 2]), z), s_zt, NZ)
                            own(dve.tensor_tensor(sqz[:, m % 2], zs[:, m % 2], zs[:, m % 2], ALU.mult), s_nq, 6)
                            if m:
                                finish(m - 1)
                        elif name in KVROW:
                            if m == 6:
                                finish(5)
                            o = slot()
                            own(dve.tensor_copy(W(o), z), s_zt, NZ)
                            staged(dve.nop())
                        elif name[:2] == "cc":
                            own(dve.tensor_copy(W(ccs[:]), z), s_zt, NZ)
                        elif name[:2] == "ch":
                            j = int(name[2])
                            own(dve.tensor_tensor(W(u[:, j, 2:CH + 2]), z, W(ccs[:]), ALU.mult), s_zt, NZ)
                            link(dve.tensor_scalar(cv[:], u[:, j, 2:CH + 2], cw[:, j, 2:3], None, ALU.mult))
                            link(dve.scalar_tensor_tensor(cv[:], u[:, j, 1:CH + 1], cw[:, j, 1:2], cv[:], ALU.mult, ALU.add))
                            link(dve.scalar_tensor_tensor(cv[:], u[:, j, 0:CH], cw[:, j, 0:1], cv[:], ALU.mult, ALU.add))
                            if last:
                                sc = cv[:, CH - NB:CH]
                                for i, past in enumerate((u[:, j, CH + 2 - NB:CH + 2], sst[:, j, 1], sst[:, j, 0])):
                                    wi = cw[:, j, 2 - i:3 - i]
                                    ins = dve.scalar_tensor_tensor(sc, past, wi, sc, ALU.mult, ALU.add) if i else \
                                        dve.tensor_scalar(sc, past, wi, None, ALU.mult)
                                    ins.then_inc(s_fix, 1)
                                    dve.wait_ge(s_fix, ONE + 3 * j + i + 1)
                            else:
                                own(dve.tensor_copy(u[:, j, 0:2], u[:, j, CH:CH + 2]), s_carry, 4)
                        else:
                            j = int(name[2])
                            own(dve.tensor_tensor(W(y[:, j]), z, W(cv[:]), ALU.mult), s_zt, NZ)
                    sent[0] += 1
                    dve.wait_ge(s_zt, ONE + (len(ZT) - 1) * (c + 1))
                    dve.wait_ge(s_gp, ONE + c + 1)
                    for j in range(4):
                        own(dve.tensor_tensor(aT[:, j], y[:, j], y[:, j], ALU.mult), s_ysq, 4)
                    dve.wait_ge(s_rt, ONE + 2 * c + 2)
                    link(dve.reciprocal(rn[:, 0], rn[:, 0]))
                    for j in range(4):
                        staged(dve.scalar_tensor_tensor(slot(), y[:, j], gy[:, j:j + 1], rn[:, 0], ALU.mult, ALU.mult))

                with dve.Fori(0, 3) as c:
                    own.iteration(c)
                    body(c, False)
                own.iteration(3)
                body(3, True)
                own.close()


def compress(nc, d, t):
    NPG = 32
    plain = t["plain"]
    with ExitStack() as ctx:
        sb = lambda n, s, dt=F32: ctx.enter_context(nc.sbuf_tensor(n, s, dt))
        pb = lambda n, s: ctx.enter_context(nc.psum_tensor(n, s, F32))
        sem = ctx.enter_context(semaphores(nc, "cp_"))
        wc = sb("w_cmp_sb", [128, 2, CB, 128])
        pe_t = sb("cmp_pe_sb", [128, 2, CB])
        cvec = sb("pe_compressed", [128, 2])
        gk = sb("k_norm_cmp", [128, 1])
        pg = [sb(f"pages{b}", [128, NPG, 2, PAGE]) for b in range(2)]
        ptab = sb("page_table_sb", [1, NB * NPAGE], I32)
        kcT, vcT = t["kcT"], sb("vcT", [128, NCP + NCS])
        cps = [pb(f"ps_cmp{b}", [128, 512]) for b in range(2)]
        sps = pb("ps_cmp_sum", [128, 512])
        tps = pb("ps_cmp_tr", [128, 4, 128])
        relb, oneh, line = sb("relb", [32, NH]), sb("oneh", [32, LINEW]), sb("line_sb", [NH, LINEW])
        cmask = sb("cmask", [128, BANDW])
        lps = pb("ps_line", [NH, 3, 512])
        line_parts = ((0, 512), (512, 512), (1024, 128))
        sq = pg[0][:, 0:2, :, :].rearrange("p a b c -> p (a b c)")
        rt = pg[0][:, 2:4, :, :].rearrange("p a b c -> p (a b c)")
        s_z, s_w, s_c, s_cv, s_cvd, s_pr, s_sq, s_sum, s_rt, s_rc, s_kn, s_tr, s_te = (sem(n) for n in (
            "weights_cleared", "weights_loaded", "consts_loaded", "pe_summed", "pe_copied",
            "prompt_loaded", "squared", "squares_summed", "root", "reciprocal", "k_normed", "v_transposed", "v_copied"))
        s_k0 = sem("k_copied")
        s_pg, s_done, s_ev = ([sem(f"{n}{b}") for b in range(2)] for n in ("pages", "chunk_summed", "chunk_copied"))
        sem.start_at_one()
        s_ri, s_lm, s_line, s_cm, s_st, s_band, s_out = (sem(n) for n in (
            "rel_bias_loaded", "line_summed", "line_copied", "band_mask_loaded", "line_stored", "band_loaded", "band_masked"))
        NCH = NB * NPAGE // NPG
        pieces = [(512 * i, 512) for i in range(4)] + [(2048, 64)]

        HALF, AT_ONCE = NPG // 2, 8

        def load_pages(eng, side):
            with eng.Fori(0, NCH // 2) as i:
                for b in range(2):
                    eng.wait_ge(s_done[b], ONE + i)
                    plain(eng)
                    with eng.Fori(0, HALF // AT_ONCE) as j:
                        base = j * AT_ONCE + HALF * side
                        pages = [eng.value_load(ptab[0:1, ds(i * (2 * NPG) + (base + (NPG * b + x)), 1)], min_val=0,
                                                max_val=d["cache_cmp"].shape[0] - 1) for x in range(AT_ONCE)]
                        for x, page in enumerate(pages):
                            eng.dma_start(pg[b][:, ds(base + x, 1)].rearrange("p a k n -> p (a k) n"),
                                          d["cache_cmp"][ds(page, 1)].rearrange("a p k n -> (a p) k n")).then_inc(s_pg[b], 16)

        with nc.Block() as block:
            @block.gpsimd
            def _(pool):
                own = Own(pool, ONE)
                for kv in range(2):
                    own(pool.memset(wc[:, kv], 0.0), s_z, 2)
                pool.dma_start(relb[:], d["rel_bias"]).then_inc(s_ri, 16)
                pool.dma_start(oneh[:], d["onehot"]).then_inc(s_ri, 16)
                pool.dma_start(cmask[:], d["cmask"]).then_inc(s_cm, 16)
                pool.wait_ge(s_line, 3)
                pool.dma_start(d["line"], line[:]).then_inc(s_st, 16)
                pool.wait_ge(s_st, 16)
                every = bass.AP(tensor=d["line"].tensor, offset=0, ap=[[0, 128], [1, NH * LINEW]])
                pool.dma_start(d["skew"], every).then_inc(s_st, 16)
                pool.wait_ge(s_st, 32)
                src = bass.AP(tensor=d["skew"].tensor, offset=128,
                              ap=[[NH * LINEW - 1, 128], [LINEW, NH], [1, BANDW]])
                pool.dma_start(t["band"][:], src).then_inc(s_band, 16)

            @block.sync
            def _(sp):
                for a, b in ((pe_t, "cmp_pe"), (gk, "k_norm_cmp"), (ptab, "page_table")):
                    sp.dma_start(a[:], d[b]).then_inc(s_c, 16)
                sp.wait_ge(s_z, ONE + 2)
                for g in range(2):
                    for kv in range(2):
                        sp.dma_start(wc[64 * g:64 * g + 64, kv, :, 64 * g:64 * g + 64], d["w_cmp"][kv]).then_inc(s_w, 16)
                sp.wait_ge(s_c, ONE + 48)
                load_pages(sp, 0)
                sp.wait_ge(s_done[0], ONE + NCH // 2)
                for kv in range(2):
                    sp.dma_start(pg[0][:, 0:SEQ // PAGE, kv, :],
                                 d["kvT"][kv, :, 0:SEQ].rearrange("p (a n) -> p a n", n=PAGE)).then_inc(s_pr, 16)

            @block.scalar
            def _(act):
                act.wait_ge(s_c, ONE + 48)
                load_pages(act, 1)
                for i, (a, n) in enumerate(pieces):
                    if i:
                        act.wait_ge(s_kn, ONE + i)
                    else:
                        act.wait_ge(s_ev[0], ONE + NCH // 2 + 1)
                        act.wait_ge(s_ev[1], ONE + NCH // 2)
                    act.activation(sq[:, 0:n], kcT[:, a:a + n], ACT.Square).then_inc(s_sq, 1)
                    act.wait_ge(s_sum, ONE + i + 1)
                    act.activation(rt[:, 0:n], sps[:, 0:n], ACT.Sqrt, bias=t["eps"][:]).then_inc(s_rt, 1)

            @block.tensor
            def _(pe):
                pe.wait_ge(s_ri, 32)
                for i, (a, n) in enumerate(line_parts):
                    pe.matmul(lps[:, i, 0:n], relb[:], oneh[:, a:a + n], start=True, stop=True).then_inc(s_lm, 1)
                pe.wait_ge(s_w, ONE + 64)
                pe.wait_ge(s_c, ONE + 48)
                for kv in range(2):
                    for l in range(CB):
                        mm = pe.matmul(sps[:, kv:kv + 1], wc[:, kv, l], pe_t[:, kv, l:l + 1], start=(l == 0), stop=(l == CB - 1))
                mm.then_inc(s_cv, 1)

                def chunk(b, np_):
                    for kv in range(2):
                        for l in range(CB):
                            mm = pe.matmul(cps[b][:, 128 * kv:128 * kv + 4 * np_], wc[:, kv, l],
                                           pg[b][:, 0:np_, kv, l::CB], start=(l == 0), stop=(l == CB - 1))
                    mm.then_inc(s_done[b], 1)
                with pe.Fori(0, NCH // 2) as i:
                    for b in range(2):
                        pe.wait_ge(s_pg[b], ONE + 16 * NPG * (i + 1))
                        pe.wait_ge(s_ev[b], ONE + i)
                        chunk(b, NPG)
                pe.wait_ge(s_pr, ONE + 32)
                pe.wait_ge(s_ev[0], ONE + NCH // 2)
                chunk(0, SEQ // PAGE)
                for i, (a, n) in enumerate(pieces):
                    pe.wait_ge(s_sq, ONE + i + 1)
                    if i:
                        pe.wait_ge(s_rt, ONE + i)
                    else:
                        pe.wait_ge(s_cvd, ONE + 1)
                    pe.matmul(sps[:, 0:n], t["ones_hd"][:], sq[:, 0:n], start=True, stop=True).then_inc(s_sum, 1)
                for q in range(5):
                    if q:
                        pe.wait_ge(s_te, ONE + q)
                    if q < 4:
                        for j in range(4):
                            a = NCP + 512 * q + 128 * j
                            mm = pe.transpose(tps[:, j], vcT[:, a:a + 128], t["ident"][:])
                    else:
                        mm = pe.transpose(tps[0:NCP, 0], vcT[:, 0:NCP], t["ident"][:])
                    mm.then_inc(s_tr, 1)

            @block.vector
            def _(dve):
                for i, (a, n) in enumerate(line_parts):
                    dve.wait_ge(s_lm, i + 1)
                    dve.tensor_copy(line[:, a:a + n], lps[:, i, 0:n]).then_inc(s_line, 1)
                dve.wait_ge(s_cv, ONE + 1)
                dve.tensor_copy(cvec[:], sps[:, 0:2]).then_inc(s_cvd, 1)
                dve.wait_ge(s_cvd, ONE + 1)

                def copy(b, a, n):
                    dve.tensor_scalar(kcT[:, a], cps[b][:, 0:n], cvec[:, 0:1], None, ALU.add).then_inc(s_k0, 1)
                    dve.tensor_scalar(vcT[:, a], cps[b][:, 128:128 + n], cvec[:, 1:2], None, ALU.add).then_inc(s_ev[b], 1)
                with dve.Fori(0, NCH // 2) as i:
                    for b in range(2):
                        dve.wait_ge(s_done[b], ONE + i + 1)
                        copy(b, ds(i * 256 + (NCP + 128 * b), 128), 128)
                dve.wait_ge(s_band, 16)
                dve.wait_ge(s_cm, 16)
                for h in range(NH):
                    dve.scalar_tensor_tensor(t["band"][:, h, :], t["band"][:, h, :], HD ** 0.5, cmask[:], ALU.mult,
                                             ALU.add).then_inc(s_out, 1)
                dve.wait_ge(s_done[0], ONE + NCH // 2 + 1)
                copy(0, slice(0, NCP), NCP)
                dve.wait_ge(s_k0, ONE + NCH + 1)
                for i, (a, n) in enumerate(pieces):
                    dve.wait_ge(s_rt, ONE + i + 1)
                    dve.reciprocal(rt[:, 0:n], rt[:, 0:n]).then_inc(s_rc, 1)
                    dve.wait_ge(s_rc, ONE + i + 1)
                    dve.scalar_tensor_tensor(kcT[:, a:a + n], kcT[:, a:a + n], gk[:, 0:1], rt[:, 0:n], ALU.mult,
                                             ALU.mult).then_inc(s_kn, 1)
                    dve.wait_ge(s_kn, ONE + i + 1)
                for g in range(2):
                    r = slice(64 * g, 64 * g + 64)
                    o = slice(64 - 64 * g, 128 - 64 * g)
                    dve.tensor_copy(t["kcz"][r, g], kcT[r, 0:NCP])
                    dve.memset(t["kcz"][o, g], 0.0)
                for q in range(5):
                    dve.wait_ge(s_tr, ONE + q + 1)
                    if q < 4:
                        dve.tensor_copy(t["vcs"][:, 4 * q:4 * q + 4], tps[:]).then_inc(s_te, 1)
                    else:
                        dve.tensor_copy(t["vcp"][:], tps[0:NCP, 0]).then_inc(s_te, 1)


def prompt_keys(nc, d, t):
    with ExitStack() as ctx:
        sem = ctx.enter_context(semaphores(nc, "pk_"))
        vT = t["S_sel"]
        ps = [ctx.enter_context(nc.psum_tensor(f"ps_vt{b}", [128, 4, 128], F32)) for b in range(2)]
        s_wb = sem("window_band")
        s_v, s_k, s_t, s_e, s_m = (sem(n) for n in ("v_loaded", "k_loaded", "v_transposed", "v_copied", "cleared"))
        with nc.Block() as block:
            @block.sync
            def _(sp):
                for i, n in enumerate(("vs", "vw")):
                    sp.dma_start(vT[:, i], d["kvT"][KVROW[n], :, 0:SEQ]).then_inc(s_v, 16)
                for n in ("ks", "kw"):
                    for g in range(2):
                        r = slice(64 * g, 64 * g + 64)
                        sp.dma_start(t[n][r, g], d["kvT"][KVROW[n], r, 0:SEQ]).then_inc(s_k, 16)
                for n in ("tri", "score_band", "att_gain"):
                    sp.dma_start(t[n][:], d[n]).then_inc(s_k, 16)
                sp.wait_ge(s_k, 16 * 7)

            @block.gpsimd
            def _(pool):
                own = Own(pool)
                for n in ("ks", "kw"):
                    for g in range(2):
                        own(pool.memset(t[n][64 - 64 * g:128 - 64 * g, g], 0.0), s_m, 5)
                own(pool.memset(t["half"][:], -0.5), s_m, 5)

            @block.tensor
            def _(pe):
                pe.wait_ge(s_v, 32)
                for q in range(8):
                    if q >= 2:
                        pe.wait_ge(s_e, q - 1)
                    for j in range(4):
                        k = 4 * (q % 4) + j
                        mm = pe.transpose(ps[q % 2][:, j], vT[:, q // 4, 128 * k:128 * k + 128], t["ident"][:])
                    mm.then_inc(s_t, 1)

            @block.vector
            def _(dve):
                dve.memset(t["cband"][:, :, 0:56], 0.0)
                dve.memset(t["cband"][:, :, 64:124], NEG)
                dve.wait_ge(s_k, 16 * 7)
                for h in range(NH):
                    dve.tensor_copy(t["wband"][:, h], t["band"][:, h, 0:640]).then_inc(s_wb, 1)
                    dve.wait_ge(s_wb, 2 * h + 1)
                    dve.tensor_tensor(t["wband"][:, h, 0:128], t["wband"][:, h, 0:128], t["tri"][:], ALU.add).then_inc(s_wb, 1)
                    dve.wait_ge(s_wb, 2 * h + 2)
                dve.tensor_copy(t["cband"][:, :, 56:64], t["band"][:, :, 415:415 + 32 * 7 + 1:32])
                for q in range(8):
                    dve.wait_ge(s_t, q + 1)
                    dst = t["vs" if q < 4 else "vw"]
                    dve.tensor_copy(dst[:, 4 * (q % 4):4 * (q % 4) + 4], ps[q % 2][:]).then_inc(s_e, 1)


def prompt(nc, d, t, cl):
    nk = cl + 1
    SC = HD ** -0.5
    CMP, AHEAD = 4, 4
    FIRST = (0, 0)
    items = [("win", h) for h in range(NH)] + [("sel", h) for h in range(NH)]
    items.insert(CMP, ("cmp", 0))
    win_chunks = [(0, 512)] if cl == 0 else [(0, 512), (512, 128)]
    far = 512 * cl - 128
    sel_chunks = ([(a, min(512, far - a)) for a in range(0, far, 512)] + [(far, 128)] if cl else []) + [(512 * cl, 512)]

    def chunks(j):
        return {"cmp": [(0, 512)], "win": win_chunks, "sel": sel_chunks}[items[j][0]]

    def groups(j):
        return {"cmp": [4, 4], "win": [4] if cl == 0 else [4, 1], "sel": [4] * nk}[items[j][0]]
    NI = len(items)
    NCK = sum(len(chunks(j)) for j in range(NI))
    NG = sum(len(groups(j)) for j in range(NI))
    NX = NI - 1
    first_group = [sum(len(groups(x)) for x in range(j)) for j in range(NI + 1)]
    first_chunk = [sum(len(chunks(x)) for x in range(j)) for j in range(NI + 1)]
    group_item = [j for j in range(NI) for _ in groups(j)]
    SEL0 = 1 + NH
    BR = {"cmp": 0, "sel": 1, "win": 2}
    MIXED = [j for j in range(NI) if items[j][0] == "sel" or (items[j][0] == "win" and cl == 0)]
    NM = len(MIXED)
    plain = t["plain"]
    bc = lambda a, n: a.rearrange("p (h o) -> p h o", o=1).to_broadcast([128, a.shape[1], n])
    blocks = lambda z: z.rearrange("p (b k) -> p b k", k=64)

    def nth(j):
        return j - (j > CMP)

    def slot(j):
        kind, h = items[j]
        return h % 3 + (3 if kind == "sel" else 0)

    def at(tile, per, n):
        return tile[0] * per + (tile[1] * per + n + ONE)

    def reuse(x, ring, per):
        return x - ring + 1 if x >= ring else max(y for y in range(per) if y % ring == x % ring) + 1 - per

    def wait_tile(eng, sem, tile, per, n):
        if n > 0 or tile is not FIRST:
            eng.wait_ge(sem, at(tile, per, n if tile[1] else max(n, 0)))

    with ExitStack() as ctx:
        pb = lambda n, s: ctx.enter_context(nc.psum_tensor(n, s, F32))
        sem = ctx.enter_context(semaphores(nc, f"pr{cl}_"))
        sp_ = [pb(f"ps_s{i}_{cl}", [128, 512]) for i in range(3)]
        tp_ = [pb(f"ps_p{i}_{cl}", [128, 4, 128]) for i in range(2)]
        O = [pb(f"ps_o{i}_{cl}", [128, NH, HD]) for i in range(3)]
        PT, g_, gn = t["PT"], t["g_tiles"], t["gates_tok"]
        q_ = {"near": t["q_near"], "sel": t["q_sel"]}
        mixT = O[1][:].rearrange("p h n -> p (h n)")
        s_in, s_gt, s_ge, s_qk, s_ev, s_mx, s_exp, s_tp, s_pte, s_pv = (sem(n) for n in (
            "gates_loaded", "gates_transposed", "gates_copied", "scores_done", "scores_copied", "max_ready", "probs_ready",
            "probs_transposed", "transposed_copied", "values_done"))
        s_cs, s_cx, s_cp, s_mk, s_mb, s_dv = (sem(n) for n in (
            "cmp_shifted", "cmp_exp_done", "cmp_probs_ready", "mask_ready", "bias_mixed", "dve_steps"))
        s_cw, s_cr, s_cf, s_vr, s_pw, s_on, s_mt, s_mc, s_mo = (sem(n) for n in (
            "win_sums_used", "win_cmp_outputs_read", "sel_sums_used", "variance_ready", "rstd_ready", "mix_normed",
            "mix_transposed", "mix_copied", "mix_sent"))
        s_q = {k: sem(f"q_{k}_loaded") for k in ("near", "sel")}
        sem.start_at_one()

        def buf(j, a, n):
            if items[j][0] == "cmp":
                return t["S_cmp"][:, a:a + n]
            return t["S_win" if items[j][0] == "win" else "S_sel"][:, slot(j) % 3, a:a + n]

        with nc.Block() as block:
            @block.sync
            def _(sp):
                def load(kind, tile):
                    col = tile[0] * 128 + (128 * tile[1] + 512 * cl)
                    sp.dma_start(q_[kind][:], d["qT"][:, :, ds(col, 128)].rearrange("r p n -> p r n")).then_inc(s_q[kind], 16)

                def send(tile):
                    sp.wait_ge(s_mc, at(tile, 1, 1))
                    plain(sp)
                    col = tile[0] * 128 + 512 * cl
                    sp.dma_start(d["mixT"][0:4, :, ds(col, 128)].rearrange("r p n -> p r n"), t["mix_tile"][:]).then_inc(s_mo, 16)
                load("near", FIRST)
                sp.dma_start(g_[:], d["gT"][:, 512 * cl:512 * cl + 512]).then_inc(s_in, 16)
                load("sel", FIRST)
                with sp.Fori(0, 3) as i:
                    for kind, used in (("near", SEL0), ("sel", NI)):
                        sp.wait_ge(s_qk, at((i, 0), NCK, first_chunk[used]))
                        plain(sp)
                        load(kind, (i, 1))
                    send((i, 0))
                send((3, 0))
                sp.wait_ge(s_mo, ONE + 64)

            @block.tensor
            def _(pe):
                def scores(j, tile):
                    kind, h = items[j]
                    g, r = h // 4, h % 4
                    q = lambda r: q_["sel" if kind == "sel" else "near"][:, r]
                    if j == 0:
                        pe.wait_ge(s_q["near"], at(tile, 16, 16))
                    if j == SEL0:
                        pe.wait_ge(s_q["sel"], at(tile, 16, 16))
                    for ci, (a, n) in enumerate(chunks(j)):
                        k = first_chunk[j] + ci
                        wait_tile(pe, s_ev, tile, NCK, reuse(k, 3, NCK))
                        plain(pe)
                        if kind == "cmp":
                            for hh in range(NH):
                                mm = pe.matmul(sp_[k % 3][:, 64 * hh:64 * hh + 64], q(hh % 4), t["kcz"][:, hh // 4],
                                               start=True, stop=True)
                        elif kind == "win" and cl:
                            keys = t["kw"][:, g, ds(tile[0] * 128 + (128 * tile[1] + 512 * cl - 512 + a), n)]
                            mm = pe.matmul(sp_[k % 3][:, 0:n], q(r), keys, start=True, stop=True)
                        else:
                            keys = t["ks" if kind == "sel" else "kw"][:, g, a:a + n]
                            mm = pe.matmul(sp_[k % 3][:, 0:n], q(r), keys, start=True, stop=True)
                        mm.then_inc(s_qk, 1)

                def turn(q, tile):
                    j = group_item[q]
                    gi = q - first_group[j]
                    if gi == 0 and j == CMP:
                        pe.wait_ge(s_cp, at(tile, 1, 1))
                    elif gi == 0:
                        pe.wait_ge(s_exp, at(tile, NX, nth(j) + 1))
                    wait_tile(pe, s_pte, tile, NG, reuse(q, 2, NG))
                    plain(pe)
                    for y in range(groups(j)[gi]):
                        if j == CMP:
                            mm = pe.transpose(tp_[q % 2][0:64, y], buf(j, 256 * gi + 64 * y, 64), t["ident"][:])
                        else:
                            mm = pe.transpose(tp_[q % 2][:, y], buf(j, 512 * gi + 128 * y, 128), t["ident"][:])
                    mm.then_inc(s_tp, 1)

                def values(q, tile):
                    j = group_item[q]
                    kind, h = items[j]
                    gi, g, n = q - first_group[j], h // 4, len(groups(j))
                    pe.wait_ge(s_pte, at(tile, NG, q + 1))
                    if q == 0:
                        wait_tile(pe, s_cr, tile, 1, 0)
                    if q == first_group[SEL0]:
                        wait_tile(pe, s_mc, tile, 1, 0)
                    plain(pe)
                    for y in range(groups(j)[gi]):
                        if kind == "cmp":
                            hh = 4 * gi + y
                            mm = pe.matmul(O[0][:, hh], PT[0:64, q % 4, y], t["vcp"][:, 64 * gi:64 * gi + 64],
                                           start=True, stop=True)
                            continue
                        if kind == "win" and cl:
                            v = t["vw"][:, ds(tile[0] + (tile[1] + 4 * cl - 4 + 4 * gi + y), 1),
                                        64 * g:64 * g + 64].rearrange("p a n -> p (a n)")
                        else:
                            v = t["vs" if kind == "sel" else "vw"][:, 4 * gi + y, 64 * g:64 * g + 64]
                        mm = pe.matmul(O[BR[kind]][:, h], PT[:, q % 4, y], v, start=(gi == 0 and y == 0),
                                       stop=(gi == n - 1 and y == groups(j)[gi] - 1))
                    mm.then_inc(s_pv, 1)

                def item(j, tile, before, after):
                    if j + 2 < NI:
                        scores(j + 2, tile)
                    elif after:
                        scores(j + 2 - NI, after)
                    for q in range(first_group[j], first_group[j + 1]):
                        turn(q, tile)
                        if q >= 2:
                            values(q - 2, tile)
                        elif before:
                            values(NG + q - 2, before)

                def mix(tile):
                    pe.wait_ge(s_on, at(tile, 1, 1))
                    plain(pe)
                    for y in range(4):
                        mm = pe.transpose(mixT[:, 128 * y:128 * y + 128], t["o_att"][:, 128 * y:128 * y + 128], t["ident"][:])
                    mm.then_inc(s_mt, 1)

                pe.wait_ge(s_in, ONE + 16)
                for k in range(4):
                    mm = pe.transpose(tp_[0][:, k, 0:24], g_[:, 128 * k:128 * k + 128], t["ident"][0:24, 0:24])
                mm.then_inc(s_gt, 1)
                first = FIRST
                scores(0, first)
                scores(1, first)
                pe.wait_ge(s_ge, ONE + 1)
                for j in range(AHEAD):
                    item(j, first, None, None)
                with pe.Fori(0, 3) as i:
                    this, after = (i, 0), (i, 1)
                    for j in range(AHEAD, NI):
                        item(j, this, None, after)
                    for j in range(AHEAD):
                        item(j, after, this, None)
                    mix(this)
                last = (3, 0)
                for j in range(AHEAD, NI):
                    item(j, last, None, None)
                values(NG - 2, last)
                values(NG - 1, last)
                mix(last)

            @block.scalar
            def _(act):
                def exp(j, tile):
                    if j == CMP:
                        act.wait_ge(s_cs, at(tile, 1, 1))
                        act.activation(t["S_cmp"][:], t["S_cmp"][:], ACT.Exp, scale=SC).then_inc(s_cx, 1)
                        return
                    n = sum(c[1] for c in chunks(j))
                    if j == 0:
                        wait_tile(act, s_cw, tile, 1, 0)
                    if j == SEL0:
                        wait_tile(act, s_cf, tile, 1, 0)
                    act.wait_ge(s_mx, at(tile, NX, nth(j) + 1))
                    act.activation(buf(j, 0, n), buf(j, 0, n), ACT.Exp, bias=t["nmax"][:, slot(j):slot(j) + 1],
                                   accum_out=t["rsum"][:, nth(j):nth(j) + 1]).then_inc(s_exp, 1)

                def copies(j, tile):
                    rows = 64 if j == CMP else 128
                    for gi, n in enumerate(groups(j)):
                        q = first_group[j] + gi
                        act.wait_ge(s_tp, at(tile, NG, q + 1))
                        wait_tile(act, s_pv, tile, NG, reuse(q, 4, NG))
                        act.activation(PT[0:rows, q % 4, 0:n], tp_[q % 2][0:rows, 0:n], ACT.Copy).then_inc(s_pte, 1)

                def item(j, tile, after):
                    if j + 1 < NI:
                        exp(j + 1, tile)
                    elif after:
                        exp(0, after)
                    copies(j, tile)

                def mix(tile):
                    act.wait_ge(s_mt, at(tile, 1, 1))
                    act.wait_ge(s_mo, at(tile, 16, 0))
                    for y in range(4):
                        ins = act.activation(t["mix_tile"][:, y], mixT[:, 128 * y:128 * y + 128], ACT.Copy,
                                             scale=t["att_gain"][:, y:y + 1])
                    ins.then_inc(s_mc, 1)

                act.wait_ge(s_gt, ONE + 1)
                act.activation(gn[:], tp_[0][:, :, 0:24], ACT.Copy).then_inc(s_ge, 1)
                exp(0, FIRST)
                for j in range(AHEAD):
                    item(j, FIRST, None)
                with act.Fori(0, 3) as i:
                    for j in range(AHEAD, NI):
                        item(j, (i, 0), (i, 1))
                    for j in range(AHEAD):
                        item(j, (i, 1), None)
                    mix((i, 0))
                for j in range(AHEAD, NI):
                    item(j, (3, 0), None)
                mix((3, 0))

            @block.gpsimd
            def _(pool):
                own = Own(pool, ONE)

                def mix_bias(j, tile):
                    m = MIXED.index(j)
                    kind, h = items[j]
                    used = reuse(m, 3, NM)
                    wait_tile(pool, s_ev, tile, NCK, first_chunk[MIXED[used - 1] + 1] if used > 0 else
                              first_chunk[MIXED[NM + used - 1] + 1] - NCK)
                    plain(pool)
                    q0 = lambda n, c: ds(tile[0] * -128 + (c - 128 * tile[1]), n)
                    if kind == "win":
                        own(pool.tensor_copy(t["mix_bias"][:, m % 3, 128:640], t["band"][:, h, q0(512, 512)]), s_mb, NM)
                        return
                    pool.wait_ge(s_mk, at(tile, 1, 1))
                    plain(pool)
                    lo = 128 if cl == 0 else 0
                    own(pool.tensor_tensor(blocks(t["mix_bias"][:, m % 3, lo:640]),
                                           blocks(t["band"][:, h, q0(640 - lo, 384 + lo)]),
                                           bc(t["mask"][:, h // 4, 8 * cl - 2 + lo // 64:8 * cl + 8], 64), ALU.add), s_mb, NM)

                def power(tile):
                    pool.wait_ge(s_vr, at(tile, 1, 1))
                    own(pool.tensor_tensor(t["rstd"][:], t["var"][:], t["half"][:], ALU.pow), s_pw, 1)

                def items_of(lo, hi, tile):
                    for j in range(lo, hi):
                        if j in MIXED:
                            mix_bias(j, tile)

                items_of(0, AHEAD, FIRST)
                with pool.Fori(0, 3) as i:
                    own.iteration(i)
                    items_of(AHEAD, NI, (i, 0))
                    items_of(0, 2, (i, 1))
                    power((i, 0))
                    items_of(2, AHEAD, (i, 1))
                own.iteration(3)
                items_of(AHEAD, NI, (3, 0))
                power((3, 0))

            @block.vector
            def _(dve):
                own = Own(dve, ONE)
                step = lambda ins: own(ins, s_dv, 20)
                ahead = lambda ins: own.post(ins, s_dv, 20)
                settle = lambda: own.settle(s_dv, 20)
                imp, m8, r8 = t["imp"], t["cmax"], t["csum"]
                p = t["S_cmp"][:].rearrange("p (h n) -> p h n", n=64)
                rs, cf, o, o2 = t["rsum"], t["coef"], t["o_att"], t["o_tmp"]
                hv = lambda a: a.rearrange("p (h n) -> p h n", n=64)

                def fetch(j, tile):
                    kind, h = items[j]
                    g, b = h // 4, slot(j)
                    used = reuse(h, 3, NH)
                    base = 0 if kind == "win" else SEL0
                    item_at = lambda h: h + (kind == "win" and h >= CMP) + base
                    wait_tile(dve, s_tp, tile, NG, first_group[item_at(used - 1) + 1] if used > 0 else
                              first_group[item_at(NH + used - 1) + 1] - NG)
                    if j in MIXED:
                        m = MIXED.index(j)
                        dve.wait_ge(s_mb, at(tile, NM, m + 1))
                    for ci, (a, w) in enumerate(chunks(j)):
                        k = first_chunk[j] + ci
                        dve.wait_ge(s_qk, at(tile, NCK, k + 1))
                        src, dst = sp_[k % 3][:, 0:w], buf(j, a, w)
                        if kind == "win" and cl:
                            add = t["wband"][:, h, a:a + w]
                        elif j in MIXED and a >= far:
                            add = t["mix_bias"][:, m % 3, a - far:a - far + w]
                        else:
                            src, dst, add = blocks(src), blocks(dst), bc(t["mask"][:, g, a // 64:(a + w) // 64], 64)
                        plain(dve)
                        own.post(dve.tensor_tensor_reduce(dst, src, add, SC, -3e38, ALU.add, ALU.max,
                                                            t["chunk_max"][:, b, ci:ci + 1]), s_ev, NCK)
                    own.settle(s_ev, NCK)
                    own.post(dve.tensor_reduce(t["nmax"][:, b:b + 1], t["chunk_max"][:, b, 0:len(chunks(j))], X, ALU.max, negate=True),
                        s_mx, NX)

                def cmp_shift(tile):
                    dve.wait_ge(s_qk, at(tile, NCK, first_chunk[CMP] + 1))
                    wait_tile(dve, s_tp, tile, NG, first_group[CMP + 1] - NG)
                    cb = t["cband"][:, :, ds(tile[0] * -4 + (60 - 16 * cl - 4 * tile[1]), 64)]
                    own(dve.tensor_tensor(p, sp_[first_chunk[CMP] % 3][:].rearrange("p (h n) -> p h n", n=64), cb, ALU.add),
                        s_ev, NCK)
                    step(dve.tensor_reduce(m8[:], p, X, ALU.max))
                    step(dve.tensor_scalar(m8[:], m8[:], -1e20, None, ALU.max))
                    own(dve.tensor_tensor(p, p, bc(m8[:], 64), ALU.subtract), s_cs, 1)

                def cmp_probs(tile):
                    dve.wait_ge(s_cx, at(tile, 1, 1))
                    step(dve.tensor_reduce(r8[:], p, X, ALU.add))
                    step(dve.tensor_scalar(r8[:], r8[:], 1e-30, None, ALU.max))
                    step(dve.reciprocal(r8[:], r8[:]))
                    own(dve.tensor_tensor(p, p, bc(r8[:], 64), ALU.mult), s_cp, 1)
                    for g in range(2):
                        pv = t["S_cmp"][:, 256 * g:256 * g + 256].rearrange("p (r j w) -> p j r w", r=4, w=2)
                        ahead(dve.tensor_reduce(imp[:, g], pv, XY, ALU.add))
                    settle()

                def choose(tile):
                    sbw = t["score_band"][:, ds(tile[0] * -2 + (30 - 8 * cl - 2 * tile[1]), 32)]
                    for g in range(2):
                        ahead(dve.tensor_tensor(imp[:, g], imp[:, g], sbw, ALU.add))
                    settle()
                    step(dve.tensor_scalar(imp[:, :, 0], imp[:, :, 0], 1e4, None, ALU.max))
                    for g in range(2):
                        plain(dve)
                        ahead(dve.max(t["top"][:, g], imp[:, g]))
                    settle()
                    for g in range(2):
                        plain(dve)
                        ahead(dve.match_replace(t["mask"][:, g], t["top"][:, g], imp[:, g], -2e30))
                    settle()
                    own(dve.tensor_scalar(t["mask"][:], t["mask"][:], -1.5e30, NEG, ALU.is_gt, ALU.mult), s_mk, 1)

                def coefficients(tile, c, gate, s):
                    step(dve.reciprocal(cf[:, c:c + 8], rs[:, c:c + 8]))
                    own(dve.tensor_tensor(cf[:, c:c + 8], cf[:, c:c + 8], gates(tile, gate), ALU.mult), s, 1)

                def gates(tile, gate):
                    return gn[:, ds(tile[0] + tile[1], 1), gate:gate + 8].rearrange("p a n -> p (a n)")

                def near_outputs(tile):
                    dve.wait_ge(s_exp, at(tile, NX, NH))
                    coefficients(tile, 0, 16, s_cw)
                    dve.wait_ge(s_pv, at(tile, NG, first_group[SEL0]))
                    dve.wait_ge(s_mt, at(tile, 1, 0))
                    step(dve.tensor_tensor(hv(o[:]), O[0][:], bc(gates(tile, 0), 64), ALU.mult))
                    own(dve.tensor_tensor(hv(o2[:]), O[2][:], bc(cf[:, 0:8], 64), ALU.mult), s_cr, 1)
                    step(dve.tensor_tensor(o[:], o[:], o2[:], ALU.add))

                def sel_outputs(tile):
                    dve.wait_ge(s_exp, at(tile, NX, NX))
                    coefficients(tile, 8, 8, s_cf)
                    dve.wait_ge(s_pv, at(tile, NG, NG))
                    step(dve.tensor_tensor(hv(o2[:]), O[1][:], bc(cf[:, 8:16], 64), ALU.mult))
                    step(dve.tensor_tensor(o[:], o[:], o2[:], ALU.add))
                    own(dve.tensor_tensor_reduce(o2[:], o[:], o[:], 1 / 512, EPS, ALU.mult, ALU.add, t["var"][:]), s_vr, 1)

                def norm(tile):
                    dve.wait_ge(s_pw, at(tile, 1, 1))
                    own(dve.tensor_scalar(o[:], o[:], t["rstd"][:, 0:1], None, ALU.mult), s_on, 1)

                def rest(tile):
                    cmp_shift(tile)
                    fetch(CMP + 1, tile)
                    cmp_probs(tile)
                    fetch(CMP + 2, tile)
                    choose(tile)
                    for j in range(CMP + 3, NI):
                        fetch(j, tile)
                        if j == SEL0 + 2:
                            near_outputs(tile)

                dve.wait_ge(s_ge, ONE + 1)
                for j in range(AHEAD):
                    fetch(j, FIRST)
                with dve.Fori(0, 3) as i:
                    own.iteration(i)
                    rest((i, 0))
                    fetch(0, (i, 1))
                    fetch(1, (i, 1))
                    sel_outputs((i, 0))
                    fetch(2, (i, 1))
                    norm((i, 0))
                    fetch(3, (i, 1))
                own.iteration(3)
                rest((3, 0))
                sel_outputs((3, 0))
                norm((3, 0))


def sample(nc, d, t):
    ROWS = NB * NH
    with ExitStack() as ctx:
        sb = lambda n, s, dt=F32: ctx.enter_context(nc.sbuf_tensor(n, s, dt))
        pb = lambda n, s: ctx.enter_context(nc.psum_tensor(n, s, F32))
        sem = ctx.enter_context(semaphores(nc, "sm_"))
        wk, wv = sb("win_k", [128, NB, 512]), sb("win_v", [128, NB, 4, 128])
        kv = sb("sel_kv", [64, NB, 2, 2, 8, 64])
        ksn = sb("new_ks", [64, 2, NB])
        kwn = sb("new_kw", [128, NB])
        qz, qs = sb("q_padded", [128, NH, NB]), sb("q_groups", [64, 2, 4, NB])
        gr = sb("gate_rows", [ROWS, 3])
        bias = {"cmp": sb("bias_cmp", [ROWS, 256]), "win": sb("bias_win", [ROWS, 512]), "sel": sb("bias_sel", [ROWS, 512])}
        near = sb("bias_near", [ROWS, 64])
        pti, pb2 = sb("pages_int", [ROWS, NPAGE], I32), sb("phys_block", [ROWS, NPAGE, 2])
        iota, own4, own8 = sb("iota", [ROWS, 128]), sb("same_group", [ROWS, ROWS]), sb("same_token", [ROWS, ROWS])
        side = sb("group_rows", [ROWS, 2])
        gain = sb("gain_rows", [ROWS, HD])
        sT, R = sb("scores_T", [128, 4, ROWS]), {k: sb("rows_" + k, [ROWS, n]) for k, n in (("cmp", 256), ("win", 512), ("sel", 512))}
        pT = {k: sb("probs_T_" + k, [128, n, ROWS]) for k, n in (("cmp", 2), ("win", 4))}
        pT["sel"] = sb("probs_T_sel", [64, 8, ROWS])
        imp, junk = sb("importance", [ROWS, 128]), sb("picked", [ROWS, 128])
        top, idx, idf, ind = sb("top", [ROWS, 8]), sb("top_index", [ROWS, 8], U32), sb("top_float", [ROWS, 8]), sb("is_last", [ROWS, 8])
        ph, phi, prow = sb("phys", [ROWS, 7]), sb("phys_int", [ROWS, 7], I32), sb("phys_row", [1, ROWS * 7], I32)
        mx, rsm = sb("row_max", [ROWS, 3]), sb("row_sum", [ROWS, 3])
        aw, dd, o = sb("out_cmp_win", [128, ROWS]), sb("out_sel", [64, ROWS]), sb("o_rows", [ROWS, HD])
        o2, ss, sd = sb("o_scratch", [ROWS, HD]), sb("o_sumsq", [ROWS, 1]), sb("o_std", [ROWS, 1])
        om = sb("o_heads", [HD, NH, NB])
        psS, psR, psP = pb("ps_sT", [128, 4, ROWS]), pb("ps_rows", [ROWS, 4, 128]), pb("ps_pT", [128, 8, ROWS])
        psI, psA, psD, psX = pb("ps_imp", [ROWS, 128]), pb("ps_aw", [128, ROWS]), pb("ps_sel_o", [64, ROWS]), pb("ps_turn", [64, 256])
        s_z, s_c, s_n, s_wo, s_ph, s_pr, s_sel, s_mm, s_dv, s_ac, s_mo = (sem(n) for n in (
            "cleared", "inputs_loaded", "new_token_placed", "window_out", "phys_stored", "phys_loaded", "selected_loaded",
            "pe_steps", "dve_steps", "act_steps", "mix_sent"))
        s_wl = sem("window_loaded")
        col = slice(SEQ, NTOK)
        PE = ["sT_cmp", "R_cmp", "imp", "pT_cmp", "sT_win", "R_win", "pT_win", "sT_sel", "R_sel", "pT_sel", "aw", "sel_o",
              "turn", "token_sum", "heads"]
        pe_at = {n: i + 1 for i, n in enumerate(PE)}
        DV = ["sc_cmp", "s_cmp", "nm_cmp", "rec_cmp", "p_cmp", "pair_sum", "imp", "top", "index", "float", "plus_one", "pages_f", "even", "odd",
              "pick0", "pick1", "pick2", "pick3", "pick4", "ph1", "ph2", "phys_int", "gated_cmp", "c_pT_cmp",
              "new_kw", "new_ks", "sc_win", "s_win", "nm_win", "rec_win", "p_win", "c_pT_win",
              "is_last", "b3", "b4", "b5", "b6", "b7", "sc_sel", "s_sel", "nm_sel", "rec_sel", "p_sel", "c_pT_sel",
              "c_aw", "c_dd", "o_a", "o_b", "o_c", "o_sq", "o_ss", "std_r", "o_n", "o_g", "c_heads"]
        dv_at = {n: i + 1 for i, n in enumerate(DV)}
        n_in = 2 + 5 + 5 + 3 + 4 + 4 + 1
        n_new, n_win = 3 * NB, 1 + 4

        def load_selected(eng, g):
            with eng.Fori(0, NB) as b:
                phys = [eng.value_load(prow[0:1, ds(b * 56 + (28 * g + s), 1)], min_val=0, max_val=d["sel_kv"].shape[0] - 1)
                        for s in range(7)]
                for s, v in enumerate(phys):
                    eng.dma_start(kv[:, ds(b, 1), g, :, s + 1].rearrange("p a k n -> p (a k) n"),
                                  d["sel_kv"][ds(v, 1), g].rearrange("a p k n -> (a p) k n")).then_inc(s_sel, 16)

        with nc.Block() as block:
            @block.gpsimd
            def _(pool):
                own = Own(pool)
                for a, v in ((qz[:], 0.0), (kv[:, :, :, 0, 0], 0.0), (kv[:, :, :, 1, 0], 0.0), (bias["cmp"][:], 0.0),
                             (bias["sel"][:, 0:64], NEG), (bias["sel"][:, 64:128], 0.0)):
                    own(pool.memset(a, v), s_z, 6)

            @block.sync
            def _(sp):
                ld = lambda a, b: sp.dma_start(a, b).then_inc(s_c, 16)
                sp.wait_ge(s_z, 6)
                for g in range(2):
                    r = slice(64 * g, 64 * g + 64)
                    ld(qz[r, 4 * g:4 * g + 4], d["qT"][:, r, col].rearrange("r p n -> p r n"))
                heads = lambda a, n: bass.AP(tensor=d["line"].tensor, offset=a, ap=[[0, NB], [LINEW, NH], n])
                ld(bias["win"][:], heads(129, [1, 512]))
                ld(bias["sel"][:, 128:192], heads(576, [1, 64]))
                ld(near[:], heads(512, [1, 64]))
                ld(pti[:], bass.AP(tensor=d["page_table"].tensor, offset=0, ap=[[NPAGE, NB], [0, NH], [1, NPAGE]]))
                ld(gain[:], bass.AP(tensor=d["out_gain"].tensor, offset=0, ap=[[0, NB], [HD, NH], [1, HD]]))
                with nc.allow_non_contiguous_dma(reason="a few values per row"):
                    for m in range(4):
                        ld(bias["cmp"][:, 252 + m:253 + m], heads(543 + 32 * m, [1, 1]))
                    ld(bias["sel"][:, 0:1], heads(640, [1, 1]))
                    for k in range(3):
                        ld(gr[:, k:k + 1], bass.AP(tensor=d["gT"].tensor, offset=NH * k * NTOK + SEQ, ap=[[1, NB], [NTOK, NH], [1, 1]]))
                for a, n in ((own4, "same_group"), (iota, "iota"), (own8, "same_token"), (side, "group_rows")):
                    ld(a[:], d[n])
                for g in range(2):
                    r = slice(64 * g, 64 * g + 64)
                    ld(qs[:, g], d["qT"][:, r, col].rearrange("r p n -> p r n"))
                    ld(ksn[:, g], d["kvT"][KVROW["ks"], 64 * g:64 * g + 64, col])
                ld(kwn[:], d["kvT"][KVROW["kw"], :, col])
                with nc.allow_non_contiguous_dma(reason="the new tokens' values"):
                    for b in range(NB):
                        new = lambda n, a, w: d["kvT"][KVROW[n], a:a + w, SEQ + b:SEQ + b + 1].rearrange("p n -> n p")
                        sp.dma_start(wv[127:128, b, 3], new("vw", 0, 128)).then_inc(s_n, 16)
                        for g in range(2):
                            sp.dma_start(kv[0:1, b, g, 1, 0], new("vs", 64 * g, 64)).then_inc(s_n, 16)
                sp.dma_start(d["conv_prev"], d["state_conv"][:, :, 1]).then_inc(s_wo, 16)
                sp.wait_ge(s_dv, dv_at["phys_int"])
                sp.dma_start(d["phys"], phi[:]).then_inc(s_ph, 16)
                sp.wait_ge(s_ph, 16)
                sp.dma_start(prow[:], d["phys"].rearrange("r s -> (r s)").rearrange("(o n) -> o n", o=1)).then_inc(s_pr, 16)
                sp.wait_ge(s_pr, 16)
                load_selected(sp, 0)
                sp.wait_ge(s_dv, dv_at["new_kw"])
                sp.wait_ge(s_wl, 16 * n_win)
                sp.wait_ge(s_n, 16 * n_new)
                sp.dma_start(d["win_k_out"].rearrange("b p n -> p b n"), wk[:]).then_inc(s_wo, 16)
                sp.dma_start(d["win_v_out"].rearrange("b (t p) n -> p b t n", p=128), wv[:]).then_inc(s_wo, 16)
                sp.wait_ge(s_dv, dv_at["c_heads"])
                dst = d["mixT"][0:4].rearrange("j (a d) n -> d (j a) n", a=2)[:, :, col]
                sp.dma_start(dst, om[:]).then_inc(s_mo, 16)
                sp.wait_ge(s_mo, 16)
                sp.wait_ge(s_wo, 48)

            @block.tensor
            def _(pe):
                def done(mm):
                    mm.then_inc(s_mm, 1)

                def rows(k, n):
                    for y in range(n):
                        mm = pe.transpose(psR[:, y], sT[:, y], t["ident"][:])
                    done(mm)

                def probs(k, n, w=128):
                    for y in range(n):
                        mm = pe.transpose(psP[0:w, y], R[k][:, w * y:w * y + w], t["ident"][0:ROWS, 0:ROWS])
                    done(mm)
                pe.wait_ge(s_c, 16 * n_in)
                for b in range(NB):
                    for y in range(2):
                        a = NCP + 256 * b + 128 * y
                        mm = pe.matmul(psS[:, y, NH * b:NH * b + NH], t["kcT"][:, a:a + 128], qz[:, :, b], start=True, stop=True)
                done(mm)
                pe.wait_ge(s_dv, dv_at["sc_cmp"])
                rows("cmp", 2)
                pe.wait_ge(s_dv, dv_at["pair_sum"])
                done(pe.matmul(psI[:], own4[:], junk[:], start=True, stop=True))
                pe.wait_ge(s_dv, dv_at["gated_cmp"])
                probs("cmp", 2)
                pe.wait_ge(s_dv, dv_at["new_kw"])
                for b in range(NB):
                    for y in range(4):
                        mm = pe.matmul(psS[:, y, NH * b:NH * b + NH], wk[:, b, 128 * y:128 * y + 128], qz[:, :, b],
                                       start=True, stop=True)
                done(mm)
                pe.wait_ge(s_dv, dv_at["sc_win"])
                rows("win", 4)
                pe.wait_ge(s_dv, dv_at["p_win"])
                probs("win", 4)
                pe.wait_ge(s_sel, 16 * 2 * 7 * NB)
                pe.wait_ge(s_n, 16 * n_new)
                for b in range(NB):
                    for g in range(2):
                        for y in range(4):
                            a = NH * b + 4 * g
                            mm = pe.matmul(psS[:, y, a:a + 4], kv[:, b, g, 0, 2 * y:2 * y + 2].rearrange("p s n -> p (s n)"),
                                           qs[:, g, :, b], start=True, stop=True)
                done(mm)
                pe.wait_ge(s_dv, dv_at["sc_sel"])
                rows("sel", 4)
                pe.wait_ge(s_dv, dv_at["p_sel"])
                probs("sel", 8, 64)
                pe.wait_ge(s_dv, dv_at["c_pT_sel"])
                for b in range(NB):
                    a = NH * b
                    for y in range(2):
                        pe.matmul(psA[:, a:a + NH], t["vcs"][:, 2 * b + y], pT["cmp"][:, y, a:a + NH], start=(y == 0), stop=False)
                    for y in range(4):
                        mm = pe.matmul(psA[:, a:a + NH], wv[:, b, y], pT["win"][:, y, a:a + NH], start=False, stop=(y == 3))
                done(mm)
                for b in range(NB):
                    for g in range(2):
                        a = NH * b + 4 * g
                        for y in range(8):
                            mm = pe.matmul(psD[:, a:a + 4], kv[:, b, g, 1, y], pT["sel"][:, y, a:a + 4], start=(y == 0), stop=(y == 7))
                done(mm)
                pe.wait_ge(s_dv, dv_at["c_dd"])
                pe.transpose(psX[:, 0:128], aw[:], t["ident"][:])
                done(pe.transpose(psX[:, 128:192], dd[:], t["ident"][0:64, 0:64]))
                pe.wait_ge(s_dv, dv_at["o_ss"])
                done(pe.matmul(psI[:, 0:1], own8[:], ss[:], start=True, stop=True))
                pe.wait_ge(s_dv, dv_at["o_g"])
                done(pe.transpose(psX[:, 192:256], o[:], t["ident"][0:64, 0:64]))

            @block.scalar
            def _(act):
                def exp(k, i):
                    act.wait_ge(s_dv, dv_at["nm_" + k])
                    act.activation(R[k][:], R[k][:], ACT.Exp, bias=mx[:, i:i + 1], accum_out=rsm[:, i:i + 1]).then_inc(s_ac, 1)
                act.dma_start(wk[:, :, 0:511], d["win_k"][:, :, 1:512].rearrange("b p n -> p b n")).then_inc(s_wl, 16)
                for y in range(4):
                    n = 127 if y == 3 else 128
                    act.dma_start(wv[0:n, :, y], d["win_v"][:, 128 * y + 1:128 * y + 1 + n].rearrange("b p n -> p b n")).then_inc(s_wl, 16)
                exp("cmp", 0)
                act.wait_ge(s_pr, 16)
                load_selected(act, 1)
                exp("win", 1)
                exp("sel", 2)
                act.wait_ge(s_mm, pe_at["token_sum"])
                act.activation(sd[:], psI[:, 0:1], ACT.Sqrt, bias=t["eps"][0:ROWS]).then_inc(s_ac, 1)

            @block.vector
            def _(dve):
                n = [0]

                def step(name, ins):
                    assert DV[n[0]] == name, (DV[n[0]], name)
                    n[0] += 1
                    ins.then_inc(s_dv, 1)
                    dve.wait_ge(s_dv, n[0])
                SC = HD ** -0.5

                def scores(k, tiles):
                    dve.wait_ge(s_mm, pe_at["sT_" + k])
                    step("sc_" + k, dve.tensor_copy(sT[:, 0:tiles], psS[:, 0:tiles]))
                    dve.wait_ge(s_mm, pe_at["R_" + k])
                    src = psR[:, 0:tiles].rearrange("p a b -> p (a b)")
                    step("s_" + k, dve.scalar_tensor_tensor(R[k][:], src, SC, bias[k][:], ALU.mult, ALU.add))
                    i = "cmp win sel".split().index(k)
                    step("nm_" + k, dve.tensor_reduce(mx[:, i:i + 1], R[k][:], X, ALU.max, negate=True))
                    dve.wait_ge(s_ac, i + 1)

                dve.wait_ge(s_c, 16 * n_in)
                scores("cmp", 2)
                p = R["cmp"]
                step("rec_cmp", dve.reciprocal(rsm[:, 0:1], rsm[:, 0:1]))
                step("p_cmp", dve.tensor_scalar(p[:], p[:], rsm[:, 0:1], None, ALU.mult))
                pv = p[:].rearrange("p (j w) -> p j w", w=2)
                step("pair_sum", dve.scalar_tensor_tensor(junk[:], pv[:, :, 0], 1.0, pv[:, :, 1], ALU.mult, ALU.add))
                dve.wait_ge(s_mm, pe_at["imp"])
                step("imp", dve.tensor_copy(imp[:], psI[:]))
                step("top", dve.max(top[:], imp[:, 1:127]))
                step("index", dve.max_index(idx[:], top[:], imp[:, 1:127]))
                step("float", dve.tensor_copy(idf[:], idx[:]))
                step("plus_one", dve.tensor_scalar(idf[:], idf[:], 1.0, None, ALU.add))
                step("pages_f", dve.tensor_copy(pb2[:, :, 1], pti[:]))
                step("even", dve.tensor_scalar(pb2[:, :, 0], pb2[:, :, 1], 2.0, None, ALU.mult))
                step("odd", dve.tensor_scalar(pb2[:, :, 1], pb2[:, :, 0], 1.0, None, ALU.add))
                blocks = pb2[:].rearrange("p a b -> p (a b)")
                for k in range(5):
                    step(f"pick{k}", dve.scalar_tensor_tensor(junk[:], iota[:], idf[:, k:k + 1], blocks, ALU.is_equal, ALU.mult,
                                                              accum_out=ph[:, 2 + k:3 + k]))
                step("ph1", dve.tensor_copy(ph[:, 0:1], blocks[:, 0:1]))
                step("ph2", dve.tensor_copy(ph[:, 1:2], blocks[:, 127:128]))
                step("phys_int", dve.tensor_copy(phi[:], ph[:]))
                step("gated_cmp", dve.tensor_scalar(p[:], p[:], gr[:, 0:1], None, ALU.mult))
                dve.wait_ge(s_mm, pe_at["pT_cmp"])
                step("c_pT_cmp", dve.tensor_copy(pT["cmp"][:], psP[:, 0:2]))
                dve.wait_ge(s_wl, 16 * n_win)
                step("new_kw", dve.tensor_copy(wk[:, :, 511], kwn[:]))
                step("new_ks", dve.tensor_copy(kv[:, :, :, 0, 0, 0].rearrange("p b g -> p g b"), ksn[:]))

                def weigh(k, i, g):
                    step("p_" + k, dve.tensor_scalar(R[k][:], R[k][:], rsm[:, i:i + 1], gr[:, g:g + 1], ALU.mult, ALU.mult))
                scores("win", 4)
                step("rec_win", dve.reciprocal(rsm[:, 1:2], rsm[:, 1:2]))
                weigh("win", 1, 2)
                dve.wait_ge(s_mm, pe_at["pT_win"])
                step("c_pT_win", dve.tensor_copy(pT["win"][:], psP[:, 0:4]))
                step("is_last", dve.tensor_scalar(ind[:], idf[:], 126.0, None, ALU.is_equal))
                for k in range(5):
                    step(f"b{3 + k}", dve.tensor_scalar(bias["sel"][:, 64 * (3 + k):64 * (4 + k)], near[:], ind[:, k:k + 1], None, ALU.mult))
                scores("sel", 4)
                step("rec_sel", dve.reciprocal(rsm[:, 2:3], rsm[:, 2:3]))
                weigh("sel", 2, 1)
                dve.wait_ge(s_mm, pe_at["pT_sel"])
                step("c_pT_sel", dve.tensor_copy(pT["sel"][:], psP[0:64]))
                dve.wait_ge(s_mm, pe_at["aw"])
                step("c_aw", dve.tensor_copy(aw[:], psA[:]))
                dve.wait_ge(s_mm, pe_at["sel_o"])
                step("c_dd", dve.tensor_copy(dd[:], psD[:]))
                dve.wait_ge(s_mm, pe_at["turn"])
                step("o_a", dve.tensor_scalar(o2[:], psX[:, 0:64], side[:, 0:1], None, ALU.mult))
                step("o_b", dve.scalar_tensor_tensor(o[:], psX[:, 64:128], side[:, 1:2], o2[:], ALU.mult, ALU.add))
                step("o_c", dve.tensor_tensor(o[:], o[:], psX[:, 128:192], ALU.add))
                step("o_sq", dve.tensor_tensor(o2[:], o[:], o[:], ALU.mult))
                step("o_ss", dve.tensor_reduce(ss[:], o2[:], X, ALU.add))
                dve.wait_ge(s_ac, 4)
                step("std_r", dve.reciprocal(sd[:], sd[:]))
                step("o_n", dve.tensor_scalar(o[:], o[:], sd[:, 0:1], None, ALU.mult))
                step("o_g", dve.tensor_tensor(o[:], o[:], gain[:], ALU.mult))
                dve.wait_ge(s_mm, pe_at["heads"])
                step("c_heads", dve.tensor_copy(om[:], psX[:, 192:256].rearrange("p (b h) -> p h b", h=NH)))
                assert n[0] == len(DV)


def tail(nc, d, t):
    U_OUT, U_PA, U_UP, U_DOWN, U_PB, U_GATE, NU = np.cumsum([0, KT, 1, FT, 4 * KT, 1, KT]).tolist()
    RING = 6
    with ExitStack() as ctx:
        sb = lambda n, s, dt=F32: ctx.enter_context(nc.sbuf_tensor(n, s, dt))
        pb = lambda n, s: ctx.enter_context(nc.psum_tensor(n, s, F32))
        sem = ctx.enter_context(semaphores(nc, "tl_"))
        h = sb("h", [128, KT, CH])
        xb = sb("x_chunk_t", [128, KT, CH])
        mx = sb("mix_chunk", [128, KT, CH])
        a = sb("h_normed", [128, KT, CH])
        pr = sb("p_projected", [128, KT, CH])
        pT = sb("p_chunk", [128, 2, CH])
        ff = sb("ff", [128, FT, CH])
        sq = sb("h_square", [128, 2, CH])
        rs = sb("rstd_h", [128, CH])
        wr = sb("w_ring", [128, RING, 8, 128])
        gm = sb("norm_mlp_sb", [128, KT])
        gp = sb("norm_ple_sb", [128, KT])
        zp = [pb(f"ps_t{i}", [128, 2, 512]) for i in range(3)]
        ssp = pb("ps_hs", [128, 2, 512])
        V = lambda ps: ps[:, :, 0:HF]
        W = lambda a: a.rearrange("p (h n) -> p h n", h=2)
        s_c, s_in, s_o, s_wu, s_h1, s_sq, s_sqf, s_rs, s_a, s_ut, s_f, s_h2, s_g, s_gs, s_pj, s_y, s_rt = \
            (sem(n) for n in (
                "consts_loaded", "inputs_loaded", "y_sent", "unit_used", "h1_ready", "h_squared",
                "h_square_summed", "rstd_ready", "a_ready", "up_taken", "ff_ready", "h2_ready", "gate_done",
                "gate_ready", "proj_done", "y_ready", "roots_taken"))
        s_pc, s_p = sem("proj_copied"), sem("p_loaded")
        s_w = [sem(f"w{i}") for i in range(RING)]
        sem.start_at_one()
        per_slot = [len(range(s, NU, RING)) for s in range(RING)]

        with nc.Block() as block:
            @block.sync
            def _(sp):
                sp.dma_start(gm[:], d["norm_mlp"]).then_inc(s_c, 16)
                sp.dma_start(gp[:], d["norm_ple"]).then_inc(s_c, 16)

                def load_unit(un):
                    sp.dma_start(wr[:, un % RING], d["w_tail"][un]).then_inc(s_w[un % RING], 16)

                def load_in(c):
                    sp.dma_start(mx[:], d["mixT"][:, :, ds(c * CH, CH)].rearrange("k p n -> p k n")).then_inc(s_in, 16)
                    sp.dma_start(xb[:], d["xT"][:, :, ds(c * CH, CH)].rearrange("k p n -> p k n")).then_inc(s_in, 16)

                def load_p(c):
                    sp.dma_start(pT[:], d["pT"][:, :, ds(c * CH, CH)].rearrange("k p n -> p k n")).then_inc(s_p, 16)

                load_in(0)
                load_p(0)
                for un in range(RING):
                    load_unit(un)

                def body(c, last):
                    for un in range(RING, NU):
                        sp.wait_ge(s_wu, ONE + NU * c + un - RING + 1)
                        load_unit(un)
                        if un == U_UP + RING + 8 and not last:
                            sp.wait_ge(s_h1, ONE + KT * (c + 1))
                            load_in(c + 1)
                        if un == U_PB + RING + 1 and not last:
                            load_p(c + 1)
                    if not last:
                        before = lambda un: max(range(un, NU, RING))
                        for un in sorted(range(RING), key=before):
                            sp.wait_ge(s_wu, ONE + NU * c + before(un) + 1)
                            load_unit(un)
                    for k in range(KT):
                        sp.wait_ge(s_y, ONE + KT * c + k + 1)
                        sp.dma_start(d["yT"][k, :, ds(c * CH, CH)], h[:, k]).then_inc(s_o, 16)
                with sp.Fori(0, 3) as c:
                    body(c, False)
                body(3, True)
                sp.wait_ge(s_o, ONE + 16 * KT * 4)

            @block.tensor
            def _(pe):
                with pe.Fori(0, 4) as c:
                    un = [0]

                    def unit():
                        n = un[0]
                        pe.wait_ge(s_w[n % RING], ONE + 16 * (per_slot[n % RING] * c + n // RING + 1))
                        return wr[:, n % RING]

                    def used(mm):
                        mm.then_inc(s_wu, 1)
                        un[0] += 1

                    def sums(k0):
                        for k in range(KT):
                            pe.wait_ge(s_sq, ONE + 2 * KT * c + k0 + k + 1)
                            for hh in range(2):
                                mm = pe.matmul(ssp[:, hh, 0:HF], t["ones_d"][:], sq[:, k % 2, hh * HF:(hh + 1) * HF],
                                               start=(k == 0), stop=(k == KT - 1))
                            mm.then_inc(s_sqf, 1)

                    def tile(zi, src, ks, w, first=True, final=True):
                        for hh in range(2):
                            for i, k in enumerate(ks):
                                mm = pe.matmul(zp[zi][:, hh, 0:HF], w[:, i], src[:, k, hh * HF:(hh + 1) * HF],
                                               start=(first and i == 0), stop=(final and i == len(ks) - 1),
                                               skip_group_check=True)
                        return mm

                    def project(half):
                        w = unit()
                        for i in range(4):
                            if i == 3:
                                pe.wait_ge(s_pc, ONE + 8 * c + 4 * half + 1)
                            mm = tile(i % 3, pT, range(2), w[:, 2 * i:2 * i + 2])
                            if i == 3:
                                used(mm)
                            else:
                                mm.then_inc(s_pj, 1)

                    def normed(half, m, w):
                        for hh in range(2):
                            for k in range(KT):
                                if m == 0 and hh == 0:
                                    pe.wait_ge(s_a, ONE + 2 * KT * c + KT * half + k + 1)
                                mm = pe.matmul(zp[(m + 1) % 3][:, hh, 0:HF], w[:, k], a[:, k, hh * HF:(hh + 1) * HF],
                                               start=(k == 0), stop=(k == KT - 1), skip_group_check=True)
                        used(mm)

                    pe.wait_ge(s_in, ONE + 32 * c + 32)
                    for m in range(KT):
                        w = unit()
                        if m == 0:
                            pe.wait_ge(s_gs, ONE + KT * c)
                        if m >= 3:
                            pe.wait_ge(s_h1, ONE + KT * c + m - 2)
                        used(tile(m % 3, mx, range(KT), w))
                    sums(0)
                    pe.wait_ge(s_h1, ONE + KT * (c + 1))
                    pe.wait_ge(s_p, ONE + 16 * c + 16)
                    project(0)
                    for m in range(FT):
                        w = unit()
                        if m >= 3:
                            pe.wait_ge(s_ut, ONE + FT * c + m - 2)
                        else:
                            pe.wait_ge(s_pc, ONE + 8 * c + m + 2)
                        normed(0, m, w)
                    for m in range(KT):
                        if m >= 3:
                            pe.wait_ge(s_h2, ONE + KT * c + m - 2)
                        for g in range(4):
                            w = unit()
                            if m == 0:
                                if g == 0:
                                    pe.wait_ge(s_ut, ONE + FT * (c + 1))
                                pe.wait_ge(s_f, ONE + FT * c + 8 * g + 8)
                            used(tile(m % 3, ff, range(8 * g, 8 * g + 8), w, g == 0, g == 3))
                    sums(KT)
                    pe.wait_ge(s_h2, ONE + KT * (c + 1))
                    project(1)
                    for m in range(KT):
                        w = unit()
                        if m >= 3:
                            pe.wait_ge(s_gs, ONE + KT * c + m - 2)
                        else:
                            pe.wait_ge(s_pc, ONE + 8 * c + m + 6)
                        normed(1, m, w)

            @block.scalar
            def _(act):
                with act.Fori(0, 4) as c:
                    act.wait_ge(s_y, ONE + KT * c)
                    for r in range(2):
                        for k in range(KT):
                            if r == 0:
                                act.wait_ge(s_h1, ONE + KT * c + k + 1)
                            else:
                                act.wait_ge(s_h2, ONE + KT * c + k + 1)
                            if k >= 2:
                                act.wait_ge(s_sqf, ONE + 2 * KT * c + KT * r + k - 1)
                            act.activation(sq[:, k % 2], h[:, k], ACT.Square).then_inc(s_sq, 1)
                        act.wait_ge(s_sqf, ONE + 2 * KT * c + KT * (r + 1))
                        act.activation(W(rs[:]), V(ssp), ACT.Sqrt, bias=t["eps"][:]).then_inc(s_rt, 1)
                        for i in range(4):
                            if i == 3:
                                act.wait_ge(s_wu, ONE + NU * c + (U_PB if r else U_PA) + 1)
                            else:
                                act.wait_ge(s_pj, ONE + 6 * c + 3 * r + i + 1)
                            act.activation(W(pr[:, 4 * r + i]), V(zp[i % 3]), ACT.Copy).then_inc(s_pc, 1)
                        if r == 0:
                            for m in range(FT):
                                act.wait_ge(s_wu, ONE + NU * c + U_UP + m + 1)
                                act.activation(W(ff[:, m]), V(zp[(m + 1) % 3]), ACT.Relu).then_inc(s_ut, 1)
                    for m in range(KT):
                        act.wait_ge(s_wu, ONE + NU * c + U_GATE + m + 1)
                        act.activation(W(ff[:, m]), V(zp[(m + 1) % 3]), ACT.Sigmoid).then_inc(s_gs, 1)

            @block.vector
            def _(dve):
                dve.wait_ge(s_c, ONE + 32)
                own = Own(dve, ONE)
                with dve.Fori(0, 4) as c:
                    own.iteration(c)
                    dve.wait_ge(s_in, ONE + 32 * c + 32)
                    dve.wait_ge(s_o, ONE + 16 * KT * c)
                    for m in range(KT):
                        dve.wait_ge(s_wu, ONE + NU * c + m + 1)
                        own(dve.tensor_tensor(W(h[:, m]), V(zp[m % 3]), W(xb[:, m]), ALU.add), s_h1, KT)

                    def norm(r, gain):
                        dve.wait_ge(s_rt, ONE + 2 * c + r + 1)
                        own(dve.reciprocal(rs[:], rs[:]), s_rs, 2)
                        for k in range(KT):
                            own(dve.scalar_tensor_tensor(a[:, k], h[:, k], gain[:, k:k + 1], rs[:], ALU.mult,
                                                         ALU.mult), s_a, 2 * KT)
                    norm(0, gm)
                    for m in range(FT):
                        dve.wait_ge(s_ut, ONE + FT * c + m + 1)
                        own(dve.tensor_tensor(ff[:, m], ff[:, m], ff[:, m], ALU.mult), s_f, FT)
                    for m in range(KT):
                        dve.wait_ge(s_wu, ONE + NU * c + U_DOWN + 4 * (m + 1))
                        own(dve.tensor_tensor(W(h[:, m]), V(zp[m % 3]), W(h[:, m]), ALU.add), s_h2, KT)
                    norm(1, gp)
                    for m in range(KT):
                        dve.wait_ge(s_gs, ONE + KT * c + m + 1)
                        if m == 0:
                            dve.wait_ge(s_pc, ONE + 8 * (c + 1))
                        own(dve.tensor_tensor(ff[:, m], ff[:, m], pr[:, m], ALU.mult), s_g, KT)
                        own(dve.tensor_tensor(h[:, m], h[:, m], ff[:, m], ALU.add), s_y, KT)


def build(nc, d):
    with ExitStack() as ctx:
        sb = lambda n, s, dt=F32: ctx.enter_context(nc.sbuf_tensor(n, s, dt))
        t = {n: sb(n, [128, 128]) for n in ("ident", "ones_d", "ones_w", "ones_hd")}
        t["eps"] = sb("eps", [128, 1])
        s_k = ctx.enter_context(nc.semaphore("matrices_loaded"))
        live = ctx.enter_context(nc.semaphore("waits_passed"))

        def plain(eng):
            eng.sem_inc(live, 1)
        t["plain"] = plain
        with nc.Block() as block:
            @block.sync
            def _(sp):
                for i, n in enumerate(("ident", "ones_d", "ones_w", "ones_hd")):
                    sp.dma_start(t[n][:], d["matrices"][i]).then_inc(s_k, 16)
                sp.wait_ge(s_k, 64)

            @block.gpsimd
            def _(pool):
                pool.memset(t["eps"][:], EPS)
        project(nc, d, t)
        with ExitStack() as held:
            keep = lambda n, s, dt=F32: t.__setitem__(n, held.enter_context(nc.sbuf_tensor(n + "_sb", s, dt)))
            keep("band", [128, NH, BANDW])
            keep("kcT", [128, NCP + NCS])
            keep("kcz", [128, 2, NCP])
            keep("vcp", [NCP, 128])
            keep("vcs", [128, 2 * NB, 128])
            compress(nc, d, t)
            with ExitStack() as inner:
                keep = lambda n, s, dt=F32: t.__setitem__(n, inner.enter_context(nc.sbuf_tensor(n + "_pr", s, dt)))
                for n in ("ks", "kw"):
                    keep(n, [128, 2, SEQ])
                for n in ("vs", "vw"):
                    keep(n, [128, SEQ // 128, 128])
                for n, shape in (("S_sel", [128, 3, SEQ]), ("S_win", [128, 3, 640]), ("S_cmp", [128, 512]), ("mix_bias", [128, 3, 640]), ("wband", [128, NH, 640]), ("chunk_max", [128, 6, 8]),
                                 ("PT", [128, 4, 4, 128]), ("cband", [128, NH, 124]),
                                 ("score_band", [128, 64]), ("tri", [128, 128]), ("half", [128, 1]), ("att_gain", [128, 4]),
                                 ("q_near", [128, 4, 128]), ("q_sel", [128, 4, 128]), ("g_tiles", [24, 512]), ("gates_tok", [128, 4, 24]),
                                 ("mix_tile", [128, 4, 128]), ("nmax", [128, 6]), ("rsum", [128, 16]), ("coef", [128, 16]), ("cmax", [128, NH]),
                                 ("csum", [128, NH]), ("imp", [128, 2, 32]), ("top", [128, 2, 8]), ("mask", [128, 2, 32]),
                                 ("o_att", [128, 512]), ("o_tmp", [128, 512]), ("var", [128, 1]), ("rstd", [128, 1])):
                    keep(n, shape)
                prompt_keys(nc, d, t)
                for cl in range(4):
                    prompt(nc, d, t, cl)
            sample(nc, d, t)
        tail(nc, d, t)


def constants():
    p = np.arange(128)
    ident = np.eye(128, dtype=np.float32)
    blk = (p[:, None] // HD == p[None, :] // HD).astype(np.float32) / HD
    mats = np.stack([ident, np.full((128, 128), 1 / D), np.full((128, 128), 1 / 512), blk]).astype(np.float32)
    dist = 640 - np.arange(LINEW)
    n = np.maximum(dist, 1).astype(np.float32)
    large = 16 + (np.log(n / 16) / np.float32(np.log(8.0)) * 16).astype(np.int32)
    bucket = np.where(dist < 16, np.maximum(dist, 0), np.minimum(large, 31))
    onehot = (np.arange(32)[:, None] == bucket[None]).astype(np.float32)
    onehot[31] -= 1.0
    onehot[:, dist < 0] = 0
    rel = np.arange(BANDW) - 512
    cmask = np.where(rel[None] > p[:, None], NEG, 0).astype(np.float32)
    tri = np.where(p[None] > p[:, None], 0, NEG).astype(np.float32)
    r = np.arange(NB * NH)
    rel_blk, cur = np.arange(64)[None] - 30, (p >= 64).astype(int)[:, None]
    score = np.where(rel_blk > cur, NEG, np.where(rel_blk >= cur - 1, 1e4, 0)).astype(np.float32)
    return {"matrices": mats, "onehot": onehot, "cmask": cmask, "tri": tri, "score_band": score,
            "iota": np.broadcast_to(np.arange(128, dtype=np.float32), (NB * NH, 128)).copy(),
            "same_group": (r[:, None] // 4 == r[None] // 4).astype(np.float32),
            "same_token": ((r[:, None] // NH == r[None] // NH) / 512).astype(np.float32),
            "group_rows": np.stack([r % NH < 4, r % NH >= 4], axis=1).astype(np.float32)}


def lay_out(x):
    a = {k: np.asarray(v) for k, v in x.items()}
    A = np.ascontiguousarray
    feat = lambda v, n: v.reshape(-1, n * 128).T.reshape(n, 128, -1)
    tok = lambda p, s, n: A(np.concatenate([feat(p, n), feat(s, n)], axis=2))
    tiles = lambda w: w.reshape(w.shape[0] // 128, 128, -1, 128).transpose(2, 1, 0, 3)
    w = a["w_in"][0]
    o = 512
    cols = {k: np.arange(o + 128 * i, o + 128 * (i + 1)) for i, k in enumerate(("kc", "vc", "ks", "vs", "kw", "vw"))}
    for j in range(4):
        cols[f"q{j}"] = np.r_[HD * j:HD * (j + 1), HD * (4 + j):HD * (5 + j)]
        for i, k in enumerate(("cb", "cc", "ch")):
            s = 512 + 768 + 24 + 512 * i + 128 * j
            cols[f"{k}{j}"] = np.arange(s, s + 128)
    order = np.concatenate([cols[k] for k in ZT[:-1]])
    r = {"xT": tok(a["x_prompt"], a["x_sample"], 8), "pT": tok(a["p_prompt"], a["p_sample"], 2)}
    r["w_in"] = A(tiles(w[:, order]))
    r["w_gates"] = A(w[:, 1280:1304].reshape(8, 128, 24).transpose(1, 0, 2))
    vec = lambda v: A(v.reshape(-1, 128).T)
    r["norm_mix"], r["norm_mlp"], r["norm_ple"] = (vec(a[k]) for k in ("norm_mix", "norm_mlp", "norm_ple"))
    on = vec(a["out_norm"])
    r["att_gain"], r["conv_gain"] = A(on[:, 0:4]), A(on[:, 4:8])
    two = lambda v: np.concatenate([v, v])
    r["qk_gain"] = A(np.stack([two(a["q_norm"][0])] * 4 + [two(a["k_norm"][0, 1]), two(a["k_norm"][0, 2])], axis=1))
    r["conv_w"] = A(a["conv_w"][0].reshape(3, 4, 128).transpose(2, 1, 0))
    r["state_conv"] = A(a["state_conv"][0].reshape(NB, 2, 4, 128).transpose(3, 2, 1, 0))
    r["rel_bias"] = a["rel_bias"]
    r["cache_cmp"] = A(a["cache_cmp_kv"][0].transpose(0, 3, 4, 2, 1).reshape(-1, 128, 2, PAGE))
    r["page_table"] = A(a["page_table"].reshape(1, -1))
    r["w_cmp"] = A(a["w_cmp"][0].transpose(0, 2, 1, 3))
    r["cmp_pe"] = A(np.concatenate([a["cmp_pe"][0].transpose(2, 0, 1)] * 2))
    sel = a["cache_sel_kv"][0].reshape(-1, 64, 2, 2, HD)
    r["sel_kv"] = np.stack([sel[:, :, 0].transpose(0, 2, 3, 1), sel[:, :, 1].transpose(0, 2, 1, 3)], axis=3)
    w = a["state_win_kv"][0].reshape(NB, 512, 2, 128)
    r["win_k"], r["win_v"] = A(w[:, :, 0].transpose(0, 2, 1)), A(w[:, :, 1])
    r["out_gain"] = A(a["out_norm"][0, :512].reshape(NH, HD))
    r["k_norm_cmp"] = A(two(a["k_norm"][0, 0])[:, None])
    up, down, out_, gate = tiles(a["w_up"][0]), tiles(a["w_down"][0]), tiles(a["w_out"][0]), tiles(a["w_ple_gate"][0])
    down = down.reshape(8, 128, 4, 8, 128).transpose(0, 2, 1, 3, 4).reshape(32, 128, 8, 128)
    proj = tiles(a["w_ple_proj"][0]).reshape(2, 4, 128, 2, 128).transpose(0, 2, 1, 3, 4).reshape(2, 128, 8, 128)
    r["w_tail"] = A(np.concatenate([out_, proj[:1], up, down, proj[1:], gate]))
    return r


OUTS = {"yT": [8, 128, NTOK], "kvT": [6, 128, NTOK], "uT": [4, 128, NB + 2],
        "win_k_out": [NB, 128, 512], "win_v_out": [NB, 512, 128], "conv_prev": [128, 4, NB]}
SCRATCH = {"qT": [4, 128, NTOK], "mixT": [8, 128, NTOK], "gT": [24, NTOK], "line": [NH, LINEW],
           "skew": [128, NH * LINEW], "phys": [NB * NH, 7]}


def kernel(**inputs):
    import concourse.bacc as bacc
    from concourse.bass_utils import run_bass_kernel_spmd

    nc = bacc.Bacc("TRN2", target_bir_lowering=False, num_devices=1)
    arrays = {**lay_out(inputs), **constants()}
    d = {n: nc.dram_tensor("in_" + n, v.shape, mybir.dt.from_np(v.dtype), kind="ExternalInput").ap()
         for n, v in arrays.items()}
    for n, s in OUTS.items():
        d[n] = nc.dram_tensor("out_" + n, s, F32, kind="ExternalOutput").ap()
    for n, s in SCRATCH.items():
        d[n] = nc.dram_tensor("scratch_" + n, s, I32 if n == "phys" else F32, kind="Internal").ap()
    build(nc, d)
    r = run_bass_kernel_spmd(nc, [{"in_" + n: v for n, v in arrays.items()}], core_ids=[0]).results[0]
    g = {n: r["out_" + n] for n in OUTS}
    y = g["yT"].reshape(D, NTOK).T
    kv = g["kvT"].reshape(6, 128, NTOK).transpose(2, 0, 1).reshape(NTOK, 3, 2, 2, HD)
    uT = g["uT"].reshape(512, NB + 2).T
    p, s = kv[:SEQ], kv[SEQ:]
    wk, wv = g["win_k_out"].transpose(0, 2, 1).reshape(NB, 512, 2, HD), g["win_v_out"].reshape(NB, 512, 2, HD)
    wk = np.stack([wk, wv], axis=2)[None]
    prev = g["conv_prev"].transpose(2, 1, 0).reshape(NB, 512)
    sc = np.stack([prev, uT[2:]], axis=1)[None]
    return (y[None, :SEQ].copy(), y[SEQ:, None].copy(), p[None, None, :, 0].copy(), p[None, None, :, 1].copy(),
            p[None, None, -512:, 2].copy(), uT[None, None, 0:2].copy(), s[None, :, None, 0].copy(),
            s[None, :, None, 1].copy(), wk, sc)
```
